# Optimizing a Trainium2 kernel written in Bass

```python
import jax, jax.numpy as jnp
from jax import lax
import numpy as np
import math
import jax
import jax.numpy as jnp

D_MODEL = 1024
BATCH = 1
SEQ = 256
DEPTH = 2

GRID_W = 64
CTX_LEN = 256
D_FF = 2816
CONV_WIDTH = 31
CONV_PAD = (CONV_WIDTH - 1) // 2
N_Q_HEADS = 16
N_KV_HEADS = 4
HEAD_DIM = 64
WINDOW = 128
BLOCK = 128
ROPE_BASE = 10000.0
NORM_EPS = 1e-6
N_MOD = 9
N_CONV_LAYERS = (DEPTH + 1) // 2
N_ATTN_LAYERS = DEPTH // 2
Q_DIM = N_Q_HEADS * HEAD_DIM
KV_DIM = N_KV_HEADS * HEAD_DIM


def rmsnorm(x, g):
    xf = x.astype(jnp.float32)
    y = xf * lax.rsqrt(jnp.mean(xf * xf, axis=-1, keepdims=True) + NORM_EPS)
    return y.astype(x.dtype) * g

def modulate(x, g, shift, scale):
    return rmsnorm(x, g) * (1 + scale) + shift

def swiglu(h, w_in, w_out):
    gu = h @ w_in
    gate, up = jnp.split(gu, 2, axis=-1)
    return (jax.nn.silu(gate) * up) @ w_out

def conformer_conv(h, pw1_w, pw1_b, dw_w, dw_b, ln_g, ln_b, pw2_w, pw2_b):
    a = h @ pw1_w + pw1_b
    u, g = jnp.split(a, 2, axis=-1)
    u = u * jax.nn.sigmoid(g)
    u = lax.conv_general_dilated(
        u, dw_w[:, None, :].astype(u.dtype), window_strides=(1,),
        padding=[(CONV_PAD, CONV_PAD)], dimension_numbers=("NWC", "WIO", "NWC"),
        feature_group_count=D_MODEL) + dw_b
    uf = u.astype(jnp.float32)
    mu = jnp.mean(uf, axis=-1, keepdims=True)
    var = jnp.mean(jnp.square(uf - mu), axis=-1, keepdims=True)
    u = ((uf - mu) * lax.rsqrt(var + NORM_EPS)).astype(u.dtype) * ln_g + ln_b
    return jax.nn.silu(u) @ pw2_w + pw2_b

def axial_rope_tables(n_tok):
    n_rows = n_tok // GRID_W
    row = jnp.repeat(jnp.arange(n_rows), GRID_W).astype(jnp.float32)
    col = jnp.tile(jnp.arange(GRID_W), n_rows).astype(jnp.float32)
    n_freq = HEAD_DIM // 4
    inv = ROPE_BASE ** (-jnp.arange(n_freq, dtype=jnp.float32) / n_freq)
    ang = jnp.stack([row[:, None] * inv, col[:, None] * inv], axis=1)
    return jnp.cos(ang), jnp.sin(ang)

def apply_rope(x, cos, sin):
    n_freq = HEAD_DIM // 4
    xs = x.reshape(x.shape[:-1] + (2, 2, n_freq))
    x1 = xs[..., 0, :]
    x2 = xs[..., 1, :]
    bshape = (1, cos.shape[0]) + (1,) * (x.ndim - 3) + (2, n_freq)
    cs = cos.reshape(bshape).astype(x.dtype)
    sn = sin.reshape(bshape).astype(x.dtype)
    out = jnp.stack([x1 * cs - x2 * sn, x1 * sn + x2 * cs], axis=-2)
    return out.reshape(x.shape)

def windowed_gqa_sink(h_lat, h_ctx, w_qkv, w_o, sink, with_ctx_out):
    B, S, _ = h_lat.shape
    C = h_ctx.shape[1]
    G = N_Q_HEADS // N_KV_HEADS
    scale = HEAD_DIM ** -0.5

    def proj(h):
        qkv = h @ w_qkv
        q = qkv[..., :Q_DIM].reshape(h.shape[:2] + (N_KV_HEADS, G, HEAD_DIM))
        k = qkv[..., Q_DIM:Q_DIM + KV_DIM].reshape(h.shape[:2] + (N_KV_HEADS, HEAD_DIM))
        v = qkv[..., Q_DIM + KV_DIM:].reshape(h.shape[:2] + (N_KV_HEADS, HEAD_DIM))
        return q, k, v

    ql, kl, vl = proj(h_lat)
    qc, kc, vc = proj(h_ctx)
    cos, sin = axial_rope_tables(S)
    ql = apply_rope(ql, cos, sin) * scale
    kl = apply_rope(kl, cos, sin)
    pad = ((0, 0), (WINDOW, WINDOW), (0, 0), (0, 0))
    k_pad = jnp.pad(kl, pad)
    v_pad = jnp.pad(vl, pad)
    sink_col = sink.reshape(N_KV_HEADS, G, 1, 1).astype(jnp.float32)
    kw = BLOCK + 2 * WINDOW

    def one_block(n):
        start = n * BLOCK
        qb = lax.dynamic_slice_in_dim(ql, start, BLOCK, axis=1)
        kb = lax.dynamic_slice_in_dim(k_pad, start, kw, axis=1)
        vb = lax.dynamic_slice_in_dim(v_pad, start, kw, axis=1)
        i_pos = start + jnp.arange(BLOCK)
        j_pos = start - WINDOW + jnp.arange(kw)
        valid = ((jnp.abs(j_pos[None, :] - i_pos[:, None]) <= WINDOW)
                 & (j_pos[None, :] >= 0) & (j_pos[None, :] < S))
        s_win = jnp.einsum('bqhgd,bkhd->bhgqk', qb, kb).astype(jnp.float32)
        s_win = jnp.where(valid, s_win, -jnp.inf)
        s_ctx = jnp.einsum('bqhgd,bchd->bhgqc', qb, kc).astype(jnp.float32)
        sinks = jnp.broadcast_to(sink_col, s_win.shape[:-1] + (1,))
        p = jax.nn.softmax(jnp.concatenate([s_win, s_ctx, sinks], axis=-1), axis=-1).astype(vb.dtype)
        o = (jnp.einsum('bhgqk,bkhd->bqhgd', p[..., :kw], vb)
             + jnp.einsum('bhgqc,bchd->bqhgd', p[..., kw:kw + C], vc))
        return o.reshape(B, BLOCK, Q_DIM)

    o = lax.map(one_block, jnp.arange(S // BLOCK))
    y_lat = jnp.moveaxis(o, 0, 1).reshape(B, S, Q_DIM) @ w_o

    y_ctx = None
    if with_ctx_out:
        s = jnp.einsum('bqhgd,bkhd->bhgqk', qc * scale, kc).astype(jnp.float32)
        sinks = jnp.broadcast_to(sink_col, s.shape[:-1] + (1,))
        p = jax.nn.softmax(jnp.concatenate([s, sinks], axis=-1), axis=-1).astype(vc.dtype)
        oc = jnp.einsum('bhgqk,bkhd->bqhgd', p[..., :C], vc)
        y_ctx = oc.reshape(B, C, Q_DIM) @ w_o
    return y_lat, y_ctx

def first_inputs(seed: int = 0) -> dict:
    key = jax.random.key(seed)
    ks = jax.random.split(key, 32)
    f32 = jnp.float32

    def nrm(k, shape, s):
        return jax.random.normal(k, shape, f32) * s

    D, F = D_MODEL, D_FF
    NC, NA = N_CONV_LAYERS, N_ATTN_LAYERS
    return {
        "x": nrm(ks[0], (BATCH, SEQ, D), 1.0),
        "c": nrm(ks[1], (BATCH, D), 1.0),
        "ctx": nrm(ks[2], (BATCH, CTX_LEN, D), 1.0),
        "c_ctx": nrm(ks[3], (D,), 1.0),
        "norm_g": 1.0 + nrm(ks[4], (DEPTH, 3, D), 0.05),
        "ada_w": nrm(ks[5], (DEPTH, D, N_MOD * D), D ** -0.5),
        "ada_b": nrm(ks[6], (DEPTH, N_MOD * D), 0.02),
        "ffn1_wi": nrm(ks[7], (DEPTH, D, 2 * F), D ** -0.5),
        "ffn1_wo": nrm(ks[8], (DEPTH, F, D), F ** -0.5),
        "ffn2_wi": nrm(ks[9], (DEPTH, D, 2 * F), D ** -0.5),
        "ffn2_wo": nrm(ks[10], (DEPTH, F, D), F ** -0.5),
        "conv_pw1_w": nrm(ks[11], (NC, D, 2 * D), D ** -0.5),
        "conv_pw1_b": nrm(ks[12], (NC, 2 * D), 0.02),
        "conv_dw_w": nrm(ks[13], (NC, CONV_WIDTH, D), CONV_WIDTH ** -0.5),
        "conv_dw_b": nrm(ks[14], (NC, D), 0.02),
        "conv_ln_g": 1.0 + nrm(ks[15], (NC, D), 0.05),
        "conv_ln_b": nrm(ks[16], (NC, D), 0.02),
        "conv_pw2_w": nrm(ks[17], (NC, D, D), D ** -0.5),
        "conv_pw2_b": nrm(ks[18], (NC, D), 0.02),
        "attn_w_qkv": nrm(ks[19], (NA, D, Q_DIM + 2 * KV_DIM), D ** -0.5),
        "attn_w_o": nrm(ks[20], (NA, Q_DIM, D), Q_DIM ** -0.5),
        "attn_sink": nrm(ks[21], (NA, N_Q_HEADS), 1.0),
        "final_g": 1.0 + nrm(ks[22], (D,), 0.05),
    }

def first_block(x, c, ctx, c_ctx, norm_g, ada_w, ada_b, ffn1_wi, ffn1_wo, ffn2_wi, ffn2_wo,
              conv_pw1_w, conv_pw1_b, conv_dw_w, conv_dw_b, conv_ln_g, conv_ln_b,
              conv_pw2_w, conv_pw2_b, attn_w_qkv, attn_w_o, attn_sink, final_g):
    for i in range(DEPTH):
        last = i == DEPTH - 1
        m_lat = (jax.nn.silu(c) @ ada_w[i] + ada_b[i])[:, None, :]
        m_ctx = (jax.nn.silu(c_ctx) @ ada_w[i] + ada_b[i])[None, None, :]
        sh1, sc1, gt1, sh2, sc2, gt2, sh3, sc3, gt3 = jnp.split(m_lat, N_MOD, axis=-1)
        ch1, cs1, cg1, ch2, cs2, cg2, ch3, cs3, cg3 = jnp.split(m_ctx, N_MOD, axis=-1)
        g1, g2, g3 = norm_g[i, 0], norm_g[i, 1], norm_g[i, 2]

        x = x + 0.5 * gt1 * swiglu(modulate(x, g1, sh1, sc1), ffn1_wi[i], ffn1_wo[i])
        ctx = ctx + 0.5 * cg1 * swiglu(modulate(ctx, g1, ch1, cs1), ffn1_wi[i], ffn1_wo[i])

        hx = modulate(x, g2, sh2, sc2)
        hc = modulate(ctx, g2, ch2, cs2)
        j = i // 2
        if i % 2 == 0:
            conv_args = (conv_pw1_w[j], conv_pw1_b[j], conv_dw_w[j], conv_dw_b[j],
                         conv_ln_g[j], conv_ln_b[j], conv_pw2_w[j], conv_pw2_b[j])
            y_lat = conformer_conv(hx, *conv_args)
            y_ctx = None if last else conformer_conv(hc, *conv_args)
        else:
            y_lat, y_ctx = windowed_gqa_sink(hx, hc, attn_w_qkv[j], attn_w_o[j],
                                             attn_sink[j], not last)
        x = x + gt2 * y_lat

        x = x + 0.5 * gt3 * swiglu(modulate(x, g3, sh3, sc3), ffn2_wi[i], ffn2_wo[i])
        if not last:
            ctx = ctx + cg2 * y_ctx
            ctx = ctx + 0.5 * cg3 * swiglu(modulate(ctx, g3, ch3, cs3), ffn2_wi[i], ffn2_wo[i])
    return rmsnorm(x, final_g)


N_HEADS = D_MODEL // HEAD_DIM
MOBA_HEADS = N_HEADS // 2
DIL_HEADS = N_HEADS - MOBA_HEADS
MOBA_BLOCK = 256
MOBA_TOPK = 3
MOBA_QCHUNK = 16
DIL_PAIRS = ((128, 1), (512, 4), (2048, 16))
DIL_BLOCK = 128
NSA_HEADS = N_HEADS
NSA_GROUPS = 4
NSA_HPG = NSA_HEADS // NSA_GROUPS
NSA_CMP_LEN = 32
NSA_CMP_STRIDE = 16
NSA_CMP_HIDDEN = 2 * HEAD_DIM
NSA_SEL_BLOCK = 64
NSA_SEL_TOPN = 16
NSA_WINDOW = 512
NSA_WIN_BLOCK = 128
NSA_QCHUNK = 32
NSA_FORCE = 1.0e6
REL_BUCKETS = 32
REL_MAX_DIST = 2048
FFN_HIDDEN = -((-8 * D_MODEL) // (3 * 256)) * 256
PLE_DIM = 256
N_EVEN = (DEPTH + 1) // 2
N_ODD = DEPTH // 2
RMS_EPS = 1e-6
ATTN_SCALE = HEAD_DIM ** -0.5
F32 = jnp.float32


def _rms(x, g):
    xf = x.astype(F32)
    y = xf * lax.rsqrt(jnp.mean(xf * xf, axis=-1, keepdims=True) + RMS_EPS)
    return (y * g.astype(F32)).astype(x.dtype)

def _heads(t, n):
    B, S, _ = t.shape
    return t.reshape(B, S, n, HEAD_DIM).transpose(0, 2, 1, 3)

def _rel_bucket(dist):
    n = jnp.maximum(dist, 0)
    exact = REL_BUCKETS // 2
    nf = jnp.maximum(n, 1).astype(F32)
    large = exact + (jnp.log(nf / exact) / math.log(REL_MAX_DIST / exact) * (REL_BUCKETS - exact)).astype(jnp.int32)
    return jnp.where(n < exact, n, jnp.minimum(large, REL_BUCKETS - 1))

def _masked_softmax(s, mask):
    s = jnp.where(mask, s.astype(F32), -jnp.inf)
    m = jnp.max(s, axis=-1, keepdims=True)
    m = jnp.where(jnp.isfinite(m), m, 0.0)
    e = jnp.exp(s - m)
    l = jnp.sum(e, axis=-1, keepdims=True)
    p = e / jnp.where(l > 0, l, 1.0)
    return p, (m + jnp.log(l))[..., 0]

def _moba(q, k, v, tab):
    B, H, S, hd = q.shape
    nb = -(-S // MOBA_BLOCK)
    padw = ((0, 0), (0, 0), (0, nb * MOBA_BLOCK - S), (0, 0))
    kb = jnp.pad(k, padw).reshape(B, H, nb, MOBA_BLOCK, hd)
    vb = jnp.pad(v, padw).reshape(B, H, nb, MOBA_BLOCK, hd)
    kmean = jnp.mean(kb.astype(F32), axis=3)
    own = jnp.arange(S) // MOBA_BLOCK
    gate = jnp.einsum('bhsd,bhnd->bhsn', q.astype(F32), kmean)
    gate = jnp.where(jnp.arange(nb)[None, :] < own[:, None], gate, -jnp.inf)
    n_sel = min(MOBA_TOPK, nb)
    _, sel = lax.top_k(gate, n_sel)
    sel_ok = sel < own[:, None]
    nc = S // MOBA_QCHUNK

    def to_chunks(t):
        return jnp.moveaxis(t.reshape(B, H, nc, MOBA_QCHUNK, *t.shape[3:]), 2, 0)

    b_ix = jnp.arange(B)[:, None, None, None]
    h_ix = jnp.arange(H)[None, :, None, None]
    a_blk = jnp.arange(MOBA_BLOCK)

    def chunk(args):
        c, qc, sc, okc = args
        t = c * MOBA_QCHUNK + jnp.arange(MOBA_QCHUNK)
        j = (c * MOBA_QCHUNK) // MOBA_BLOCK
        k_own = lax.dynamic_index_in_dim(kb, j, axis=2, keepdims=False)
        v_own = lax.dynamic_index_in_dim(vb, j, axis=2, keepdims=False)
        d_own = t[:, None] - (j * MOBA_BLOCK + a_blk)[None, :]
        s_own = jnp.einsum('bhqd,bhkd->bhqk', qc, k_own).astype(F32) * ATTN_SCALE + tab[:, _rel_bucket(d_own)].astype(F32)
        m_own = jnp.broadcast_to(d_own >= 0, s_own.shape)
        k_sel = kb[b_ix, h_ix, sc].reshape(B, H, MOBA_QCHUNK, n_sel * MOBA_BLOCK, hd)
        v_sel = vb[b_ix, h_ix, sc].reshape(B, H, MOBA_QCHUNK, n_sel * MOBA_BLOCK, hd)
        kpos = (sc[..., None] * MOBA_BLOCK + a_blk).reshape(B, H, MOBA_QCHUNK, n_sel * MOBA_BLOCK)
        s_sel = jnp.einsum('bhqd,bhqkd->bhqk', qc, k_sel).astype(F32) * ATTN_SCALE + tab[h_ix, _rel_bucket(t[:, None] - kpos)].astype(F32)
        m_sel = jnp.repeat(okc, MOBA_BLOCK, axis=-1)
        pr, _ = _masked_softmax(jnp.concatenate([s_own, s_sel], axis=-1), jnp.concatenate([m_own, m_sel], axis=-1))
        p_own = pr[..., :MOBA_BLOCK].astype(v.dtype)
        p_sel = pr[..., MOBA_BLOCK:].astype(v.dtype)
        return jnp.einsum('bhqk,bhkd->bhqd', p_own, v_own) + jnp.einsum('bhqk,bhqkd->bhqd', p_sel, v_sel)

    out = lax.map(chunk, (jnp.arange(nc), to_chunks(q), to_chunks(sel), to_chunks(sel_ok)))
    return jnp.moveaxis(out, 0, 2).reshape(B, H, S, hd)

def _stride_split(t, dil, L):
    B, H, S, hd = t.shape
    t = jnp.pad(t, ((0, 0), (0, 0), (0, L * dil - S), (0, 0)))
    return t.reshape(B, H, L, dil, hd).transpose(0, 1, 3, 2, 4)

def _band(t):
    prev = jnp.pad(t, ((0, 0), (0, 0), (0, 0), (1, 0), (0, 0), (0, 0)))[:, :, :, :-1]
    return jnp.concatenate([prev, t], axis=4)

def _dilated(q, k, v, tab):
    B, H, S, hd = q.shape
    blk = DIL_BLOCK
    outs, lses = [], []
    for window, dil in DIL_PAIRS:
        steps = window // dil
        L = -(-S // (dil * blk)) * blk
        nbk = L // blk
        qs = _stride_split(q, dil, L).reshape(B, H, dil, nbk, blk, hd)
        ks = _stride_split(k, dil, L).reshape(B, H, dil, nbk, blk, hd)
        vs = _stride_split(v, dil, L).reshape(B, H, dil, nbk, blk, hd)
        step = jnp.arange(blk)[:, None] + blk - jnp.arange(2 * blk)[None, :]
        key_ok = (jnp.arange(nbk)[:, None] * blk - blk + jnp.arange(2 * blk)[None, :]) >= 0
        mask = ((step >= 0) & (step <= steps))[None] & key_ok[:, None, :]
        bias = tab[:, _rel_bucket(step * dil)].astype(F32)
        s = jnp.einsum('bhrjqd,bhrjkd->bhrjqk', qs, _band(ks)).astype(F32) * ATTN_SCALE + bias[None, :, None, None]
        pr, lse = _masked_softmax(s, mask)
        o = jnp.einsum('bhrjqk,bhrjkd->bhrjqd', pr.astype(v.dtype), _band(vs))
        outs.append(o.reshape(B, H, dil, L, hd).transpose(0, 1, 3, 2, 4).reshape(B, H, L * dil, hd)[:, :, :S])
        lses.append(lse.reshape(B, H, dil, L).transpose(0, 1, 3, 2).reshape(B, H, L * dil)[:, :, :S])
    w = jax.nn.softmax(jnp.stack(lses), axis=0)
    o = jnp.einsum('nbhs,nbhsd->bhsd', w, jnp.stack(outs).astype(F32))
    return o.astype(q.dtype)

def _compress(t, pos_emb, w1, b1, w2, b2):
    B, G, S, hd = t.shape
    nc = (S - NSA_CMP_LEN) // NSA_CMP_STRIDE + 1
    idx = jnp.arange(nc)[:, None] * NSA_CMP_STRIDE + jnp.arange(NSA_CMP_LEN)[None, :]
    blocks = (t[:, :, idx] + pos_emb).reshape(B, G, nc, NSA_CMP_LEN * hd)
    return jax.nn.gelu(blocks @ w1 + b1) @ w2 + b2

def _nsa(q, kc, vc, ks, vs, kw, vw, gates, tab):
    B, H, S, hd = q.shape
    G, hpg = NSA_GROUPS, NSA_HPG
    qg = q.reshape(B, G, hpg, S, hd)
    tabg = tab.reshape(G, hpg, REL_BUCKETS)
    t = jnp.arange(S)
    nc = kc.shape[2]
    dc = t[:, None] - (jnp.arange(nc) * NSA_CMP_STRIDE + NSA_CMP_LEN - 1)[None, :]
    s = jnp.einsum('bghsd,bgcd->bghsc', qg, kc).astype(F32) * ATTN_SCALE + tabg[:, :, _rel_bucket(dc)].astype(F32)
    p_cmp, _ = _masked_softmax(s, dc >= 0)
    o_cmp = jnp.einsum('bghsc,bgcd->bghsd', p_cmp.astype(vc.dtype), vc)
    n_sel = -(-S // NSA_SEL_BLOCK)
    cstart = jnp.arange(nc) * NSA_CMP_STRIDE
    sstart = jnp.arange(n_sel) * NSA_SEL_BLOCK
    overlap = jnp.maximum(jnp.minimum(cstart[:, None] + NSA_CMP_LEN, sstart[None, :] + NSA_SEL_BLOCK) - jnp.maximum(cstart[:, None], sstart[None, :]), 0).astype(F32)
    imp = jnp.einsum('bghsc,cn->bgsn', p_cmp, overlap)
    cur = (t // NSA_SEL_BLOCK)[:, None]
    blk_id = jnp.arange(n_sel)[None, :]
    forced = (blk_id == 0) | (blk_id == cur) | (blk_id == cur - 1)
    imp = jnp.where(blk_id <= cur, imp + jnp.where(forced, NSA_FORCE, 0.0), -jnp.inf)
    n_top = min(NSA_SEL_TOPN, n_sel)
    _, sel = lax.top_k(imp, n_top)
    padw = ((0, 0), (0, 0), (0, n_sel * NSA_SEL_BLOCK - S), (0, 0))
    ksb = jnp.pad(ks, padw).reshape(B, G, n_sel, NSA_SEL_BLOCK, hd)
    vsb = jnp.pad(vs, padw).reshape(B, G, n_sel, NSA_SEL_BLOCK, hd)
    nq = S // NSA_QCHUNK
    b_ix = jnp.arange(B)[:, None, None, None]
    g_ix = jnp.arange(G)[None, :, None, None]
    h_ix = jnp.arange(hpg)[None, None, :, None, None]
    a_blk = jnp.arange(NSA_SEL_BLOCK)

    def sel_chunk(args):
        c, qc, sc = args
        tq = c * NSA_QCHUNK + jnp.arange(NSA_QCHUNK)
        kk = ksb[b_ix, g_ix, sc].reshape(B, G, NSA_QCHUNK, n_top * NSA_SEL_BLOCK, hd)
        vv = vsb[b_ix, g_ix, sc].reshape(B, G, NSA_QCHUNK, n_top * NSA_SEL_BLOCK, hd)
        kpos = (sc[..., None] * NSA_SEL_BLOCK + a_blk).reshape(B, G, NSA_QCHUNK, n_top * NSA_SEL_BLOCK)
        dist = tq[:, None] - kpos
        bias = tabg[g_ix[..., None], h_ix, _rel_bucket(dist)[:, :, None]].astype(F32)
        s = jnp.einsum('bghqd,bgqkd->bghqk', qc, kk).astype(F32) * ATTN_SCALE + bias
        pr, _ = _masked_softmax(s, (dist >= 0)[:, :, None])
        return jnp.einsum('bghqk,bgqkd->bghqd', pr.astype(vv.dtype), vv)

    qch = jnp.moveaxis(qg.reshape(B, G, hpg, nq, NSA_QCHUNK, hd), 3, 0)
    sch = jnp.moveaxis(sel.reshape(B, G, nq, NSA_QCHUNK, n_top), 2, 0)
    o_slc = jnp.moveaxis(lax.map(sel_chunk, (jnp.arange(nq), qch, sch)), 0, 3).reshape(B, G, hpg, S, hd)
    nw = S // NSA_WIN_BLOCK
    span = NSA_WINDOW + NSA_WIN_BLOCK
    kwp = jnp.pad(kw, ((0, 0), (0, 0), (NSA_WINDOW, 0), (0, 0)))
    vwp = jnp.pad(vw, ((0, 0), (0, 0), (NSA_WINDOW, 0), (0, 0)))
    kidx = jnp.arange(span)[None, :]
    dw = jnp.arange(NSA_WIN_BLOCK)[:, None] + NSA_WINDOW - kidx
    bias_w = tabg[:, :, _rel_bucket(dw)].astype(F32)

    def win_block(args):
        j, qb = args
        kb_ = lax.dynamic_slice_in_dim(kwp, j * NSA_WIN_BLOCK, span, axis=2)
        vb_ = lax.dynamic_slice_in_dim(vwp, j * NSA_WIN_BLOCK, span, axis=2)
        ok = (dw >= 0) & (dw < NSA_WINDOW) & (j * NSA_WIN_BLOCK - NSA_WINDOW + kidx >= 0)
        s = jnp.einsum('bghqd,bgkd->bghqk', qb, kb_).astype(F32) * ATTN_SCALE + bias_w
        pr, _ = _masked_softmax(s, ok)
        return jnp.einsum('bghqk,bgkd->bghqd', pr.astype(vb_.dtype), vb_)

    qwb = jnp.moveaxis(qg.reshape(B, G, hpg, nw, NSA_WIN_BLOCK, hd), 3, 0)
    o_win = jnp.moveaxis(lax.map(win_block, (jnp.arange(nw), qwb)), 0, 3).reshape(B, G, hpg, S, hd)
    o = (gates[..., 0:1] * o_cmp.reshape(B, H, S, hd) + gates[..., 1:2] * o_slc.reshape(B, H, S, hd)
         + gates[..., 2:3] * o_win.reshape(B, H, S, hd))
    return o.astype(q.dtype)

def _mixer_ab(xn, w_in, w_out, qn_a, kn_a, qn_b, kn_b, rel_bias):
    B, S, _ = xn.shape
    wa = MOBA_HEADS * HEAD_DIM
    wb = DIL_HEADS * HEAD_DIM
    qa, ka, va, qb, kb, vb = jnp.split(xn @ w_in, [wa, 2 * wa, 3 * wa, 3 * wa + wb, 3 * wa + 2 * wb], axis=-1)
    oa = _moba(_rms(_heads(qa, MOBA_HEADS), qn_a), _rms(_heads(ka, MOBA_HEADS), kn_a), _heads(va, MOBA_HEADS), rel_bias[:, :MOBA_HEADS].T)
    ob = _dilated(_rms(_heads(qb, DIL_HEADS), qn_b), _rms(_heads(kb, DIL_HEADS), kn_b), _heads(vb, DIL_HEADS), rel_bias[:, MOBA_HEADS:].T)
    o = jnp.concatenate([oa, ob], axis=1).transpose(0, 2, 1, 3).reshape(B, S, D_MODEL)
    return o @ w_out

def _mixer_nsa(xn, w_in, w_out, qn, kn_c, kn_s, kn_w, cmp_k, cmp_v, rel_bias):
    B, S, _ = xn.shape
    qw = NSA_HEADS * HEAD_DIM
    kvw = NSA_GROUPS * HEAD_DIM
    q, kc, vc, ks, vs, kw, vw, g = jnp.split(xn @ w_in, [qw + i * kvw for i in range(7)], axis=-1)
    q = _rms(_heads(q, NSA_HEADS), qn)
    kc = _rms(_compress(_heads(kc, NSA_GROUPS), *cmp_k), kn_c)
    vc = _compress(_heads(vc, NSA_GROUPS), *cmp_v)
    ks = _rms(_heads(ks, NSA_GROUPS), kn_s)
    kw = _rms(_heads(kw, NSA_GROUPS), kn_w)
    gates = jax.nn.sigmoid(g.astype(F32)).reshape(B, S, NSA_HEADS, 3).transpose(0, 2, 1, 3)
    o = _nsa(q, kc, vc, ks, _heads(vs, NSA_GROUPS), kw, _heads(vw, NSA_GROUPS), gates, rel_bias.T)
    return o.transpose(0, 2, 1, 3).reshape(B, S, D_MODEL) @ w_out

def _swiglu(x, wg, wu, wd):
    return (jax.nn.silu(x @ wg) * (x @ wu)) @ wd

def second_inputs(seed: int = 0) -> dict:
    key = jax.random.key(seed)
    keys = iter(jax.random.split(key, 40))

    def nrm(shape, scale):
        return jax.random.normal(next(keys), shape, F32) * scale

    def gain(shape):
        return 1.0 + nrm(shape, 0.02)

    D, hd, F, CH = D_MODEL, HEAD_DIM, FFN_HIDDEN, NSA_CMP_HIDDEN
    res = (2 * DEPTH) ** -0.5
    w_ab = 3 * (MOBA_HEADS + DIL_HEADS) * hd
    w_nsa = NSA_HEADS * hd + 6 * NSA_GROUPS * hd + 3 * NSA_HEADS
    cin = NSA_CMP_LEN * hd
    return {
        'x': nrm((BATCH, SEQ, D), 1.0),
        'p': nrm((DEPTH, BATCH, SEQ, PLE_DIM), 1.0),
        'rel_bias': nrm((REL_BUCKETS, N_HEADS), 0.5),
        'norm_mix': gain((DEPTH, D)),
        'norm_ffn': gain((DEPTH, D)),
        'norm_ple': gain((DEPTH, D)),
        'w_ffn_gate': nrm((DEPTH, D, F), D ** -0.5),
        'w_ffn_up': nrm((DEPTH, D, F), D ** -0.5),
        'w_ffn_down': nrm((DEPTH, F, D), F ** -0.5 * res),
        'w_ple_proj': nrm((DEPTH, PLE_DIM, D), PLE_DIM ** -0.5 * res),
        'w_ple_gate': nrm((DEPTH, D, D), D ** -0.5),
        'w_in_ab': nrm((N_EVEN, D, w_ab), D ** -0.5),
        'w_out_ab': nrm((N_EVEN, D, D), D ** -0.5 * res),
        'qn_moba': gain((N_EVEN, hd)),
        'kn_moba': gain((N_EVEN, hd)),
        'qn_dil': gain((N_EVEN, hd)),
        'kn_dil': gain((N_EVEN, hd)),
        'w_in_nsa': nrm((N_ODD, D, w_nsa), D ** -0.5),
        'w_out_nsa': nrm((N_ODD, D, D), D ** -0.5 * res),
        'qn_nsa': gain((N_ODD, hd)),
        'kn_cmp': gain((N_ODD, hd)),
        'kn_slc': gain((N_ODD, hd)),
        'kn_win': gain((N_ODD, hd)),
        'cmp_k_pos': nrm((N_ODD, NSA_CMP_LEN, hd), 0.1),
        'cmp_k_w1': nrm((N_ODD, cin, CH), cin ** -0.5),
        'cmp_k_b1': nrm((N_ODD, CH), 0.01),
        'cmp_k_w2': nrm((N_ODD, CH, hd), CH ** -0.5),
        'cmp_k_b2': nrm((N_ODD, hd), 0.01),
        'cmp_v_pos': nrm((N_ODD, NSA_CMP_LEN, hd), 0.1),
        'cmp_v_w1': nrm((N_ODD, cin, CH), cin ** -0.5),
        'cmp_v_b1': nrm((N_ODD, CH), 0.01),
        'cmp_v_w2': nrm((N_ODD, CH, hd), CH ** -0.5),
        'cmp_v_b2': nrm((N_ODD, hd), 0.01),
    }

def second_block(x, p, rel_bias, norm_mix, norm_ffn, norm_ple, w_ffn_gate, w_ffn_up, w_ffn_down,
              w_ple_proj, w_ple_gate, w_in_ab, w_out_ab, qn_moba, kn_moba, qn_dil, kn_dil,
              w_in_nsa, w_out_nsa, qn_nsa, kn_cmp, kn_slc, kn_win,
              cmp_k_pos, cmp_k_w1, cmp_k_b1, cmp_k_w2, cmp_k_b2,
              cmp_v_pos, cmp_v_w1, cmp_v_b1, cmp_v_w2, cmp_v_b2):
    h = x
    for i in range(DEPTH):
        e = i // 2
        xn = _rms(h, norm_mix[i])
        if i % 2 == 0:
            mix = _mixer_ab(xn, w_in_ab[e], w_out_ab[e], qn_moba[e], kn_moba[e], qn_dil[e], kn_dil[e], rel_bias)
        else:
            cmp_k = (cmp_k_pos[e], cmp_k_w1[e], cmp_k_b1[e], cmp_k_w2[e], cmp_k_b2[e])
            cmp_v = (cmp_v_pos[e], cmp_v_w1[e], cmp_v_b1[e], cmp_v_w2[e], cmp_v_b2[e])
            mix = _mixer_nsa(xn, w_in_nsa[e], w_out_nsa[e], qn_nsa[e], kn_cmp[e], kn_slc[e], kn_win[e], cmp_k, cmp_v, rel_bias)
        h = h + mix.astype(h.dtype)
        h = h + _swiglu(_rms(h, norm_ffn[i]), w_ffn_gate[i], w_ffn_up[i], w_ffn_down[i])
        gate = jax.nn.sigmoid(_rms(h, norm_ple[i]) @ w_ple_gate[i])
        h = h + gate * (p[i] @ w_ple_proj[i])
    return h


def setup_inputs(seed=0):
    out = dict(first_inputs(seed))
    for name, value in second_inputs(seed + 1).items():
        if name != "x":
            out[name + "_2"] = value
    return out


def reference(
    x, c, ctx, c_ctx, norm_g, ada_w, ada_b, ffn1_wi, ffn1_wo, ffn2_wi, ffn2_wo, conv_pw1_w,
    conv_pw1_b, conv_dw_w, conv_dw_b, conv_ln_g, conv_ln_b, conv_pw2_w, conv_pw2_b, attn_w_qkv,
    attn_w_o, attn_sink, final_g, p_2, rel_bias_2, norm_mix_2, norm_ffn_2, norm_ple_2,
    w_ffn_gate_2, w_ffn_up_2, w_ffn_down_2, w_ple_proj_2, w_ple_gate_2, w_in_ab_2, w_out_ab_2,
    qn_moba_2, kn_moba_2, qn_dil_2, kn_dil_2, w_in_nsa_2, w_out_nsa_2, qn_nsa_2, kn_cmp_2,
    kn_slc_2, kn_win_2, cmp_k_pos_2, cmp_k_w1_2, cmp_k_b1_2, cmp_k_w2_2, cmp_k_b2_2,
    cmp_v_pos_2, cmp_v_w1_2, cmp_v_b1_2, cmp_v_w2_2, cmp_v_b2_2,
):
    x = first_block(
        x, c, ctx, c_ctx, norm_g, ada_w, ada_b, ffn1_wi, ffn1_wo, ffn2_wi, ffn2_wo, conv_pw1_w,
        conv_pw1_b, conv_dw_w, conv_dw_b, conv_ln_g, conv_ln_b, conv_pw2_w, conv_pw2_b,
        attn_w_qkv, attn_w_o, attn_sink, final_g,
    )
    return second_block(
        x, p_2, rel_bias_2, norm_mix_2, norm_ffn_2, norm_ple_2, w_ffn_gate_2, w_ffn_up_2,
        w_ffn_down_2, w_ple_proj_2, w_ple_gate_2, w_in_ab_2, w_out_ab_2, qn_moba_2, kn_moba_2,
        qn_dil_2, kn_dil_2, w_in_nsa_2, w_out_nsa_2, qn_nsa_2, kn_cmp_2, kn_slc_2, kn_win_2,
        cmp_k_pos_2, cmp_k_w1_2, cmp_k_b1_2, cmp_k_w2_2, cmp_k_b2_2, cmp_v_pos_2, cmp_v_w1_2,
        cmp_v_b1_2, cmp_v_w2_2, cmp_v_b2_2,
    )


_drawn_inputs = setup_inputs


def setup_inputs(seed=0):
    import zlib

    import numpy as np

    out = dict(_drawn_inputs(seed))
    spreads = {}
    factors = {'conv_pw1_b': 8.0,
     'conv_dw_b': 5.316,
     'conv_ln_b': 7.179,
     'conv_pw2_b': 4.038,
     'attn_sink': 8.0,
     'norm_mix_2': 8.0,
     'norm_ffn_2': 5.176,
     'norm_ple_2': 200.0,
     'qn_moba_2': 8.0,
     'kn_moba_2': 8.0,
     'qn_dil_2': 8.0,
     'kn_dil_2': 8.0,
     'qn_nsa_2': 8.0,
     'kn_cmp_2': 100.314,
     'kn_slc_2': 8.0,
     'kn_win_2': 8.0,
     'cmp_k_pos_2': 8.0,
     'cmp_k_b1_2': 64.0,
     'cmp_k_b2_2': 187.564,
     'cmp_v_pos_2': 24.371,
     'cmp_v_b1_2': 200.0,
     'cmp_v_b2_2': 64.0}
    for name, (base, spread) in spreads.items():
        noise = np.random.default_rng([zlib.crc32(name.encode()), seed]).standard_normal(out[name].shape)
        drawn = base * np.exp(spread * noise) if base else spread * noise
        out[name] = jnp.asarray(drawn.astype(out[name].dtype))
    for name, factor in factors.items():
        out[name] = (out[name] * factor).astype(out[name].dtype)
    return out
```

```python
from contextlib import ExitStack

import numpy as np

import concourse.bass as bass
from concourse import mybir

F32 = mybir.dt.float32
F32R = mybir.dt.float32r
ALU = mybir.AluOpType
ACT = mybir.ActivationFunctionType
AX = mybir.AxisListType

P = 128
D = 1024
DT = D // P
S = 256
HID = 2816
HT = HID // P
NH, HD, NKV = 16, 64, 4
SLAB_K, SLAB_N = 8, 256
SLAB = SLAB_K * SLAB_N
FIRST, SECOND = slice(0, SLAB // 2), slice(SLAB // 2, SLAB)
CONV_W = 31
PAD = (CONV_W - 1) // 2
SP_ = S + 2 * PAD
NCMP = (S - 32) // 16 + 1
EPS = 1e-6
MASKED = -1.0e30
LOWEST = -3.0e38


def rel_bucket(dist):
    n = np.maximum(dist, 0)
    nf = np.maximum(n, 1).astype(np.float32)
    large = 16 + (np.log(nf / np.float32(16)) / np.float32(np.log(2048 / 16)) * 16).astype(np.int32)
    return np.where(n < 16, n, np.minimum(large, 31))


def line_tables():
    m = np.arange(384)
    d = 255 - m
    hot = (rel_bucket(d)[None, :] == np.arange(32)[:, None]) & (d >= 0)[None, :]
    count = np.zeros(384)
    for window, dil in ((128, 1), (512, 4), (2048, 16)):
        count += (d >= 0) & (d % dil == 0) & (d // dil <= window // dil)
    causal = np.where(d >= 0, 0.0, MASKED)
    dilated = np.where(count > 0, np.log(np.maximum(count, 1)), MASKED)
    t = np.zeros((33, 2, 384), np.float32)
    t[:32] = hot[:, None, :]
    t[32, 0], t[32, 1] = causal, dilated
    return t.reshape(33, 768)


def rope_tables():
    p = np.arange(P) % HD
    inv = (np.float32(10000.0) ** (-np.arange(16, dtype=np.float32) / 16)).astype(np.float32)
    tok = np.arange(S)
    pos = np.stack([tok // 64, tok % 64]).astype(np.float32)
    ang = pos[p // 32] * inv[p % 16][:, None]
    c, s = np.cos(ang), np.sin(ang)
    scale = HD ** -0.5
    return np.stack([c * scale, s * scale, c, s], 1).astype(np.float32).reshape(P, 4 * S)


def small_constants():
    i = np.arange(P)
    ident = np.eye(P)
    blocks = (i[:, None] // HD == i[None, :] // HD)
    rot = np.zeros((P, P))
    for q in range(P):
        if (q // 16) % 2 == 0:
            rot[q + 16, q] = -1.0
        else:
            rot[q - 16, q] = 1.0
    t = i[:, None, None] + P * np.arange(2)[None, :, None]
    valid = (t - (16 * np.arange(NCMP) + 31)[None, None, :]) >= 0
    pick = np.zeros((P, 2))
    pick[[0, 2], 0] = 1
    pick[[1, 3], 1] = 1
    return np.concatenate([ident, blocks, np.ones((P, P)), rot, valid.reshape(P, -1), pick], 1).astype(np.float32)


def window_mask():
    q = np.arange(P)[:, None, None] + P * np.arange(2)[None, :, None]
    k = np.arange(S)[None, None, :]
    m = np.zeros((P, 2, 2 * S), np.float32)
    m[:, :, :S] = np.where(np.abs(q - k) <= 128, 0.0, MASKED)
    return m.reshape(P, -1)


VECTORS = [("norm_g", 6 * DT), ("ada_b", 144), ("final_g", DT), ("pw1_b", 16), ("dw_b", DT), ("ln_g", DT),
           ("ln_b", DT), ("pw2_b", DT), ("dw_w", CONV_W * DT), ("c", DT), ("c_ctx", DT), ("norm_mix", 2 * DT),
           ("norm_ffn", 2 * DT), ("norm_ple", 2 * DT), ("qk_gain_ab", 8), ("qk_gain_nsa", 6), ("kn_cmp", 1),
           ("cmp_b1", 2), ("cmp_k_b2", 1), ("cmp_pos", 32), ("sink", NH)]
VCOL = {}
_at = 0
for _name, _n in VECTORS:
    VCOL[_name] = _at
    _at += _n
NVEC = _at
NCONST = 4 * P + 2 * NCMP + 2


class Stage:

    def __init__(self, kind, slabs=0, T=S, mod=None, layer=0, ada=0, gate=None, how=None, gain=None, what=None):
        self.kind, self.slabs, self.T, self.mod, self.layer = kind, slabs, T, mod, layer
        self.ada, self.gate, self.how, self.gain, self.what = ada, gate, how, gain, what


def ffn_stages(layer, tokens, ada=0, mod=None):
    return [Stage("up", 22 + ada, T=tokens, ada=ada), Stage("down", 12, T=tokens, mod=mod)]


def make_plan():
    st = [Stage("start"), Stage("ada", 12)]
    both = 2 * S
    for layer in range(2):
        st += [Stage("mods", mod=0, layer=layer),
               Stage("norm", T=both, how="mod", mod=0)]
        st += ffn_stages(layer, both, ada=22 if layer == 0 else 16, mod=0)
        st += [Stage("mods", mod=1, layer=layer),
               Stage("norm", T=both, how="mod", mod=1)]
        if layer == 1:
            st.insert(-1, Stage("mods", mod=2, layer=1))
        if layer == 0:
            st += [Stage("pw1", 8, T=both), Stage("conv"), Stage("pw2", 4, T=both, mod=1),
                   Stage("mods", mod=2, layer=0, gate=False),
                   Stage("norm", T=both, how="mod", mod=2),
                   Stage("up", 44, T=both, ada=22), Stage("mods", mod=2, layer=0, gate=True),
                   Stage("down", 12, T=both, mod=2)]
        else:
            st += [Stage("qkv", 6), Stage("att", what="window"), Stage("wo", 4, T=S, mod=1),
                   Stage("norm", T=S, how="mod", mod=2)]
            st += ffn_stages(1, S, mod=2)
    st += [Stage("norm", T=S, how="final")]
    for layer in range(2):
        st += [Stage("norm", T=S, how="gain", gain=VCOL["norm_mix"] + DT * layer)]
        if layer == 0:
            st += [Stage("qknorm", 8, gain=VCOL["qk_gain_ab"]), Stage("vab", 4), Stage("att", what="ab")]
        else:
            st += [Stage("qknorm", 6, gain=VCOL["qk_gain_nsa"]), Stage("nsakv", 5), Stage("cmp", 2),
                   Stage("att", what="nsa")]
        st += [Stage("wo", 4, T=S, mod=None),
               Stage("norm", T=S, how="gain", gain=VCOL["norm_ffn"] + DT * layer)]
        st += ffn_stages(layer, S)
        st += [Stage("norm", T=S, how="gain", gain=VCOL["norm_ple"] + DT * layer),
               Stage("pleproj", 1, layer=layer), Stage("plegate", 4, layer=layer)]
    st += [Stage("end")]
    return st


def plan_with_counts():
    at = dict(n=0, m=0, u=0, h=0, sq=0, sum=0, std=0, g=0, q=0, att=0, qk=0)
    plan = make_plan()
    made = 0
    for st in plan:
        st.made = made
        st.n0, st.m0, st.g0, st.q0, st.qk0, st.att0 = at["n"], at["m"], at["g"], at["q"], at["qk"], at["att"]
        st.u0, st.h0, st.sq0, st.sum0, st.std0 = at["u"], at["h"], at["sq"], at["sum"], at["std"]
        at["n"] += st.slabs
        groups = dict(up=22, pw1=8, down=4, pw2=4, wo=4, plegate=4, pleproj=4, conv=2, cmp=2)
        at["m"] += st.slabs if st.kind in ("qkv", "qknorm", "vab", "nsakv") else groups.get(st.kind, 0)
        if st.kind == "up":
            at["g"] += 11
            at["q"] += st.ada
        elif st.kind == "ada":
            at["q"] += st.slabs
        elif st.kind == "norm":
            st.items = 2 * DT if (st.how == "mod" and st.T == 2 * S) else DT
            at["u"] += st.items
            at["h"] += st.items if st.how != "final" else 0
            made = st.items
        elif st.kind == "conv":
            at["u"] += DT
            at["h"] += DT
            made = DT
        elif st.kind == "att":
            at["att"] += 1
        elif st.kind == "qknorm":
            at["qk"] += st.slabs
            at["sum"] += st.slabs
            at["std"] += st.slabs
        if st.kind in ("norm", "conv"):
            at["sq"] += DT
            at["sum"] += DT
            at["std"] += 1
    return plan, at["n"]


def landed(n):
    return 16 * (n // 2 + 1)


def room(m):
    return 1 + m // 2


def freed(m):
    return 2 + m // 2


class Steps:

    def __init__(self, eng, sem):
        self.eng, self.sem, self.n, self.dyn = eng, sem, 0, 0

    def done(self, ins):
        ins.then_inc(self.sem, 1)
        self.n += 1
        self.eng.wait_ge(self.sem, self.n + self.dyn)

    def mark(self, ins):
        ins.then_inc(self.sem, 1)
        self.n += 1
        return self.n + self.dyn

    def loop(self, i, per):
        self.dyn = i * per

    def end(self, per, times):
        self.dyn = 0
        self.n += per * (times - 1)


def across(ap, n, at=1):
    dims = [list(x) for x in ap.ap]
    dims.insert(at, [0, n])
    return bass.AP(ap.tensor, ap.offset, dims)


def build(nc, slabs_d, x_d, vec_d, const_d, w2_d, tab_d, hot_d, rope_d, mask_d, p_d, out_d, stop_after=None):
    plan, NS = plan_with_counts()
    if stop_after is not None:
        end = plan[stop_after]
        end.kind = "end"
        plan = plan[:stop_after] + [end]
        NS = plan[-2].n0 + plan[-2].slabs + 2
    lines_d = nc.dram_tensor("lines_dram", (NH, 768), F32, kind="Internal").ap()
    skew_d = nc.dram_tensor("skew_dram", (P, 2 * NH * 384), F32, kind="Internal").ap()

    with ExitStack() as ctx:
        def sb(name, shape, dt=F32, where=ctx):
            return where.enter_context(nc.sbuf_tensor(name, shape, dt))

        def sem(name):
            return ctx.enter_context(nc.semaphore(name))

        x = sb("x", [P, DT, 2 * S])
        hhi = sb("hhi", [P, DT, 2 * S], F32R)
        hlo = sb("hlo", [P, DT, 2 * S], F32R)
        raw = sb("raw", [P, 2, SLAB])
        whi = sb("whi", [P, 2, SLAB], F32R)
        wlo = sb("wlo", [P, 2, SLAB], F32R)
        const = sb("const", [P, NCONST])
        vec = sb("vec", [P, NVEC])
        w2 = sb("w2", [P, 256])
        gate_sb = sb("gate_sb", [P, 2, 512])
        prod = sb("prod", [P, 2, 512])
        rs = sb("rs", [P, 2 * S])
        mA = sb("mA", [P, 3, DT, 2])
        mB = sb("mB", [P, 3, DT, 2])
        mG = sb("mG", [P, 3, DT, 2])
        cs = sb("cs", [P, DT, 2])
        c4 = sb("c4", [P, DT, 4], F32R)
        arow = sb("arow", [4, 2, SLAB_N])
        eps = sb("eps", [P, 1])
        tab = sb("tab", [33, NH])
        gb = sb("gb", [P, DT, 2])
        junk = sb("junk", [P, 1])

        with ExitStack() as ffn:
            ghi = sb("ghi", [P, HT, 2 * S], F32R, ffn)
            glo = sb("glo", [P, HT, 2 * S], F32R, ffn)
        with ExitStack() as first:
            hot = sb("hot", [33, 768], F32, first)
            lines = sb("line_rows", [NH, 768], F32, first)
        with ExitStack() as cv:
            ubuf = sb("ubuf", [P, DT, 2, SP_], F32, cv)
            v = sb("v", [P, DT, 2 * S], F32, cv)
            diag = sb("diag", [P, 2, 4, P], F32, cv)
        with ExitStack() as at:
            ohi = sb("ohi", [P, DT, S], F32R, at)
            olo = sb("olo", [P, DT, S], F32R, at)
            QK = sb("QK", [P, 16, S], F32, at)
            kd = sb("kd", [P, 2 * NKV, S], F32, at)
            vt = sb("vt", [P, 2048], F32, at)
            sc = sb("sc", [P, 4, 512], F32, at)
            pT = sb("pT", [P, 2, 512], F32, at)
            stt4 = sb("stt4", [P, 4, 10], F32, at)
            with ExitStack() as w:
                kraw = sb("kraw", [P, 2, 512], F32, w)
                rope = sb("rope", [P, 4, S], F32, w)
                mask = sb("mask", [P, 2, 512], F32, w)
            bt = sb("bt", [P, NH, S], F32, at)
            craw = kd[:, :, :].rearrange("p (a b) t -> p a b t", a=2)
            Vm = sb("Vm", [P, NH, HD], F32, at)
            Pc = sb("Pc", [P, 2, NH, 32], F32, at)
            PcT = sb("PcT", [P, NKV, 2, P], F32, at)
            hid = sb("hid", [P, 2, 4, 16], F32, at)
            kcmp = sb("kcmp", [P, 4, 16], F32, at)
            kcsq = sb("kcsq", [P, 64], F32, at)
            kcr = sb("kcr", [P, 64], F32, at)
            vcmp = sb("vcmp", [16, NKV, HD], F32, at)
            gates = sb("gates", [P, 2, 48], F32, at)
            cst = sb("cst", [P, 3, NH], F32, at)
        with ExitStack() as cm:
            bhi = sb("bhi", [P, 2, 16, 64], F32R, cm)
            blo = sb("blo", [P, 2, 16, 64], F32R, cm)
        blk = sc[:, :, :].rearrange("p a (b c) -> p (a b) c", c=64).rearrange("p (k l) c -> p k l c", k=2)
        with ExitStack() as pl:
            pT_raw = sb("ptok", [P, 2, S], F32, pl)
            phi = sb("phi", [P, 2, S], F32R, pl)
            plo = sb("plo", [P, 2, S], F32R, pl)
            pp = sb("pp", [P, DT, S], F32, pl)
        ident = const[:, 0:P]
        headones = const[:, P:2 * P]
        ones = const[:, 2 * P:3 * P]
        rot = const[:, 3 * P:4 * P]
        pick = const[0:4, NCONST - 2:NCONST]
        valid = const[:, 4 * P:NCONST - 2].rearrange("p (q c) -> p q c", q=2)
        sq = gate_sb
        ub = prod[:, :, :].rearrange("p a (b c) -> p (a b) c", c=S)

        acc = ctx.enter_context(nc.psum_tensor("acc", [P, 2, 2, 512], F32))
        Mod = ctx.enter_context(nc.psum_tensor("Mod", [P, 512], F32))
        B = [Mod] + [ctx.enter_context(nc.psum_tensor(f"bank{i}", [P, 512], F32)) for i in (5, 6, 7)]
        sums = B[1]

        slab_landed = [sem("slab_landed0"), sem("slab_landed1")]
        hi_half = sem("hi_half")
        hi_ready = sem("hi_ready")
        lo_half = sem("lo_half")
        lo_ready = sem("lo_ready")
        half_used = sem("half_used")
        slab_used = sem("slab_used")
        acc_free = [sem("acc_free0"), sem("acc_free1")]
        loaded = sem("loaded")
        const_landed = sem("const_landed")
        eps_ready = sem("eps_ready")
        line_pe = sem("line_pe")
        c_ready = sem("c_ready")
        row_ready = sem("row_ready")
        row_turned = sem("row_turned")
        ple_pe = sem("ple_pe")
        ple_gate = sem("ple_gate")
        kd_dve = sem("kd_dve")
        kd_act = sem("kd_act")
        sq_ready = sem("sq_ready")
        sum_done = sem("sum_done")
        std_ready = sem("std_ready")
        u_ready = sem("u_ready")
        h_hi = sem("h_hi")
        h_ready = sem("h_ready")
        g_hi = sem("g_hi")
        g_lo = sem("g_lo")
        dve_step = sem("dve_step")
        act_step = sem("act_step")
        lines_ready = sem("lines_ready")
        lines_done = sem("lines_done")
        skew_done = sem("skew_done")
        diag_ready = sem("diag_ready")
        taps_used = sem("taps_used")
        conv_dve = sem("conv_dve")
        v_ready = sem("v_ready")
        mean_done = sem("mean_done")
        d_ready = sem("d_ready")
        qk_done = sem("qk_done")
        rot_done = sem("rot_done")
        rope_done = sem("rope_done")
        rope_landed = sem("rope_landed")
        bias_landed = sem("bias_landed")
        att_ready = sem("att_ready")
        s_ready = sem("s_ready")
        s_free = sem("s_free")
        m_ready = sem("m_ready")
        e_ready = sem("e_ready")
        p_ready = sem("p_ready")
        t_ready = sem("t_ready")
        pt_ready = sem("pt_ready")
        pv_done = sem("pv_done")
        o_hi = sem("o_hi")
        o_lo = sem("o_lo")
        cmp_pe = sem("cmp_pe")
        cmp_dve = sem("cmp_dve")
        cmp_act = sem("cmp_act")
        vm_landed = sem("vm_landed")
        vm_zero = sem("vm_zero")
        p_landed = sem("p_landed")
        p_hi = sem("p_hi")
        pool_go = sem("pool_go")
        stored = sem("stored")

        block = ctx.enter_context(nc.Block())

        def x_final(eng, st):
            m = st.m0
            if m:
                eng.wait_ge(acc_free[0], 1 + (m + 1) // 2)
                eng.wait_ge(acc_free[1], 1 + m // 2)
            if st.u0:
                eng.wait_ge(u_ready, st.u0)

        @block.sync
        def _(sp):
            sp.dma_start(raw[:, 0, :], slabs_d[0]).then_inc(slab_landed[0], 16)
            sp.dma_start(raw[:, 1, :], slabs_d[1]).then_inc(slab_landed[1], 16)
            with sp.Fori(0, (NS - 2) // 2) as i:
                for c in range(2):
                    sp.wait_ge(lo_ready, 2 * i + (c + 1))
                    sp.dma_start(raw[:, c, :], slabs_d[bass.ds(2 * i + (c + 2), 1)].rearrange("a p n -> p (a n)"))\
                      .then_inc(slab_landed[c], 16)
            if NS % 2:
                sp.wait_ge(lo_ready, NS - 2)
                sp.dma_start(raw[:, (NS - 1) % 2, :], slabs_d[NS - 1]).then_inc(slab_landed[(NS - 1) % 2], 16)
            x_final(sp, plan[-1])
            sp.dma_start(out_d, x[:, :, 0:S]).then_inc(stored, 16)
            sp.wait_ge(stored, 16)

        @block.gpsimd
        def _(pool):
            nc.gpsimd.memset(eps[:, :], EPS).then_inc(eps_ready, 1)
            nc.gpsimd.memset(tab[:, :], 1.0).then_inc(eps_ready, 1)
            pool.sem_inc(acc_free[0], 1)
            pool.sem_inc(acc_free[1], 1)
            pool.sem_inc(qk_done, 2)
            pool.sem_inc(s_free, 2)
            pool.sem_inc(pv_done, 2)
            pool.sem_inc(o_lo, 2)
            pool.sem_inc(pt_ready, 2)
            pool.sem_inc(t_ready, 4)
            pool.sem_inc(g_lo, 1)
            pool.wait_ge(eps_ready, 2)
            pool.dma_start(tab[0:32, :], tab_d).then_inc(loaded, 16)
            pool.dma_start(hot[:, :], hot_d).then_inc(loaded, 16)
            pool.wait_ge(lines_ready, 2)
            pool.dma_start(lines_d, lines[:, :]).then_inc(lines_done, 16)
            pool.wait_ge(lines_done, 16)
            pool.dma_start(skew_d, bass.AP(lines_d.tensor, 0, [[0, P], [1, NH * 768]])).then_inc(skew_done, 16)
            pool.wait_ge(skew_done, 16)

            def bias_rows(heads, kind):
                return bass.AP(skew_d.tensor, 384 * (2 * heads.start + kind) + 127,
                               [[2 * NH * 384 - 1, P], [768, len(heads)], [1, S]])

            go = 0
            for st in plan:
                if st.kind == "qkv":
                    go += 1
                    pool.wait_ge(pool_go, go)
                    pool.dma_start(rope[:, :, :], rope_d.rearrange("p (a t) -> p a t", a=4)).then_inc(rope_landed, 16)
                    pool.dma_start(mask[:, :, :], mask_d.rearrange("p (a t) -> p a t", a=2)).then_inc(rope_landed, 16)
                if st.kind == "qknorm":
                    go += 1
                    pool.wait_ge(pool_go, go)
                    ab = st.slabs == 8
                    pool.dma_start(bt[:, 0:8, :], bias_rows(range(0, 8), 0)).then_inc(bias_landed, 16)
                    pool.dma_start(bt[:, 8:16, :], bias_rows(range(8, 16), 1 if ab else 0)).then_inc(bias_landed, 16)
                    if not ab:
                        nc.gpsimd.memset(Vm[:, :, :], 0.0).then_inc(vm_zero, 1)
                        nc.gpsimd.memset(Pc[:, :, :, :], 0.0).then_inc(vm_zero, 1)
                if st.kind == "cmp":
                    pool.wait_ge(vm_zero, 2)
                    pool.wait_ge(cmp_dve, 5)
                    for hl in range(4):
                        pool.dma_start(Vm[32 * hl:32 * hl + NCMP, hl:NH:4, :], vcmp[0:NCMP, :, :])\
                            .then_inc(vm_landed, 16)
                if st.kind == "pleproj":
                    go += 1
                    pool.wait_ge(pool_go, go)
                    pool.dma_start(pT_raw[:, :, :], p_d[st.layer]).then_inc(p_landed, 16)

        @block.scalar
        def _(act):
            step = Steps(act, act_step)
            act.dma_start(x[:, :, :], x_d).then_inc(const_landed, 16)
            act.dma_start(const[:, :], const_d).then_inc(const_landed, 16)
            act.dma_start(vec[:, :], vec_d).then_inc(const_landed, 16)
            act.dma_start(w2[:, :], w2_d).then_inc(const_landed, 16)

            def hi(n, i=0, per=0):
                if n >= NS:
                    return
                act.wait_ge(slab_landed[n % 2], landed(n) + i * (8 * per))
                for cols, used, ready in ((FIRST, half_used, hi_half), (SECOND, slab_used, hi_ready)):
                    if n >= 2:
                        act.wait_ge(used, n - 1 + i * per)
                    nc.scalar.activation(whi[:, n % 2, cols], raw[:, n % 2, cols], ACT.Copy).then_inc(ready, 1)

            def start(st):
                act.wait_ge(const_landed, 64)
                act.wait_ge(eps_ready, 2)
                step.done(nc.scalar.activation(cs[:, :, 0], vec[:, VCOL["c"]:VCOL["c"] + DT], ACT.Silu))
                step.done(nc.scalar.activation(cs[:, :, 1], vec[:, VCOL["c_ctx"]:VCOL["c_ctx"] + DT], ACT.Silu))
                nc.scalar.activation(c4[:, :, 0:2], cs[:, :, :], ACT.Copy).then_inc(c_ready, 1)
                hi(0)
                hi(1)

            def ada_row(n, q, i, per):
                act.wait_ge(slab_used, n + 1 + i * per)
                if q >= 2:
                    act.wait_ge(row_turned, q - 1 + 2 * i)
                nc.scalar.activation(arow[:, q % 2, :], B[2 + q % 2][0:4, 0:SLAB_N], ACT.Copy).then_inc(row_ready, 1)

            def ada(st):
                for c in range(2):
                    ada_row(st.n0 + c, st.q0 + c, 0, 0)
                    hi(st.n0 + c + 2)
                with act.Fori(0, st.slabs // 2 - 1) as i:
                    for c in range(2):
                        ada_row(st.n0 + c + 2, st.q0 + c + 2, i, 2)
                        hi(st.n0 + c + 4, i, 2)

            def up(st):
                both = st.ada // 2
                act.wait_ge(lines_done, 16)
                for first, count, per in ((0, both, 4), (both, 11 - both, 2)):
                    if not count:
                        continue
                    n = st.n0 + 4 * first
                    m = st.m0 + 2 * first
                    with act.Fori(0, count) as i:
                        hi(n + 2, i, per)
                        act.wait_ge(acc_free[(m + 1) % 2], room(m + 1) + i)
                        nc.scalar.activation(gate_sb[:, :, 0:st.T], acc[:, m % 2, :, 0:st.T], ACT.Silu)\
                            .then_inc(acc_free[m % 2], 1)
                        hi(n + 3, i, per)
                        if per == 4:
                            ada_row(n + 1, st.q0, i, per)
                            hi(n + 4, i, per)
                            ada_row(n + 2, st.q0 + 1, i, per)
                            hi(n + 5, i, per)
                        act.wait_ge(acc_free[(m + 1) % 2], freed(m + 1) + i)
                        nc.scalar.activation(ghi[:, bass.ds(2 * first + 2 * i, 2), 0:st.T], prod[:, :, 0:st.T],
                                             ACT.Copy).then_inc(g_hi, 1)

            def residual(st):
                per = st.slabs // 2
                with act.Fori(0, 2) as i:
                    for c in range(per):
                        hi(st.n0 + 2 + c, i, per)

            def norm(st):
                x_final(act, st)
                T = st.T
                for c in range(DT):
                    if c >= 2:
                        act.wait_ge(sum_done, st.sum0 + c - 1)
                    nc.scalar.activation(sq[:, c % 2, 0:T], x[:, c, 0:T], ACT.Square).then_inc(sq_ready, 1)
                act.wait_ge(sum_done, st.sum0 + 8)
                nc.scalar.activation(rs[:, 0:T], sums[:, 0:T], ACT.Sqrt, bias=eps[:, 0:1], scale=1.0 / D)\
                    .then_inc(std_ready, 1)
                if st.how == "final":
                    return
                for k in range(st.items):
                    act.wait_ge(u_ready, st.u0 + k + 1)
                    c, s = (k // 2, k % 2) if st.items == 2 * DT else (k, 0)
                    dst = hhi[:, c, S * s:S * s + S]
                    if st.how == "mod":
                        ins = nc.scalar.activation(dst, ub[:, k % 4, :], ACT.Identity,
                                                   bias=mB[:, st.mod, c, s:s + 1])
                    else:
                        ins = nc.scalar.activation(dst, ub[:, k % 4, :], ACT.Copy)
                    ins.then_inc(h_hi, 1)

            def pw1(st):
                with act.Fori(0, 4) as i:
                    act.wait_ge(slab_used, st.n0 + 1 + 2 * i)
                    act.wait_ge(acc_free[(st.m0 + 1) % 2], room(st.m0 + 1) + i)
                    for t in range(2):
                        ins = nc.scalar.activation(gate_sb[:, t, :], acc[:, st.m0 % 2, t, :], ACT.Sigmoid,
                                                   bias=vec[:, bass.ds(VCOL["pw1_b"] + DT + t + 2 * i, 1)])
                    ins.then_inc(acc_free[st.m0 % 2], 1)
                    hi(st.n0 + 2, i, 2)
                    hi(st.n0 + 3, i, 2)

            def conv(st):
                def tap(t, par, wait):
                    if wait is not None:
                        act.wait_ge(taps_used, wait)
                    for j in range(4):
                        ins = nc.scalar.activation(diag[:, par, j, :], ident, ACT.Copy,
                                                   scale=vec[:, bass.ds(VCOL["dw_w"] + CONV_W * j + t, 1)])
                    ins.then_inc(diag_ready, 1)

                tap(0, 0, None)
                tap(1, 1, None)
                with act.Fori(0, 14) as i:
                    tap(2 * i + 2, 0, 2 * i + 1)
                    tap(2 * i + 3, 1, 2 * i + 2)
                tap(30, 0, 29)
                act.wait_ge(taps_used, 31)
                for j in range(4):
                    ins = nc.scalar.activation(v[:, j, :], acc[:, j // 2, j % 2, :], ACT.Identity,
                                               bias=vec[:, VCOL["dw_b"] + j:VCOL["dw_b"] + j + 1])
                    if j % 2:
                        ins.then_inc(acc_free[j // 2], 1)
                for c in range(DT):
                    act.wait_ge(d_ready, c + 1)
                    if c >= 2:
                        act.wait_ge(sum_done, st.sum0 + c - 1)
                    nc.scalar.activation(sq[:, c % 2, :], v[:, c, :], ACT.Square).then_inc(sq_ready, 1)
                act.wait_ge(sum_done, st.sum0 + 8)
                nc.scalar.activation(rs[:, :], sums[:, :], ACT.Sqrt, bias=eps[:, 0:1], scale=1.0 / D)\
                    .then_inc(std_ready, 1)
                for c in range(DT):
                    act.wait_ge(u_ready, st.u0 + c + 1)
                    if c >= 2:
                        act.wait_ge(h_ready, st.h0 + c - 1)
                    step.done(nc.scalar.activation(sq[:, c % 2, :], v[:, c, :], ACT.Silu,
                                                   bias=vec[:, VCOL["ln_b"] + c:VCOL["ln_b"] + c + 1]))
                    nc.scalar.activation(hhi[:, c, :], sq[:, c % 2, :], ACT.Copy).then_inc(h_hi, 1)

            def qkv(st):
                for c in range(6):
                    n, m = st.n0 + c, st.m0 + c
                    act.wait_ge(slab_used, n + 1)
                    a = acc[:, m % 2]
                    if c < 4:
                        ins = nc.scalar.activation(QK[:, 2 * c:2 * c + 2, :], a[:, :, 0:S], ACT.Copy)
                    elif c == 4:
                        ins = nc.scalar.activation(kraw[:, :, :], a, ACT.Copy)
                    else:
                        ins = nc.scalar.activation(vt[:, 0:1024], a.rearrange("p a b -> p (a b)"), ACT.Copy)
                    ins.then_inc(acc_free[m % 2], 1)
                    hi(n + 2)

            def qknorm(st):
                n, m = st.n0, st.m0
                with act.Fori(0, st.slabs // 2) as i:
                    for c in range(2):
                        act.wait_ge(slab_used, n + c + 1 + 2 * i)
                        nc.scalar.activation(QK[:, bass.ds(4 * i + 2 * c, 2), :], acc[:, (m + c) % 2, :, 0:S], ACT.Copy)
                        nc.scalar.activation(sq[:, c, :], acc[:, (m + c) % 2, :, 0:S], ACT.Square)\
                            .then_inc(acc_free[(m + c) % 2], 1)
                        hi(n + c + 2, i, 2)
                    for c in range(2):
                        act.wait_ge(sum_done, st.sum0 + c + 1 + 2 * i)
                        act.wait_ge(qk_done, st.qk0 + c + 1 + 2 * i)
                        nc.scalar.activation(prod[:, c, :], B[1 + c][:, :], ACT.Sqrt, bias=eps[:, 0:1],
                                             scale=1.0 / HD).then_inc(std_ready, 1)

            def vab(st):
                with act.Fori(0, 2) as i:
                    for c in range(2):
                        m = st.m0 + c
                        act.wait_ge(slab_used, st.n0 + c + 1 + 2 * i)
                        nc.scalar.activation(
                            vt[:, :].rearrange("p (a b) -> p a b", a=2)[:, :, bass.ds(512 * i + 256 * c, S)],
                            acc[:, m % 2, :, 0:S], ACT.Copy).then_inc(acc_free[m % 2], 1)
                        hi(st.n0 + c + 2, i, 2)

            def nsakv(st):
                for c in range(5):
                    n, m = st.n0 + c, st.m0 + c
                    act.wait_ge(slab_used, n + 1)
                    a = acc[:, m % 2, :, 0:S]
                    if c < 2:
                        for half in range(2):
                            for src in range(2):
                                ins = nc.scalar.activation(
                                    craw[64 * half:64 * half + 64, c, 2 * src:2 * src + 2, 0:S - 16 * half],
                                    acc[64 * src:64 * src + 64, m % 2, :, 16 * half:S], ACT.Copy)
                    elif c < 4:
                        ins = nc.scalar.activation(
                            vt[:, 0:1024].rearrange("p (a b) -> p a b", a=2)[:, :, 256 * (c - 2):256 * (c - 1)],
                            a, ACT.Copy)
                    else:
                        ins = nc.scalar.activation(gates[:, :, :], a[:, :, 0:48], ACT.Sigmoid)
                    ins.then_inc(acc_free[m % 2], 1)
                    hi(n + 2)

            def cmp_(st):
                act.wait_ge(cmp_dve, 2)
                nc.scalar.activation(bhi[:, :, :, :], blk, ACT.Copy).then_inc(cmp_act, 1)
                for kv in range(2):
                    m = st.m0 + kv
                    act.wait_ge(slab_used, st.n0 + kv + 1)
                    hi(st.n0 + kv + 2)
                    nc.scalar.activation(hid[:, kv, :, :].rearrange("p a b -> p (a b)"), acc[:, m % 2, 0, 0:64],
                                         ACT.Gelu_apprx_tanh, bias=vec[:, VCOL["cmp_b1"] + kv:VCOL["cmp_b1"] + kv + 1])\
                        .then_inc(acc_free[m % 2], 1)
                kf = kcmp[:, :, :].rearrange("p a b -> p (a b)")
                act.wait_ge(cmp_pe, 1)
                step.done(nc.scalar.activation(kf, B[1][:, 0:64], ACT.Identity,
                                               bias=vec[:, VCOL["cmp_k_b2"]:VCOL["cmp_k_b2"] + 1]))
                nc.scalar.activation(kcsq[:, :], kf, ACT.Square).then_inc(cmp_act, 1)
                act.wait_ge(cmp_pe, 3)
                nc.scalar.activation(kcr[:, :], B[2][:, 0:64], ACT.Sqrt, bias=eps[:, 0:1], scale=1.0 / HD)\
                    .then_inc(cmp_act, 1)
                for q, ncol in ((0, 7), (1, NCMP)):
                    act.wait_ge(cmp_dve, 6 + q)
                    nc.scalar.activation(Pc[:, q, :, 0:ncol], Pc[:, q, :, 0:ncol], ACT.Exp).then_inc(cmp_act, 1)
                for g in range(NKV):
                    act.wait_ge(cmp_pe, 8 + g)
                    nc.scalar.activation(PcT[:, g, :, :], B[1 + g % 2][:, 0:256], ACT.Copy).then_inc(cmp_act, 1)

            def copy_k(st):
                src = kraw if st.what == "window" else QK
                act.wait_ge(att_ready, st.att0 + 1)
                if st.what == "window":
                    for g in range(NKV):
                        ins = nc.scalar.activation(kd[0:64, 2 * g:2 * g + 2, :],
                                                   kraw[64 * (g % 2):64 * (g % 2) + 64, g // 2, :], ACT.Copy)
                else:
                    for j in range(8):
                        g = j % 4
                        ins = nc.scalar.activation(kd[0:64, j, :],
                                                   QK[64 * (g % 2):64 * (g % 2) + 64, 8 + 2 * (j // 4) + g // 2, :],
                                                   ACT.Copy)
                ins.then_inc(kd_act, 1)

            def att(st):
                if st.what != "ab":
                    copy_k(st)
                A0 = 32 * st.att0

                def exps(u, i):
                    q = u % 2
                    act.wait_ge(m_ready, A0 + u + 1 + 8 * i)
                    sp = stt4[:, u % 4]
                    keys = 512 if st.what == "window" else 128 * (q + 1)
                    for s in range(2 if st.what == "nsa" else 1):
                        ins = nc.scalar.activation(sc[:, u % 4, keys * s:keys * (s + 1)],
                                                   sc[:, u % 4, keys * s:keys * (s + 1)], ACT.Exp,
                                                   bias=sp[:, 2 + s:3 + s], accum_out=sp[:, 4 + s:5 + s])
                    if st.what == "window":
                        ins = nc.scalar.activation(sp[:, 6:7], vec[:, bass.ds(VCOL["sink"] + u // 2 + 4 * i, 1)],
                                                   ACT.Exp, bias=sp[:, 2:3])
                    ins.then_inc(e_ready, 1)

                def out_hi(pair, i):
                    o = A0 // 4 + pair + 2 * i
                    act.wait_ge(pv_done, 2 + A0 + 4 * pair + 4 + 8 * i)
                    nc.scalar.activation(ohi[:, bass.ds(pair + 2 * i, 1), :].rearrange("p a b -> p (a b)"),
                                         acc[:, pair, 0, 0:S], ACT.Copy).then_inc(o_hi, 1)

                with act.Fori(0, NKV) as i:
                    exps(0, i)
                    exps(1, i)
                    for u in range(8):
                        keys = 512 if st.what == "window" else 128 * (u % 2 + 1) * (2 if st.what == "nsa" else 1)
                        act.wait_ge(t_ready, 4 + A0 + u + 1 + 8 * i)
                        act.wait_ge(pv_done, A0 + u + 1 + 8 * i)
                        nc.scalar.activation(pT[:, u % 2, 0:keys], B[(3, 0)[u % 2]][:, 0:keys], ACT.Copy)\
                            .then_inc(pt_ready, 1)
                        if u + 2 < 8:
                            exps(u + 2, i)
                        if u == 5:
                            out_hi(0, i)
                    out_hi(1, i)

            def pleproj(st):
                act.wait_ge(p_landed, 16 * (st.layer + 1))
                nc.scalar.activation(phi[:, :, :], pT_raw[:, :, :], ACT.Copy).then_inc(p_hi, 1)
                for c in range(4):
                    m = st.m0 + c
                    done, count = ((ple_pe, 2 * st.layer + 1), (half_used, st.n0 + 1),
                                   (ple_pe, 2 * st.layer + 2), (slab_used, st.n0 + 1))[c]
                    act.wait_ge(done, count)
                    nc.scalar.activation(pp[:, 2 * c:2 * c + 2, :], acc[:, m % 2, :, 0:S], ACT.Copy)\
                        .then_inc(acc_free[m % 2], 1)
                hi(st.n0 + 2)

            def plegate(st):
                for c in range(4):
                    n, m = st.n0 + c, st.m0 + c
                    act.wait_ge(slab_used, n + 1)
                    if c >= 2:
                        act.wait_ge(acc_free[m % 2], freed(m - 2))
                    nc.scalar.activation(gate_sb[:, :, (c % 2) * S:(c % 2 + 1) * S], acc[:, m % 2, :, 0:S],
                                         ACT.Sigmoid).then_inc(ple_gate, 1)
                    hi(n + 2)

            run = dict(start=start, ada=ada, up=up, down=residual, pw2=residual, wo=residual, norm=norm, pw1=pw1,
                       conv=conv, qkv=qkv, qknorm=qknorm, vab=vab, nsakv=nsakv, cmp=cmp_, att=att,
                       pleproj=pleproj, plegate=plegate)
            for st in plan:
                if st.kind in run:
                    run[st.kind](st)

        @block.vector
        def _(dve):
            step = Steps(dve, dve_step)

            def lo(n, i=0, per=0):
                if n >= NS:
                    return
                for cols, ready, low in ((FIRST, hi_half, lo_half), (SECOND, hi_ready, lo_ready)):
                    dve.wait_ge(ready, n + 1 + i * per)
                    nc.vector.tensor_tensor(wlo[:, n % 2, cols], raw[:, n % 2, cols],
                                            whi[:, n % 2, cols].bitcast(F32), ALU.subtract).then_inc(low, 1)

            def let_pool_load():
                nc.vector.memset(junk[:, :], 0.0).then_inc(pool_go, 1)

            def start(st):
                dve.wait_ge(const_landed, 64)
                for col in (VCOL["qk_gain_ab"], VCOL["qk_gain_nsa"]):
                    nc.vector.tensor_scalar(vec[:, col:col + 4], vec[:, col:col + 4], HD ** -0.5, None, ALU.mult)
                dve.wait_ge(c_ready, 1)
                nc.vector.tensor_tensor(c4[:, :, 2:4], cs[:, :, :], c4[:, :, 0:2].bitcast(F32), ALU.subtract)\
                    .then_inc(c_ready, 1)
                for j in range(2):
                    dve.wait_ge(line_pe, j + 1)
                    nc.vector.tensor_copy(lines[:, 384 * j:384 * j + 384], B[1 + j][0:NH, 0:384])\
                        .then_inc(lines_ready, 1)
                lo(0)
                lo(1)

            def ada(st):
                with dve.Fori(0, st.slabs // 2) as i:
                    lo(st.n0 + 2, i, 2)
                    lo(st.n0 + 3, i, 2)

            def mods(st):
                dve.wait_ge(row_turned, st.q0)
                gate = st.gate
                first = 24 * st.mod

                def sums_of(dst, tile):
                    M = Mod[:, 144 * st.layer + 2 * tile:144 * st.layer + 2 * tile + 2 * DT]
                    b = VCOL["ada_b"] + 72 * st.layer + tile
                    step.done(nc.vector.tensor_tensor(dst, M.rearrange("p (a b) -> p a b", b=2),
                                                      across(vec[:, b:b + DT], 2, 2), ALU.add))

                if gate is not True:
                    g = VCOL["norm_g"] + DT * (3 * st.layer + st.mod)
                    sums_of(mB[:, st.mod], first)
                    sums_of(mA[:, st.mod], first + DT)
                    step.done(nc.vector.scalar_tensor_tensor(mA[:, st.mod], mA[:, st.mod], 1.0,
                                                             across(vec[:, g:g + DT], 2, 2), ALU.add, ALU.mult))
                if gate is not False:
                    sums_of(mG[:, st.mod], first + 2 * DT)
                    if st.mod != 1:
                        step.done(nc.vector.tensor_scalar(mG[:, st.mod], mG[:, st.mod], 0.5, None, ALU.mult))

            def norm(st):
                x_final(dve, st)
                T = st.T
                dve.wait_ge(std_ready, st.std0 + 1)
                step.done(nc.vector.reciprocal(rs[:, 0:T], rs[:, 0:T]))

                def place(k):
                    return (k // 2, k % 2) if st.items == 2 * DT else (k, 0)

                def scaled(k):
                    c, s = place(k)
                    cols = slice(S * s, S * s + S)
                    if st.how == "mod":
                        g = mA[:, st.mod, c, s:s + 1]
                    elif st.how == "gain":
                        g = vec[:, st.gain + c:st.gain + c + 1]
                    else:
                        g = vec[:, VCOL["final_g"] + c:VCOL["final_g"] + c + 1]
                    dst = x[:, c, cols] if st.how == "final" else ub[:, k % 4, :]
                    nc.vector.scalar_tensor_tensor(dst, x[:, c, cols], g, rs[:, cols], ALU.mult, ALU.mult)\
                        .then_inc(u_ready, 1)

                def low(k):
                    c, s = place(k)
                    cols = slice(S * s, S * s + S)
                    dve.wait_ge(h_hi, st.h0 + k + 1)
                    if st.how == "mod":
                        ins = nc.vector.scalar_tensor_tensor(hlo[:, c, cols], ub[:, k % 4, :],
                                                             mB[:, st.mod, c, s:s + 1],
                                                             hhi[:, c, cols].bitcast(F32), ALU.add, ALU.subtract)
                    else:
                        ins = nc.vector.tensor_tensor(hlo[:, c, cols], ub[:, k % 4, :],
                                                      hhi[:, c, cols].bitcast(F32), ALU.subtract)
                    ins.then_inc(h_ready, 1)

                if st.how == "final":
                    for k in range(st.items):
                        scaled(k)
                    return
                scaled(0)
                scaled(1)
                for k in range(st.items):
                    low(k)
                    if k + 2 < st.items:
                        scaled(k + 2)

            def up(st):
                both = st.ada // 2
                for first, count, per in ((0, both, 4), (both, 11 - both, 2)):
                    if not count:
                        continue
                    n = st.n0 + 4 * first
                    m = st.m0 + 2 * first
                    T = st.T
                    with dve.Fori(0, count) as i:
                        for c in range(2, per + 1):
                            lo(n + c, i, per)
                        dve.wait_ge(acc_free[m % 2], freed(m) + i)
                        dve.wait_ge(slab_used, n + per + i * per)
                        dve.wait_ge(g_lo, st.g0 + first + 1 + i)
                        nc.vector.tensor_tensor(prod[:, :, 0:T], gate_sb[:, :, 0:T], acc[:, (m + 1) % 2, :, 0:T],
                                                ALU.mult).then_inc(acc_free[(m + 1) % 2], 1)
                        lo(n + per + 1, i, per)
                        dve.wait_ge(g_hi, st.g0 + first + 1 + i)
                        tiles = bass.ds(2 * first + 2 * i, 2)
                        nc.vector.tensor_tensor(glo[:, tiles, 0:T], prod[:, :, 0:T],
                                                ghi[:, tiles, 0:T].bitcast(F32), ALU.subtract).then_inc(g_lo, 1)

            def residual(st):
                ks = st.slabs // 4
                xf = x[:, :, :].rearrange("p a b -> p (a b)")
                mGf = mG[:, :, :, :].rearrange("p a b c -> p (a b c)")
                if st.kind == "pw2":
                    b2 = VCOL["pw2_b"]
                    step.done(nc.vector.tensor_tensor(gb[:, :, :], mG[:, 1], across(vec[:, b2:b2 + DT], 2, 2), ALU.mult))
                    for c in range(DT):
                        for s in range(2):
                            ins = nc.vector.tensor_scalar(x[:, c, S * s:S * s + S], x[:, c, S * s:S * s + S],
                                                          gb[:, c, s:s + 1], None, ALU.add)
                    step.done(ins)
                with dve.Fori(0, 2) as i:
                    for c in range(2):
                        m = st.m0 + c
                        for kk in range(ks):
                            n = st.n0 + ks * c + kk
                            if kk == ks - 1:
                                dve.wait_ge(slab_used, n + 1 + i * (2 * ks))
                                if st.mod is None:
                                    tiles = bass.ds(2 * c + 4 * i, 2)
                                    ins = nc.vector.tensor_tensor(x[:, tiles, 0:S], x[:, tiles, 0:S],
                                                                  acc[:, m % 2, :, 0:S], ALU.add)
                                else:
                                    for t in range(2):
                                        for s in range(st.T // S):
                                            at = bass.ds((2 * c + t) * 2 * S + S * s + i * (8 * S), S)
                                            g = bass.ds(16 * st.mod + 2 * (2 * c + t) + s + 8 * i, 1)
                                            ins = nc.vector.scalar_tensor_tensor(
                                                xf[:, at], acc[:, m % 2, t, S * s:S * s + S], mGf[:, g],
                                                xf[:, at], ALU.mult, ALU.add)
                                ins.then_inc(acc_free[m % 2], 1)
                            lo(n + 2, i, 2 * ks)

            ub2 = ubuf[:, :, :, :].rearrange("p a s t -> p (a s) t")

            def pw1(st):
                nc.vector.memset(ub2[:, :, 0:PAD], 0.0)
                step.done(nc.vector.memset(ub2[:, :, PAD + S:SP_], 0.0))
                a, b = st.m0 % 2, (st.m0 + 1) % 2
                with dve.Fori(0, 4) as i:
                    lo(st.n0 + 2, i, 2)
                    dve.wait_ge(acc_free[a], freed(st.m0) + i)
                    dve.wait_ge(slab_used, st.n0 + 2 + 2 * i)
                    for t in range(2):
                        ins = nc.vector.scalar_tensor_tensor(
                            ub2[:, bass.ds(2 * t + 4 * i, 2), PAD:PAD + S],
                            acc[:, b, t, :].rearrange("p (s t) -> p s t", s=2),
                            vec[:, bass.ds(VCOL["pw1_b"] + t + 2 * i, 1)],
                            gate_sb[:, t, :].rearrange("p (s t) -> p s t", s=2), ALU.add, ALU.mult)
                    ins.then_inc(acc_free[b], 1)
                    lo(st.n0 + 3, i, 2)

            def conv(st):
                def tile(j):
                    return v[:, j, :].rearrange("p (s t) -> p s t", s=2)

                x_final(dve, st)
                for j in range(4, 8):
                    w, b = VCOL["dw_w"] + CONV_W * j, VCOL["dw_b"] + j
                    nc.vector.tensor_scalar(tile(j), ub2[:, 2 * j:2 * j + 2, 0:S], vec[:, w:w + 1], vec[:, b:b + 1],
                                            ALU.mult, ALU.add).then_inc(conv_dve, 1)
                with dve.Fori(0, CONV_W - 1) as i:
                    for j in range(4, 8):
                        dve.wait_ge(conv_dve, 4 * i + (j - 3))
                        nc.vector.scalar_tensor_tensor(
                            tile(j), ub2[:, 2 * j:2 * j + 2, bass.ds(i + 1, S)],
                            vec[:, bass.ds(VCOL["dw_w"] + CONV_W * j + 1 + i, 1)], tile(j), ALU.mult, ALU.add)\
                            .then_inc(conv_dve, 1)
                dve.wait_ge(mean_done, 1)
                step.done(nc.vector.tensor_scalar(rs[:, :], B[2][:, :], 1.0 / D, None, ALU.mult))
                for c in range(DT):
                    nc.vector.tensor_tensor(v[:, c, :], v[:, c, :], rs[:, :], ALU.subtract).then_inc(d_ready, 1)
                dve.wait_ge(std_ready, st.std0 + 1)
                step.done(nc.vector.reciprocal(rs[:, :], rs[:, :]))

                def scaled(c):
                    g = VCOL["ln_g"] + c
                    nc.vector.scalar_tensor_tensor(v[:, c, :], v[:, c, :], vec[:, g:g + 1], rs[:, :],
                                                   ALU.mult, ALU.mult).then_inc(u_ready, 1)

                scaled(0)
                scaled(1)
                for c in range(DT):
                    dve.wait_ge(h_hi, st.h0 + c + 1)
                    nc.vector.tensor_tensor(hlo[:, c, :], sq[:, c % 2, :], hhi[:, c, :].bitcast(F32), ALU.subtract)\
                        .then_inc(h_ready, 1)
                    if c + 2 < DT:
                        scaled(c + 2)

            def qkv(st):
                let_pool_load()
                for c in range(6):
                    lo(st.n0 + c + 2)
                dve.wait_ge(rope_landed, 32)
                for j in range(5):
                    t = QK[:, 2 * j:2 * j + 2, :] if j < 4 else kraw[:, :, 0:S]
                    cos, sin = rope[:, 2 * (j // 4), :], rope[:, 2 * (j // 4) + 1, :]
                    tmp = prod[:, 0, :].rearrange("p (a b) -> p a b", a=2)
                    dve.wait_ge(rot_done, j + 1)
                    nc.vector.tensor_tensor(tmp, B[1 + j % 2][:, :].rearrange("p (a b) -> p a b", a=2),
                                            across(sin, 2), ALU.mult).then_inc(rope_done, 1)
                    step.done(nc.vector.tensor_tensor(t, t, across(cos, 2), ALU.mult))
                    dve.wait_ge(rope_done, j + 1)
                    step.done(nc.vector.tensor_tensor(t, t, tmp, ALU.add))

            def qknorm(st):
                let_pool_load()
                n = st.n0
                with dve.Fori(0, st.slabs // 2) as i:
                    step.loop(i, 2)
                    lo(n + 2, i, 2)
                    lo(n + 3, i, 2)
                    for c in range(2):
                        dve.wait_ge(std_ready, st.std0 + c + 1 + 2 * i)
                        step.done(nc.vector.reciprocal(prod[:, c, :], prod[:, c, :]))
                        tiles = QK[:, bass.ds(2 * c + 4 * i, 2), :]
                        nc.vector.scalar_tensor_tensor(
                            tiles, tiles, vec[:, bass.ds(st.gain + c + 2 * i, 1)],
                            prod[:, c, :].rearrange("p (a b) -> p a b", a=2), ALU.mult, ALU.mult)\
                            .then_inc(qk_done, 1)
                step.end(2, st.slabs // 2)

            def vab(st):
                with dve.Fori(0, 2) as i:
                    lo(st.n0 + 2, i, 2)
                    lo(st.n0 + 3, i, 2)

            def nsakv(st):
                for c in range(5):
                    lo(st.n0 + c + 2)

            def cmp_(st):
                dve.wait_ge(acc_free[st.m0 % 2], room(st.m0))
                dve.wait_ge(acc_free[(st.m0 + 1) % 2], room(st.m0 + 1))
                step.done(nc.vector.memset(sc[:, :, :], 0.0))
                for kv in range(2):
                    r = craw[:, kv, 0, 0:1]
                    base = [list(r.ap[0])]
                    src = bass.AP(r.tensor, r.offset, base + [[1, 16], [S, NKV], [16, NCMP]])
                    pos = vec[:, VCOL["cmp_pos"] + 16 * kv:VCOL["cmp_pos"] + 16 * kv + 16]
                    pos = bass.AP(pos.tensor, pos.offset, [list(pos.ap[0]), [1, 16], [0, NKV], [0, NCMP]])
                    dst = blk[:, kv].rearrange("p l (t c) -> p l t c", t=NKV)[:, :, :, 0:NCMP]
                    nc.vector.tensor_tensor(dst, src, pos, ALU.add).then_inc(cmp_dve, 1)
                dve.wait_ge(cmp_act, 1)
                nc.vector.tensor_tensor(blo[:, :, :, :], blk, bhi[:, :, :, :].bitcast(F32), ALU.subtract)\
                    .then_inc(cmp_dve, 1)
                for c in range(2):
                    lo(st.n0 + c + 2)
                dve.wait_ge(cmp_act, 3)
                step.done(nc.vector.reciprocal(kcr[:, :], kcr[:, :]))
                kf = kcmp[:, :, :].rearrange("p a b -> p (a b)")
                nc.vector.scalar_tensor_tensor(kf, kf, vec[:, VCOL["kn_cmp"]:VCOL["kn_cmp"] + 1], kcr[:, :],
                                               ALU.mult, ALU.mult).then_inc(cmp_dve, 1)
                dve.wait_ge(cmp_pe, 2)
                nc.vector.tensor_tensor(vcmp[:, :, :], B[3][0:16, 0:256].rearrange("p (a b) -> p a b", a=4),
                                        across(w2[0:16, 192:256], 4), ALU.add).then_inc(cmp_dve, 1)
                dve.wait_ge(bias_landed, 64)
                dve.wait_ge(vm_zero, 2)
                for q, ncol, at in ((0, 7, P + 31), (1, NCMP, 31)):
                    pc = Pc[:, q, :, 0:ncol]
                    for par in range(2):
                        dve.wait_ge(cmp_pe, 4 + 2 * q + par)
                        bank = B[(1, 2, 3, 0)[2 * q + par]]
                        step.done(nc.vector.tensor_tensor(
                            Pc[:, q, par:NH:2, 0:ncol], bank[:, 0:P].rearrange("p (a b) -> p a b", a=8)[:, :, 0:ncol],
                            bt[:, par:NH:2, at:S:16], ALU.add))
                    step.done(nc.vector.tensor_reduce(cst[:, 0, :], pc, AX.X, ALU.max))
                    nc.vector.tensor_tensor(pc, pc, across(cst[:, 0, :], ncol, 2), ALU.subtract).then_inc(cmp_dve, 1)
                for q, ncol in ((0, 7), (1, NCMP)):
                    pc = Pc[:, q, :, 0:ncol]
                    dve.wait_ge(cmp_act, 4 + q)
                    step.done(nc.vector.tensor_tensor(pc, pc, across(valid[:, q, 0:ncol], NH), ALU.mult))
                    step.done(nc.vector.tensor_reduce(cst[:, 1, :], pc, AX.X, ALU.add))
                    step.done(nc.vector.tensor_scalar(cst[:, 1, :], cst[:, 1, :], 1.0, None, ALU.max))
                    step.done(nc.vector.reciprocal(cst[:, 2, :], cst[:, 1, :]))
                    step.done(nc.vector.tensor_tensor(cst[:, 2, :], cst[:, 2, :], gates[:, q, 0:48:3], ALU.mult))
                    nc.vector.tensor_tensor(pc, pc, across(cst[:, 2, :], ncol, 2), ALU.mult).then_inc(cmp_dve, 1)

            def att(st):
                A0 = 32 * st.att0
                win, nsa = st.what == "window", st.what == "nsa"
                btf = bt[:, :, :].rearrange("p a b -> p (a b)")
                nc.vector.memset(junk[:, :], 0.0).then_inc(att_ready, 1)
                if not win:
                    dve.wait_ge(bias_landed, 64 if nsa else 32)
                if win:
                    for g in range(NKV):
                        ins = nc.vector.tensor_copy(
                            kd[64:P, 2 * g:2 * g + 2, :],
                            kraw[64 * (g % 2):64 * (g % 2) + 64, g // 2, :].rearrange("p (a b) -> p a b", a=2))
                    ins.then_inc(kd_dve, 1)
                if nsa:
                    for j in range(8):
                        g = j % 4
                        ins = nc.vector.tensor_copy(kd[64:P, j, :],
                                                    QK[64 * (g % 2):64 * (g % 2) + 64, 8 + 2 * (j // 4) + g // 2, :])
                    ins.then_inc(kd_dve, 1)

                def biased(u, i):
                    q, b = u % 2, u % 4
                    sp = stt4[:, b]
                    keys = 512 if win else P * (q + 1)
                    dve.wait_ge(s_ready, A0 + u + 1 + 8 * i)
                    dve.wait_ge(t_ready, A0 + u + 1 + 8 * i)
                    bias = mask[:, q, :] if win else btf[:, bass.ds(S * (u // 2) + P * (1 - q) + 4 * S * i, keys)]
                    for s in range(2 if nsa else 1):
                        ins = nc.vector.tensor_tensor_reduce(sc[:, b, keys * s:keys * s + keys],
                                                             B[1 + q][:, keys * s:keys * s + keys], bias,
                                                             1.0, LOWEST, ALU.add, ALU.max, sp[:, s:s + 1])
                    ins.then_inc(s_free, 1)
                    dve.wait_ge(s_free, 2 + A0 + u + 1 + 8 * i)
                    if win:
                        ins = nc.vector.tensor_scalar(sp[:, 2:3], sp[:, 0:1],
                                                      vec[:, bass.ds(VCOL["sink"] + u // 2 + 4 * i, 1)], -1.0,
                                                      ALU.max, ALU.mult)
                    else:
                        w = 2 if nsa else 1
                        ins = nc.vector.tensor_scalar(sp[:, 2:2 + w], sp[:, 0:w], -1.0, None, ALU.mult)
                    ins.then_inc(m_ready, 1)

                def normalised(u, i):
                    q, b = u % 2, u % 4
                    sp = stt4[:, b]
                    dve.wait_ge(e_ready, A0 + u + 1 + 8 * i)
                    if win:
                        step.done(nc.vector.tensor_tensor(sp[:, 4:5], sp[:, 4:5], sp[:, 6:7], ALU.add))
                    w = 2 if nsa else 1
                    step.done(nc.vector.reciprocal(sp[:, 7:7 + w], sp[:, 4:4 + w]))
                    if nsa:
                        step.done(nc.vector.tensor_tensor(
                            sp[:, 7:9], sp[:, 7:9],
                            gates[:, q, :][:, bass.ds(3 * (u // 2) + 1 + 12 * i, 2)], ALU.mult))
                    keys = 512 if win else P * (q + 1)
                    for s in range(w):
                        p = sc[:, b, keys * s:keys * s + keys]
                        ins = nc.vector.tensor_scalar(p, p, sp[:, 7 + s:8 + s], None, ALU.mult)
                    ins.then_inc(p_ready, 1)

                def out_lo(pair, i):
                    dve.wait_ge(o_hi, A0 // 4 + pair + 1 + 2 * i)
                    t = bass.ds(S * pair + 2 * S * i, S)
                    nc.vector.tensor_tensor(olo[:, :, :].rearrange("p a b -> p (a b)")[:, t], acc[:, pair, 0, 0:S],
                                            ohi[:, :, :].rearrange("p a b -> p (a b)")[:, t].bitcast(F32),
                                            ALU.subtract).then_inc(o_lo, 1)

                for i in range(NKV):
                    biased(0, i)
                    biased(1, i)
                    for u in range(8):
                        normalised(u, i)
                        if u + 2 < 8:
                            biased(u + 2, i)
                        if u == 5:
                            out_lo(0, i)
                    out_lo(1, i)

            def pleproj(st):
                let_pool_load()
                dve.wait_ge(p_hi, 2 * st.layer + 1)
                nc.vector.tensor_tensor(plo[:, :, :], pT_raw[:, :, :], phi[:, :, :].bitcast(F32), ALU.subtract)\
                    .then_inc(p_hi, 1)
                lo(st.n0 + 2)

            def plegate(st):
                for c in range(4):
                    m = st.m0 + c
                    dve.wait_ge(ple_gate, 4 * st.layer + c + 1)
                    t = ub[:, 2 * (c % 2):2 * (c % 2) + 2, :]
                    step.done(nc.vector.tensor_tensor(t, gate_sb[:, :, (c % 2) * S:(c % 2 + 1) * S],
                                                      pp[:, 2 * c:2 * c + 2, :], ALU.mult))
                    xx = x[:, 2 * c:2 * c + 2, 0:S]
                    nc.vector.tensor_tensor(xx, xx, t, ALU.add).then_inc(acc_free[m % 2], 1)
                    lo(st.n0 + c + 2)

            run = dict(start=start, ada=ada, mods=mods, up=up, down=residual, pw2=residual, wo=residual, norm=norm,
                       pw1=pw1, conv=conv, qkv=qkv, qknorm=qknorm, vab=vab, nsakv=nsakv, cmp=cmp_, att=att,
                       pleproj=pleproj, plegate=plegate)
            for st in plan:
                if st.kind in run:
                    run[st.kind](st)

        @block.tensor
        def _(pe):
            def split_mm(out, w, xx, first, last):
                nc.tensor.matmul(out, w[0], xx[0], start=first, stop=False)
                nc.tensor.matmul(out, w[0], xx[1], start=False, stop=False)
                return nc.tensor.matmul(out, w[1], xx[0], start=False, stop=last)

            def w_at(n, a, b):
                return whi[:, n % 2, a:b], wlo[:, n % 2, a:b]

            def slab_there(n, i=0, per=0):
                pe.wait_ge(lo_half, n + 1 + i * per)

            def second_half(n, i=0, per=0):
                pe.wait_ge(lo_ready, n + 1 + i * per)

            def set_free(m, i=0, per=0):
                pe.wait_ge(acc_free[m % 2], room(m) + i * (per // 2))

            def tiles_of(n, m, op, T, i=0, per=0, k0=0, nk=SLAB_K, first=True, last=True, paced=None):
                for k in range(nk):
                    if k == SLAB_K // 2:
                        ins.then_inc(half_used, 1)
                        second_half(n, i, per)
                    if paced:
                        pe.wait_ge(h_ready, paced.h0 - paced.made + paced.made * (k + 1) // DT)
                    for t in range(2):
                        a = k * SLAB_N + t * P
                        ins = split_mm(acc[:, m % 2, t, 0:T], w_at(n, a, a + P),
                                       (op[0][:, k0 + k, 0:T], op[1][:, k0 + k, 0:T]),
                                       first and k == 0, last and k == nk - 1)
                return ins

            def tokens_of(n, m, count, cols=SLAB_N, i=0, per=0):
                for tt in range(count):
                    o = acc[:, m % 2, tt, 0:cols] if count == 2 else \
                        acc[:, m % 2, tt // 2, SLAB_N * (tt % 2):SLAB_N * (tt % 2) + SLAB_N]
                    for k in range(SLAB_K):
                        ks = slice(P * tt, P * tt + P)
                        a = k * SLAB_N
                        if k == SLAB_K // 2:
                            if tt == 0:
                                second_half(n, i, per)
                            if tt == count - 1:
                                ins.then_inc(half_used, 1)
                        nc.tensor.matmul(o, hhi[:, k, ks], whi[:, n % 2, a:a + cols], start=(k == 0), stop=False)
                        nc.tensor.matmul(o, hlo[:, k, ks], whi[:, n % 2, a:a + cols], start=False, stop=False)
                        ins = nc.tensor.matmul(o, hhi[:, k, ks], wlo[:, n % 2, a:a + cols], start=False,
                                               stop=(k == SLAB_K - 1))
                return ins

            def start(st):
                pe.wait_ge(loaded, 32)
                for j in range(2):
                    nc.tensor.matmul(B[1 + j][0:NH, 0:384], tab[:, :], hot[:, 384 * j:384 * j + 384],
                                     start=True, stop=True).then_inc(line_pe, 1)
                pe.wait_ge(c_ready, 2)

            def ada_slab(n, q, i, per):
                slab_there(n, i, per)
                for k in range(SLAB_K):
                    if k == SLAB_K // 2:
                        ins.then_inc(half_used, 1)
                        second_half(n, i, per)
                    cols = slice(k * SLAB_N, (k + 1) * SLAB_N)
                    for half, w in enumerate((whi, wlo)):
                        ins = nc.tensor.matmul(B[2 + q % 2][0:4, 0:SLAB_N], c4[:, k, :], w[:, n % 2, cols],
                                               start=(k + half == 0), stop=(k + half == SLAB_K))
                ins.then_inc(slab_used, 1)

            def ada_turn(q, i):
                pe.wait_ge(row_ready, q + 1 + 2 * i)
                for t in range(2):
                    ins = nc.tensor.matmul(Mod[:, bass.ds(4 * q + 2 * t + 8 * i, 2)], arow[:, q % 2, P * t:P * t + P],
                                           pick, start=True, stop=True)
                ins.then_inc(row_turned, 1)

            def ada(st):
                with pe.Fori(0, st.slabs // 2) as i:
                    for c in range(2):
                        ada_slab(st.n0 + c, st.q0 + c, i, 2)
                    for c in range(2):
                        ada_turn(st.q0 + c, i)

            def norm(st):
                T = st.T
                for c in range(DT):
                    pe.wait_ge(sq_ready, st.sq0 + c + 1)
                    nc.tensor.matmul(sums[:, 0:T], ones, sq[:, c % 2, 0:T], start=(c == 0), stop=(c == DT - 1))\
                        .then_inc(sum_done, 1)

            def half_pair(st, c, n, m, i, per):
                slab_there(n, i, per)
                set_free(m, i, 2)
                tiles_of(n, m, (hhi, hlo), st.T, i, per, paced=st if c == 0 else None).then_inc(slab_used, 1)

            def up(st):
                both = st.ada // 2
                for first, count, per in ((0, both, 4), (both, 11 - both, 2)):
                    if not count:
                        continue
                    n, m = st.n0 + 4 * first, st.m0 + 2 * first
                    with pe.Fori(0, count) as i:
                        half_pair(st, 0, n, m, i, per)
                        if per == 4:
                            ada_slab(n + 1, st.q0, i, 4)
                            ada_slab(n + 2, st.q0 + 1, i, 4)
                        half_pair(st, 1, n + per - 1, m + 1, i, per)
                        if per == 4:
                            ada_turn(st.q0, i)
                            ada_turn(st.q0 + 1, i)

            def pw1(st):
                with pe.Fori(0, 4) as i:
                    for c in range(2):
                        half_pair(st, c, st.n0 + c, st.m0 + c, i, 2)

            def residual(st):
                ks = st.slabs // 4
                if st.kind == "down":
                    pe.wait_ge(g_lo, st.g0 + 1)
                    op = (ghi, glo)
                elif st.kind == "wo":
                    pe.wait_ge(o_lo, 2 + 8 * st.att0)
                    op = (ohi, olo)
                else:
                    op = (hhi, hlo)
                with pe.Fori(0, 2) as i:
                    for c in range(2):
                        m = st.m0 + c
                        set_free(m, i, 2)
                        for kk in range(ks):
                            n = st.n0 + ks * c + kk
                            slab_there(n, i, 2 * ks)
                            nk = min(SLAB_K, HT - SLAB_K * kk) if ks == 3 else SLAB_K
                            tiles_of(n, m, op, st.T, i, 2 * ks, SLAB_K * kk, nk, kk == 0, kk == ks - 1,
                                     paced=st if st.kind == "pw2" and c == 0 else None).then_inc(slab_used, 1)

            def conv(st):
                x_final(pe, st)
                ub2 = ubuf[:, :, :, :].rearrange("p a s t -> p (a s) t")

                def tap(t, par, wait, first=False, last=False):
                    pe.wait_ge(diag_ready, wait)
                    for j in range(4):
                        ins = nc.tensor.matmul(acc[:, j // 2, j % 2, :], diag[:, par, j, :],
                                               ub2[:, 2 * j:2 * j + 2, bass.ds(t, S)], start=first, stop=last)
                    ins.then_inc(taps_used, 1)

                tap(0, 0, 1, first=True)
                tap(1, 1, 2)
                with pe.Fori(0, 14) as i:
                    tap(2 * i + 2, 0, 2 * i + 3)
                    tap(2 * i + 3, 1, 2 * i + 4)
                tap(30, 0, 31, last=True)
                m = st.m0 + 2
                pe.wait_ge(acc_free[0], 1 + (m + 1) // 2)
                pe.wait_ge(acc_free[1], 1 + m // 2)
                pe.wait_ge(conv_dve, 4 * CONV_W)
                for c in range(DT):
                    ins = nc.tensor.matmul(B[2][:, :], ones, v[:, c, :], start=(c == 0), stop=(c == DT - 1))
                ins.then_inc(mean_done, 1)
                for c in range(DT):
                    pe.wait_ge(sq_ready, st.sq0 + c + 1)
                    nc.tensor.matmul(sums[:, :], ones, sq[:, c % 2, :], start=(c == 0), stop=(c == DT - 1))\
                        .then_inc(sum_done, 1)

            def qkv(st):
                for c in range(6):
                    n, m = st.n0 + c, st.m0 + c
                    slab_there(n)
                    set_free(m)
                    if c < 5:
                        ins = tiles_of(n, m, (hhi, hlo), S if c < 4 else 2 * S, paced=st if c == 0 else None)
                    else:
                        ins = tokens_of(n, m, 4)
                    ins.then_inc(slab_used, 1)
                for j in range(5):
                    t = QK[:, 2 * j:2 * j + 2, :] if j < 4 else kraw[:, :, 0:S]
                    pe.wait_ge(acc_free[(st.m0 + j) % 2], freed(st.m0 + j))
                    if j >= 2:
                        pe.wait_ge(rope_done, j - 1)
                    nc.tensor.matmul(B[1 + j % 2][:, :], rot, t, start=True, stop=True).then_inc(rot_done, 1)

            def qknorm(st):
                n, m = st.n0, st.m0
                with pe.Fori(0, st.slabs // 2) as i:
                    for c in range(2):
                        slab_there(n + c, i, 2)
                        set_free(m + c, i, 2)
                        tiles_of(n + c, m + c, (hhi, hlo), S, i, 2, paced=None if c else st).then_inc(slab_used, 1)
                    for c in range(2):
                        pe.wait_ge(acc_free[(m + c) % 2], freed(m + c) + i)
                        nc.tensor.matmul(B[1 + c][:, :], headones, sq[:, c, :], start=True, stop=True)\
                            .then_inc(sum_done, 1)

            def vab(st):
                with pe.Fori(0, 2) as i:
                    for c in range(2):
                        slab_there(st.n0 + c, i, 2)
                        set_free(st.m0 + c, i, 2)
                        tokens_of(st.n0 + c, st.m0 + c, 2, SLAB_N, i, 2).then_inc(slab_used, 1)

            def nsakv(st):
                for c in range(5):
                    n, m = st.n0 + c, st.m0 + c
                    slab_there(n)
                    set_free(m)
                    ins = tiles_of(n, m, (hhi, hlo), S) if c < 2 else tokens_of(n, m, 2, SLAB_N if c < 4 else 48)
                    ins.then_inc(slab_used, 1)

            def cmp_(st):
                pe.wait_ge(cmp_dve, 3)
                for kv in range(2):
                    m = st.m0 + kv
                    set_free(m)
                    n = st.n0 + kv
                    slab_there(n)
                    for k in range(16):
                        if k == 8:
                            ins.then_inc(half_used, 1)
                            second_half(n)
                        ins = split_mm(acc[:, m % 2, 0, 0:64], w_at(n, P * k, P * k + P),
                                       (bhi[:, kv, k, :], blo[:, kv, k, :]), k == 0, k == 15)
                    ins.then_inc(slab_used, 1)
                pe.wait_ge(acc_free[st.m0 % 2], freed(st.m0))
                nc.tensor.matmul(B[1][:, 0:64], w2[:, 0:P], hid[:, 0, :, :].rearrange("p a b -> p (a b)"),
                                 start=True, stop=True).then_inc(cmp_pe, 1)
                pe.wait_ge(acc_free[(st.m0 + 1) % 2], freed(st.m0 + 1))
                for g in range(NKV):
                    ins = nc.tensor.matmul(B[3][0:16, HD * g:HD * g + HD], hid[:, 1, 2 * (g % 2) + g // 2, :],
                                           w2[:, P:P + HD], start=True, stop=True)
                ins.then_inc(cmp_pe, 1)
                pe.wait_ge(cmp_act, 2)
                nc.tensor.matmul(B[2][:, 0:64], headones, kcsq[:, :], start=True, stop=True).then_inc(cmp_pe, 1)
                pe.wait_ge(cmp_dve, 5)
                pe.wait_ge(qk_done, 2 + st.qk0)
                for q, ncol in ((0, 7), (1, NCMP)):
                    for par in range(2):
                        bank = B[(1, 2, 3, 0)[2 * q + par]]
                        rows = slice(64 * par, 64 * par + 64)
                        for hh in range(8):
                            g = (2 * hh + par) // 4
                            ins = nc.tensor.matmul(bank[:, 16 * hh:16 * hh + ncol], QK[rows, hh, P * q:P * q + P],
                                                   kcmp[rows, 2 * (g % 2) + g // 2, 0:ncol], start=True, stop=True)
                        ins.then_inc(cmp_pe, 1)
                pe.wait_ge(cmp_dve, 9)
                for g in range(NKV):
                    if g >= 2:
                        pe.wait_ge(cmp_act, 6 + g - 2)
                    for q in range(2):
                        ins = nc.tensor.transpose(B[1 + g % 2][:, P * q:P * q + P],
                                                  Pc[:, q, 4 * g:4 * g + 4, :].rearrange("p a b -> p (a b)"), ident)
                    ins.then_inc(cmp_pe, 1)

            def att(st):
                A0 = 32 * st.att0
                win, nsa = st.what == "window", st.what == "nsa"
                QKf = QK[:, :, :].rearrange("p a b -> p (a b)")
                kdf = kd[:, :, :].rearrange("p a b -> p (a b)")
                Vf = Vm[:, :, :].rearrange("p a b -> p (a b)")
                PcTf = PcT[:, :, :, :].rearrange("p a b c -> p (a b c)")
                x_final(pe, st)
                pe.wait_ge(att_ready, st.att0 + 1)
                if st.what != "ab":
                    pe.wait_ge(kd_dve, 2 if nsa else 1)
                    pe.wait_ge(kd_act, 2 if nsa else 1)
                if nsa:
                    pe.wait_ge(cmp_act, 9)
                    pe.wait_ge(vm_landed, 64)

                def scores(u, i):
                    q, rows = u % 2, slice(64 * ((u // 2) % 2), 64 * ((u // 2) % 2) + 64)
                    keys = 512 if win else P * (q + 1)
                    pe.wait_ge(s_free, A0 + u + 1 + 8 * i)
                    qq = QKf[rows, bass.ds(S * (u // 4) + P * q + 2 * S * i, P)]
                    for s in range(2 if nsa else 1):
                        if win:
                            kk = kdf[rows, bass.ds(512 * i, keys)]
                        elif nsa:
                            kk = kdf[rows, bass.ds(4 * S * s + S * i, keys)]
                        else:
                            kk = QKf[rows, bass.ds(8 * S + S * (u // 4) + 2 * S * i, keys)]
                        ins = nc.tensor.matmul(B[1 + q][:, keys * s:keys * s + keys], qq, kk, start=True, stop=True)
                    ins.then_inc(s_ready, 1)

                def turned(u, i):
                    q = u % 2
                    pe.wait_ge(p_ready, A0 + u + 1 + 8 * i)
                    pe.wait_ge(pt_ready, A0 + u + 1 + 8 * i)
                    nt = 4 if win else (q + 1) * (2 if nsa else 1)
                    for j in range(nt):
                        ins = nc.tensor.transpose(B[(3, 0)[q]][:, P * j:P * j + P], sc[:, u % 4, P * j:P * j + P], ident)
                    ins.then_inc(t_ready, 1)

                def values(u, i):
                    q, pair = u % 2, u // 4
                    rows = slice(64 * ((u // 2) % 2), 64 * ((u // 2) % 2) + 64)
                    o = acc[rows, pair, 0, P * q:P * q + P]
                    if u % 4 == 0:
                        pe.wait_ge(o_lo, A0 // 4 + pair + 1 + 2 * i)
                    pe.wait_ge(pt_ready, 2 + A0 + u + 1 + 8 * i)
                    first = True
                    if nsa:
                        nc.tensor.matmul(o, Vf[:, bass.ds(HD * (u // 2) + 4 * HD * i, HD)],
                                         PcTf[:, bass.ds(P * q + S * i, P)], start=True, stop=False)
                        first = False
                    nk = 4 if win else q + 1
                    ns = 2 if nsa else 1
                    for s in range(ns):
                        for k in range(nk):
                            if win:
                                at = bass.ds(S * k + HD * i, HD)
                            elif nsa:
                                at = bass.ds(512 * k + S * s + HD * i, HD)
                            else:
                                at = bass.ds(D * k + HD * (u // 2) + 4 * HD * i, HD)
                            j = s * nk + k
                            ins = nc.tensor.matmul(o, vt[:, at], pT[:, q, P * j:P * j + P], start=first,
                                                   stop=(j == ns * nk - 1))
                            first = False
                    ins.then_inc(pv_done, 1)

                for i in range(NKV):
                    scores(0, i)
                    scores(1, i)
                    for u in range(8):
                        turned(u, i)
                        if u + 2 < 8:
                            scores(u + 2, i)
                        values(u, i)

            def pleproj(st):
                pe.wait_ge(p_hi, 2 * st.layer + 2)
                slab_there(st.n0)
                for c in range(4):
                    m = st.m0 + c
                    set_free(m)
                    if c == 2:
                        second_half(st.n0)
                    for t in range(2):
                        for k in range(2):
                            a = (2 * c + k) * SLAB_N + t * P
                            ins = split_mm(acc[:, m % 2, t, 0:S], w_at(st.n0, a, a + P), (phi[:, k, :], plo[:, k, :]),
                                           k == 0, k == 1)
                    ins.then_inc((ple_pe, half_used, ple_pe, slab_used)[c], 1)

            def plegate(st):
                for c in range(4):
                    slab_there(st.n0 + c)
                    set_free(st.m0 + c)
                    tiles_of(st.n0 + c, st.m0 + c, (hhi, hlo), S, paced=None if c else st).then_inc(slab_used, 1)

            run = dict(start=start, ada=ada, norm=norm, up=up, pw1=pw1, down=residual, pw2=residual, wo=residual,
                       conv=conv, qkv=qkv, qknorm=qknorm, vab=vab, nsakv=nsakv, cmp=cmp_, att=att,
                       pleproj=pleproj, plegate=plegate)
            for st in plan:
                if st.kind in run:
                    run[st.kind](st)


def slabs_of(w):
    K, N = w.shape
    n = -(-N // SLAB_N)
    k = -(-K // (P * SLAB_K)) * SLAB_K
    full = np.zeros((k * P, n * SLAB_N), np.float32)
    full[:K, :N] = w
    a = full.reshape(k // SLAB_K, SLAB_K, P, n, SLAB_N)
    return list(a.transpose(3, 0, 2, 1, 4).reshape(n * (k // SLAB_K), P, SLAB))


def stream(z):
    out = []
    ada = slabs_of(np.asarray(z["ada_w"][0])) + slabs_of(np.asarray(z["ada_w"][1]))

    def pairs(a, b, extra=0):
        for j, (g, u) in enumerate(zip(slabs_of(a), slabs_of(b))):
            out.extend([g, ada.pop(0), ada.pop(0), u] if j < extra // 2 else [g, u])

    def ffn(wi, wo, extra=0):
        pairs(wi[:, :HID], wi[:, HID:], extra)
        out.extend(slabs_of(wo))

    for _ in range(12):
        out.append(ada.pop(0))
    for layer in range(2):
        ffn(z["ffn1_wi"][layer], z["ffn1_wo"][layer], 22 if layer == 0 else 16)
        if layer == 0:
            w = z["conv_pw1_w"][0]
            pairs(w[:, D:], w[:, :D])
            out.extend(slabs_of(z["conv_pw2_w"][0]))
            ffn(z["ffn2_wi"][0], z["ffn2_wo"][0], 22)
        else:
            out.extend(slabs_of(z["attn_w_qkv"][0]))
            out.extend(slabs_of(z["attn_w_o"][0]))
            ffn(z["ffn2_wi"][1], z["ffn2_wo"][1])
    for layer in range(2):
        if layer == 0:
            qa, ka, va, qb, kb, vb = np.split(z["w_in_ab_2"][0], 6, axis=1)
            out.extend(slabs_of(np.concatenate([qa, qb, ka, kb, va, vb], 1)))
            wo = z["w_out_ab_2"][0]
        else:
            q, kc, vc, ks, vs, kw, vw, g = np.split(z["w_in_nsa_2"][0], [D + 256 * j for j in range(7)], axis=1)
            out.extend(slabs_of(np.concatenate([q, ks, kw, kc, vc, vs, vw, g], 1)))
            for name in ("cmp_k_w1_2", "cmp_v_w1_2"):
                out.append(z[name][0].reshape(2, 16, HD, P).transpose(0, 2, 1, 3).reshape(P, SLAB))
            wo = z["w_out_nsa_2"][0]
        out.extend(slabs_of(wo))
        pairs(z["w_ffn_gate_2"][layer], z["w_ffn_up_2"][layer])
        out.extend(slabs_of(z["w_ffn_down_2"][layer]))
        w = z["w_ple_proj_2"][layer].reshape(2, P, 4, SLAB_N)
        out.append(w.transpose(1, 2, 0, 3).reshape(P, SLAB))
        out.extend(slabs_of(z["w_ple_gate_2"][layer]))
    return np.stack(out)


def columns(v):
    return np.asarray(v).reshape(-1, P).T


def both_halves(v):
    return np.concatenate([v, v]).reshape(P, 1)


def vectors(z):
    h = both_halves
    gains_ab = [z[n][0] for n in ("qn_moba_2", "qn_moba_2", "qn_dil_2", "qn_dil_2",
                                  "kn_moba_2", "kn_moba_2", "kn_dil_2", "kn_dil_2")]
    gains_nsa = [z[n][0] for n in ("qn_nsa_2",) * 4 + ("kn_slc_2", "kn_win_2")]
    pos = np.stack([z["cmp_k_pos_2"][0], z["cmp_v_pos_2"][0]]).reshape(2, 2, 16, HD)
    parts = dict(
        norm_g=columns(z["norm_g"]), ada_b=columns(z["ada_b"]), final_g=columns(z["final_g"]),
        pw1_b=columns(z["conv_pw1_b"]), dw_b=columns(z["conv_dw_b"]), ln_g=columns(z["conv_ln_g"]),
        ln_b=columns(z["conv_ln_b"]), pw2_b=columns(z["conv_pw2_b"]),
        dw_w=z["conv_dw_w"][0].reshape(CONV_W, DT, P).transpose(2, 1, 0).reshape(P, -1),
        c=columns(z["c"]), c_ctx=columns(z["c_ctx"]), norm_mix=columns(z["norm_mix_2"]),
        norm_ffn=columns(z["norm_ffn_2"]), norm_ple=columns(z["norm_ple_2"]),
        qk_gain_ab=np.concatenate([h(g) for g in gains_ab], 1),
        qk_gain_nsa=np.concatenate([h(g) for g in gains_nsa], 1),
        kn_cmp=h(z["kn_cmp_2"][0]), cmp_b1=np.stack([z["cmp_k_b1_2"][0], z["cmp_v_b1_2"][0]], 1),
        cmp_k_b2=h(z["cmp_k_b2_2"][0]), cmp_pos=pos.transpose(1, 3, 0, 2).reshape(P, 32),
        sink=np.broadcast_to(z["attn_sink"][0], (P, NH)))
    return np.concatenate([parts[n] for n, _ in VECTORS], 1)


def arrays_of(z):
    z = {k: np.asarray(v) for k, v in z.items()}
    tok = np.concatenate([z["x"][0], z["ctx"][0]], 0)
    w2 = np.concatenate([z["cmp_k_w2_2"][0], z["cmp_k_w2_2"][0], z["cmp_v_w2_2"][0],
                         np.broadcast_to(z["cmp_v_b2_2"][0], (P, HD))], 1)
    out = dict(
        slabs=stream(z), x_in=tok.reshape(2 * S, DT, P).transpose(2, 1, 0), vec=vectors(z),
        const=small_constants(), w2=w2, tab=z["rel_bias_2"], hot=line_tables(), rope=rope_tables(),
        mask=window_mask(), p=z["p_2"][:, 0].reshape(2, S, 2, P).transpose(0, 3, 2, 1))
    return {"in_" + k: np.ascontiguousarray(v, dtype=np.float32) for k, v in out.items()}


def kernel(**inputs):
    import concourse.bacc as _bacc
    from concourse.bass_utils import run_bass_kernel_spmd as _run

    arrays = arrays_of(inputs)
    nc = _bacc.Bacc("TRN2", target_bir_lowering=False, num_devices=1)
    args = [nc.dram_tensor(k, a.shape, F32, kind="ExternalInput").ap() for k, a in arrays.items()]
    args.append(nc.dram_tensor("out", (P, DT, S), F32, kind="ExternalOutput").ap())
    build(nc, *args)
    r = _run(nc, [arrays], core_ids=[0])
    return r.results[0]["out"].transpose(2, 1, 0).reshape(1, S, D)
```

```python
from contextlib import ExitStack

import numpy as np

import concourse.bass as bass
from concourse import mybir

F32 = mybir.dt.float32
F32R = mybir.dt.float32r
ALU = mybir.AluOpType
ACT = mybir.ActivationFunctionType
AX = mybir.AxisListType

P = 128
D = 1024
DT = D // P
S = 256
HID = 2816
HT = HID // P
NH, HD, NKV = 16, 64, 4
SLAB_K, SLAB_N = 8, 256
SLAB = SLAB_K * SLAB_N
FIRST, SECOND = slice(0, SLAB // 2), slice(SLAB // 2, SLAB)
CONV_W = 31
PAD = (CONV_W - 1) // 2
POOL_TILES, DVE_TILES, PE_TILES = (0,), (1, 2, 3, 4), (5, 6, 7)
SP_ = S + 2 * PAD
NCMP = (S - 32) // 16 + 1
EPS = 1e-6
MASKED = -1.0e30
UNITS = 2 * NH
LEAD = 3
LOWEST = -3.0e38


def rel_bucket(dist):
    n = np.maximum(dist, 0)
    nf = np.maximum(n, 1).astype(np.float32)
    large = 16 + (np.log(nf / np.float32(16)) / np.float32(np.log(2048 / 16)) * 16).astype(np.int32)
    return np.where(n < 16, n, np.minimum(large, 31))


def line_tables():
    m = np.arange(384)
    d = 255 - m
    hot = (rel_bucket(d)[None, :] == np.arange(32)[:, None]) & (d >= 0)[None, :]
    count = np.zeros(384)
    for window, dil in ((128, 1), (512, 4), (2048, 16)):
        count += (d >= 0) & (d % dil == 0) & (d // dil <= window // dil)
    causal = np.where(d >= 0, 0.0, MASKED)
    dilated = np.where(count > 0, np.log(np.maximum(count, 1)), MASKED)
    t = np.zeros((33, 2, 384), np.float32)
    t[:32] = hot[:, None, :]
    t[32, 0], t[32, 1] = causal, dilated
    return t.reshape(33, 768)


def rope_tables():
    p = np.arange(P) % HD
    inv = (np.float32(10000.0) ** (-np.arange(16, dtype=np.float32) / 16)).astype(np.float32)
    tok = np.arange(S)
    pos = np.stack([tok // 64, tok % 64]).astype(np.float32)
    ang = pos[p // 32] * inv[p % 16][:, None]
    c, s = np.cos(ang), np.sin(ang)
    scale = HD ** -0.5
    return np.stack([c * scale, s * scale, c, s], 1).astype(np.float32).reshape(P, 4 * S)


def small_constants():
    i = np.arange(P)
    ident = np.eye(P)
    blocks = (i[:, None] // HD == i[None, :] // HD)
    rot = np.zeros((P, P))
    for q in range(P):
        if (q // 16) % 2 == 0:
            rot[q + 16, q] = -1.0
        else:
            rot[q - 16, q] = 1.0
    t = i[:, None, None] + P * np.arange(2)[None, :, None]
    valid = (t - (16 * np.arange(NCMP) + 31)[None, None, :]) >= 0
    pick = np.zeros((P, 2))
    pick[[0, 2], 0] = 1
    pick[[1, 3], 1] = 1
    return np.concatenate([ident, blocks, np.ones((P, P)), rot, valid.reshape(P, -1), pick], 1).astype(np.float32)


def window_mask():
    q = np.arange(P)[:, None, None] + P * np.arange(2)[None, :, None]
    k = np.arange(S)[None, None, :]
    m = np.zeros((P, 2, 2 * S), np.float32)
    m[:, :, :S] = np.where(np.abs(q - k) <= 128, 0.0, MASKED)
    return m.reshape(P, -1)


VECTORS = [("norm_g", 6 * DT), ("ada_b", 144), ("final_g", DT), ("pw1_b", 16), ("dw_b", DT), ("ln_g", DT),
           ("ln_b", DT), ("pw2_b", DT), ("dw_w", CONV_W * DT), ("c", DT), ("c_ctx", DT), ("norm_mix", 2 * DT),
           ("norm_ffn", 2 * DT), ("norm_ple", 2 * DT), ("qk_gain_ab", 8), ("qk_gain_nsa", 6), ("kn_cmp", 1),
           ("cmp_b1", 2), ("cmp_k_b2", 1), ("cmp_pos", 32), ("sink", NH)]
VCOL = {}
_at = 0
for _name, _n in VECTORS:
    VCOL[_name] = _at
    _at += _n
NVEC = _at
NCONST = 4 * P + 2 * NCMP + 2


class Stage:

    def __init__(self, kind, slabs=0, T=S, mod=None, layer=0, ada=0, gate=None, how=None, gain=None, what=None):
        self.kind, self.slabs, self.T, self.mod, self.layer = kind, slabs, T, mod, layer
        self.ada, self.gate, self.how, self.gain, self.what = ada, gate, how, gain, what


def ffn_stages(layer, tokens, ada=0, mod=None):
    return [Stage("up", 22 + ada, T=tokens, ada=ada), Stage("down", 12, T=tokens, mod=mod)]


def make_plan():
    st = [Stage("start"), Stage("ada", 10)]
    both = 2 * S
    for layer in range(2):
        st += [Stage("mods", mod=0, layer=layer, gate=None if layer else False),
               Stage("norm", T=both, how="mod", mod=0)]
        st += ffn_stages(layer, both, ada=18 if layer else 22, mod=0)
        if layer == 0:
            st.insert(-1, Stage("mods", mod=0, layer=0, gate=True))
        st += [Stage("mods", mod=1, layer=layer),
               Stage("norm", T=both, how="mod", mod=1)]
        if layer == 1:
            st.insert(-1, Stage("mods", mod=2, layer=1))
        if layer == 0:
            st += [Stage("pw1", 8, T=both), Stage("conv"), Stage("pw2", 4, T=both, mod=1),
                   Stage("mods", mod=2, layer=0, gate=False),
                   Stage("norm", T=both, how="mod", mod=2),
                   Stage("up", 44, T=both, ada=22), Stage("mods", mod=2, layer=0, gate=True),
                   Stage("down", 12, T=both, mod=2)]
        else:
            st += [Stage("qkv", 6), Stage("att", what="window"), Stage("wo", 4, T=S, mod=1),
                   Stage("norm", T=S, how="mod", mod=2)]
            st += ffn_stages(1, S, mod=2)
    st += [Stage("norm", T=S, how="final")]
    for layer in range(2):
        st += [Stage("norm", T=S, how="gain", gain=VCOL["norm_mix"] + DT * layer)]
        if layer == 0:
            st += [Stage("qknorm", 8, gain=VCOL["qk_gain_ab"]), Stage("vab", 4), Stage("att", what="ab")]
        else:
            st += [Stage("qknorm", 6, gain=VCOL["qk_gain_nsa"]), Stage("nsakv", 5), Stage("cmp", 2),
                   Stage("att", what="nsa")]
        st += [Stage("wo", 4, T=S, mod=None),
               Stage("norm", T=S, how="gain", gain=VCOL["norm_ffn"] + DT * layer)]
        st += ffn_stages(layer, S)
        st += [Stage("pleload", layer=layer), Stage("norm", T=S, how="gain", gain=VCOL["norm_ple"] + DT * layer),
               Stage("pleproj", 1, layer=layer), Stage("plegate", 4, layer=layer)]
    st += [Stage("end")]
    return st


def plan_with_counts():
    at = dict(up=0, rs=0, add=0, n=0, m=0, u=0, h=0, sq=0, sum=0, std=0, g=0, q=0, att=0, qk=0)
    plan = make_plan()
    made, before = 0, None
    for st in plan:
        st.made = made
        st.add0, st.up0, st.rs0 = at["add"], at["up"], at["rs"]
        st.n0, st.m0, st.g0, st.q0, st.qk0, st.att0 = at["n"], at["m"], at["g"], at["q"], at["qk"], at["att"]
        st.u0, st.h0, st.sq0, st.sum0, st.std0 = at["u"], at["h"], at["sq"], at["sum"], at["std"]
        at["n"] += st.slabs
        groups = dict(up=22, pw1=8, down=4, pw2=4, wo=4, plegate=4, pleproj=2, conv=2, cmp=2)
        at["m"] += st.slabs if st.kind in ("qkv", "qknorm", "vab", "nsakv") else groups.get(st.kind, 0)
        if st.kind == "up":
            at["g"] += 11
            at["q"] += st.ada
        elif st.kind == "ada":
            at["q"] += st.slabs
        elif st.kind == "norm":
            st.items = 2 * DT if (st.how == "mod" and st.T == 2 * S) else DT
            st.shared = st.how == "gain"
            at["u"] += st.items // 2 if st.shared else st.items
            at["up"] += st.items // 2 if st.shared else 0
            at["rs"] += 1
            at["h"] += st.items if st.how != "final" else 0
            made = st.items
        elif st.kind == "conv":
            at["u"] += DT
            at["h"] += DT
            made = DT
        elif st.kind == "att":
            at["att"] += 1
        elif st.kind == "qknorm":
            at["qk"] += st.slabs
            at["sum"] += st.slabs
            at["std"] += st.slabs
        if st.kind in ("down", "pw2", "wo"):
            at["sq"] += 4
            at["add"] += 4
        if st.kind in ("norm", "conv"):
            st.summed = st.kind == "norm" and before in ("down", "pw2", "wo")
            at["sq"] += 0 if st.summed else DT
            at["sum"] += 1 if st.summed else DT
            at["std"] += 1
        if st.kind not in ("mods", "pleload"):
            before = st.kind
    return plan, at["n"]


def landed(n):
    return 16 * (n // 2 + 1)


def room(m):
    return 1 + m // 2


def freed(m):
    return 2 + m // 2


class Steps:

    def __init__(self, eng, sem):
        self.eng, self.sem, self.n, self.dyn = eng, sem, 0, 0

    def done(self, ins):
        ins.then_inc(self.sem, 1)
        self.n += 1
        self.eng.wait_ge(self.sem, self.n + self.dyn)

    def mark(self, ins):
        ins.then_inc(self.sem, 1)
        self.n += 1
        return self.n + self.dyn

    def loop(self, i, per):
        self.dyn = i * per

    def end(self, per, times):
        self.dyn = 0
        self.n += per * (times - 1)


def across(ap, n, at=1):
    dims = [list(x) for x in ap.ap]
    dims.insert(at, [0, n])
    return bass.AP(ap.tensor, ap.offset, dims)


def build(nc, slabs_d, x_d, vec_d, const_d, w2_d, tab_d, hot_d, rope_d, mask_d, p_d, out_d, stop_after=None):
    plan, NS = plan_with_counts()
    if stop_after is not None:
        end = plan[stop_after]
        end.kind = "end"
        plan = plan[:stop_after] + [end]
        NS = plan[-2].n0 + plan[-2].slabs + 2
    lines_d = nc.dram_tensor("lines_dram", (NH, 768), F32, kind="Internal").ap()
    skew_d = nc.dram_tensor("skew_dram", (P, 2 * NH * 384), F32, kind="Internal").ap()

    with ExitStack() as ctx:
        def sb(name, shape, dt=F32, where=ctx):
            return where.enter_context(nc.sbuf_tensor(name, shape, dt))

        def sem(name):
            return ctx.enter_context(nc.semaphore(name))

        x = sb("x", [P, DT, 2 * S])
        hhi = sb("hhi", [P, DT, 2 * S], F32R)
        hlo = sb("hlo", [P, DT, 2 * S], F32R)
        raw = sb("raw", [P, 2, SLAB])
        whi = sb("whi", [P, 2, SLAB], F32R)
        wlo = sb("wlo", [P, 2, SLAB], F32R)
        const = sb("const", [P, NCONST])
        vec = sb("vec", [P, NVEC])
        w2 = sb("w2", [P, 256])
        gate_sb = sb("gate_sb", [P, 2, 512])
        prod = sb("prod", [P, 2, 512])
        rs = sb("rs", [P, 2 * S])
        mA = sb("mA", [P, 3, DT, 2])
        mB = sb("mB", [P, 3, DT, 2])
        mG = sb("mG", [P, 3, DT, 2])
        cs = sb("cs", [P, DT, 2])
        c4 = sb("c4", [P, DT, 4], F32R)
        arow = sb("arow", [4, 2, SLAB_N])
        eps = sb("eps", [P, 1])
        tab = sb("tab", [33, NH])
        gb = sb("gb", [P, DT, 2])
        junk = sb("junk", [P, 1])
        junk_act = sb("junk_act", [P, 1])

        with ExitStack() as ffn:
            ghi = sb("ghi", [P, HT, 2 * S], F32R, ffn)
            glo = sb("glo", [P, HT, 2 * S], F32R, ffn)
        with ExitStack() as first:
            hot = sb("hot", [33, 768], F32, first)
            lines = sb("line_rows", [NH, 768], F32, first)
        with ExitStack() as cv:
            ubuf = sb("ubuf", [P, DT, 2, SP_], F32, cv)
            v = sb("v", [P, DT, 2 * S], F32, cv)
            diag = sb("diag", [P, 2, len(PE_TILES), P], F32, cv)
            tap_out = sb("tap_out", [P, len(POOL_TILES), 2 * S], F32, cv)
        with ExitStack() as at:
            ohi = sb("ohi", [P, DT, S], F32R, at)
            olo = sb("olo", [P, DT, S], F32R, at)
            QK = sb("QK", [P, 16, S], F32, at)
            kd = sb("kd", [P, 2 * NKV, S], F32, at)
            vt = sb("vt", [P, 2048], F32, at)
            sc = sb("sc", [P, 4, 512], F32, at)
            pT = sb("pT", [P, 2, 512], F32, at)
            stt4 = sb("stt4", [P, 4, 10], F32, at)
            with ExitStack() as w:
                kraw = sb("kraw", [P, 2, 512], F32, w)
                rope = sb("rope", [P, 4, S], F32, w)
                mask = sb("mask", [P, 2, 512], F32, w)
            bt = sb("bt", [P, NH, S], F32, at)
            craw = kd[:, :, :].rearrange("p (a b) t -> p a b t", a=2)
            Vm = sb("Vm", [P, NH, HD], F32, at)
            Pc = sb("Pc", [P, 2, NH, 32], F32, at)
            PcT = sb("PcT", [P, NKV, 2, P], F32, at)
            hid = sb("hid", [P, 2, 4, 16], F32, at)
            kcmp = sb("kcmp", [P, 4, 16], F32, at)
            kcsq = sb("kcsq", [P, 64], F32, at)
            kcr = sb("kcr", [P, 64], F32, at)
            vcmp = sb("vcmp", [16, NKV, HD], F32, at)
            gates = sb("gates", [P, 2, 48], F32, at)
            cst = sb("cst", [P, 3, NH], F32, at)
        with ExitStack() as cm:
            bhi = sb("bhi", [P, 2, 16, 64], F32R, cm)
            blo = sb("blo", [P, 2, 16, 64], F32R, cm)
        blk = sc[:, :, :].rearrange("p a (b c) -> p (a b) c", c=64).rearrange("p (k l) c -> p k l c", k=2)
        with ExitStack() as pl:
            pT_raw = sb("ptok", [P, 2, S], F32, pl)
            phi = sb("phi", [P, 2, S], F32R, pl)
            plo = sb("plo", [P, 2, S], F32R, pl)
            pp = sb("pp", [P, DT, S], F32, pl)
        ident = const[:, 0:P]
        headones = const[:, P:2 * P]
        ones = const[:, 2 * P:3 * P]
        rot = const[:, 3 * P:4 * P]
        pick = const[0:4, NCONST - 2:NCONST]
        valid = const[:, 4 * P:NCONST - 2].rearrange("p (q c) -> p q c", q=2)
        sq = gate_sb
        ub2 = ubuf[:, :, :, :].rearrange("p a s t -> p (a s) t")
        ub = prod[:, :, :].rearrange("p a (b c) -> p (a b) c", c=S)

        acc = ctx.enter_context(nc.psum_tensor("acc", [P, 2, 2, 512], F32))
        Mod = ctx.enter_context(nc.psum_tensor("Mod", [P, 512], F32))
        B = [Mod] + [ctx.enter_context(nc.psum_tensor(f"bank{i}", [P, 512], F32)) for i in (5, 6, 7)]
        sums = B[1]

        slab_landed = [sem("slab_landed0"), sem("slab_landed1")]
        hi_half = sem("hi_half")
        hi_ready = sem("hi_ready")
        lo_half = sem("lo_half")
        lo_ready = sem("lo_ready")
        half_used = sem("half_used")
        slab_used = sem("slab_used")
        acc_free = [sem("acc_free0"), sem("acc_free1")]
        loaded = sem("loaded")
        vec_landed = sem("vec_landed")
        const_landed = sem("const_landed")
        x_landed = sem("x_landed")
        eps_ready = sem("eps_ready")
        line_pe = sem("line_pe")
        c_ready = sem("c_ready")
        row_ready = sem("row_ready")
        row_turned = sem("row_turned")
        ple_gate = sem("ple_gate")
        kd_dve = sem("kd_dve")
        kd_act = sem("kd_act")
        sq_ready = sem("sq_ready")
        sq_added = sem("sq_added")
        sum_done = sem("sum_done")
        std_ready = sem("std_ready")
        rs_ready = sem("rs_ready")
        u_ready = sem("u_ready")
        u_pool = sem("u_pool")
        h_hi = sem("h_hi")
        h_ready = sem("h_ready")
        g_hi = sem("g_hi")
        g_lo = sem("g_lo")
        dve_step = sem("dve_step")
        act_step = sem("act_step")
        lines_ready = sem("lines_ready")
        lines_done = sem("lines_done")
        skew_done = sem("skew_done")
        diag_ready = sem("diag_ready")
        taps_used = sem("taps_used")
        conv_dve = sem("conv_dve")
        conv_pool = sem("conv_pool")
        mean_done = sem("mean_done")
        d_ready = sem("d_ready")
        qk_done = sem("qk_done")
        rot_done = sem("rot_done")
        rope_done = sem("rope_done")
        rope_landed = sem("rope_landed")
        bias_landed = sem("bias_landed")
        att_ready = sem("att_ready")
        s_ready = sem("s_ready")
        s_free = sem("s_free")
        m_ready = sem("m_ready")
        e_ready = sem("e_ready")
        p_ready = sem("p_ready")
        t_ready = sem("t_ready")
        pt_ready = sem("pt_ready")
        pv_done = sem("pv_done")
        o_hi = sem("o_hi")
        o_lo = sem("o_lo")
        cmp_pe = sem("cmp_pe")
        cmp_dve = sem("cmp_dve")
        cmp_act = sem("cmp_act")
        blk_hi = sem("blk_hi")
        blk_lo = sem("blk_lo")
        vm_landed = sem("vm_landed")
        vm_zero = sem("vm_zero")
        p_landed = sem("p_landed")
        p_split = sem("p_split")
        pool_go = sem("pool_go")
        stored = sem("stored")

        block = ctx.enter_context(nc.Block())

        def x_final(eng, st):
            m = st.m0
            if m:
                eng.wait_ge(acc_free[0], 1 + (m + 1) // 2)
                eng.wait_ge(acc_free[1], 1 + m // 2)
            if st.u0:
                eng.wait_ge(u_ready, st.u0)
                eng.wait_ge(u_pool, st.up0)
            else:
                eng.wait_ge(x_landed, 16)

        def place(st, k):
            return (k // 2, k % 2) if st.items == 2 * DT else (k, 0)

        def conv_out(j):
            e = j - PE_TILES[0]
            return acc[:, e // 2, e % 2, :]

        def scaled_row(engine, st, k):
            c, s = place(st, k)
            cols = slice(S * s, S * s + S)
            if st.how == "mod":
                g = mA[:, st.mod, c, s:s + 1]
            elif st.how == "gain":
                g = vec[:, st.gain + c:st.gain + c + 1]
            else:
                g = vec[:, VCOL["final_g"] + c:VCOL["final_g"] + c + 1]
            dst = x[:, c, cols] if st.how == "final" else ub[:, k % 4, :]
            return engine.scalar_tensor_tensor(dst, x[:, c, cols], g, rs[:, cols], ALU.mult, ALU.mult)

        @block.sync
        def _(sp):
            sp.dma_start(raw[:, 0, :], slabs_d[0]).then_inc(slab_landed[0], 16)
            sp.dma_start(raw[:, 1, :], slabs_d[1]).then_inc(slab_landed[1], 16)
            with sp.Fori(0, (NS - 2) // 2) as i:
                for c in range(2):
                    sp.wait_ge(lo_ready, 2 * i + (c + 1))
                    sp.dma_start(raw[:, c, :], slabs_d[bass.ds(2 * i + (c + 2), 1)].rearrange("a p n -> p (a n)"))\
                      .then_inc(slab_landed[c], 16)
            if NS % 2:
                sp.wait_ge(lo_ready, NS - 2)
                sp.dma_start(raw[:, (NS - 1) % 2, :], slabs_d[NS - 1]).then_inc(slab_landed[(NS - 1) % 2], 16)
            x_final(sp, plan[-1])
            sp.dma_start(out_d, x[:, :, 0:S]).then_inc(stored, 16)
            sp.wait_ge(stored, 16)

        @block.gpsimd
        def _(pool):
            nc.gpsimd.memset(eps[:, :], EPS).then_inc(eps_ready, 1)
            nc.gpsimd.memset(tab[:, :], 1.0).then_inc(eps_ready, 1)
            pool.sem_inc(acc_free[0], 1)
            pool.sem_inc(acc_free[1], 1)
            pool.sem_inc(qk_done, 2)
            pool.sem_inc(s_free, 4)
            pool.sem_inc(pv_done, 2)
            pool.sem_inc(o_lo, 2)
            pool.sem_inc(pt_ready, 2)
            pool.sem_inc(t_ready, 4)
            pool.sem_inc(g_lo, 1)
            pool.sem_inc(sq_added, 1)
            pool.wait_ge(eps_ready, 2)
            pool.dma_start(tab[0:32, :], tab_d).then_inc(loaded, 16)
            pool.dma_start(hot[:, :], hot_d).then_inc(loaded, 16)
            pool.wait_ge(lines_ready, 2)
            pool.dma_start(lines_d, lines[:, :]).then_inc(lines_done, 16)
            pool.wait_ge(lines_done, 16)

            def bias_rows(heads, kind):
                return bass.AP(skew_d.tensor, 384 * (2 * heads.start + kind) + 127,
                               [[2 * NH * 384 - 1, P], [768, len(heads)], [1, S]])

            def norm_share(st):
                x_final(pool, st)
                pool.wait_ge(rs_ready, st.rs0 + 1)
                for k in range(1, st.items, 2):
                    if k >= 4:
                        pool.wait_ge(h_ready, st.h0 + k - 3)
                    nc.gpsimd.tensor_tensor(ub[:, k % 4, :], x[:, k, 0:S], rs[:, 0:S], ALU.mult).then_inc(u_pool, 1)

            def conv_share(st):
                pool.wait_ge(acc_free[(st.m0 + 1) % 2], freed(st.m0 + 1))
                n = len(POOL_TILES)
                done = 0
                for t in range(CONV_W):
                    for add in (False, True) if t else (False,):
                        for j in POOL_TILES:
                            w, b = VCOL["dw_w"] + CONV_W * j + t, VCOL["dw_b"] + j
                            src = ub2[:, 2 * j:2 * j + 2, t:t + S]
                            out = v[:, j, :].rearrange("p (s t) -> p s t", s=2)
                            if t:
                                pool.wait_ge(conv_pool, done - n + 1)
                            if add:
                                ins = nc.gpsimd.tensor_tensor(v[:, j, :], v[:, j, :], tap_out[:, j, :], ALU.add)
                            elif t:
                                ins = nc.gpsimd.tensor_scalar(
                                    tap_out[:, j, :].rearrange("p (s t) -> p s t", s=2), src, vec[:, w:w + 1], None,
                                    ALU.mult)
                            else:
                                ins = nc.gpsimd.tensor_scalar(out, src, vec[:, w:w + 1], vec[:, b:b + 1],
                                                              ALU.mult, ALU.add)
                            ins.then_inc(conv_pool, 1)
                            done += 1

            go, skewed = 0, False
            for st in plan:
                if st.kind == "norm" and st.shared:
                    norm_share(st)
                if st.kind == "pw1":
                    conv_share(st)
                if st.kind == "down" and not skewed:
                    skewed = True
                    pool.wait_ge(slab_used, st.n0)
                    pool.dma_start(skew_d, bass.AP(lines_d.tensor, 0, [[0, P], [1, NH * 768]])).then_inc(skew_done, 16)
                if st.kind == "qkv":
                    go += 1
                    pool.wait_ge(pool_go, go)
                    pool.dma_start(rope[:, :, :], rope_d.rearrange("p (a t) -> p a t", a=4)).then_inc(rope_landed, 16)
                    pool.dma_start(mask[:, :, :], mask_d.rearrange("p (a t) -> p a t", a=2)).then_inc(rope_landed, 16)
                if st.kind == "qknorm":
                    go += 1
                    pool.wait_ge(pool_go, go)
                    ab = st.slabs == 8
                    pool.wait_ge(skew_done, 16)
                    pool.dma_start(bt[:, 0:8, :], bias_rows(range(0, 8), 0)).then_inc(bias_landed, 16)
                    pool.dma_start(bt[:, 8:16, :], bias_rows(range(8, 16), 1 if ab else 0)).then_inc(bias_landed, 16)
                    if not ab:
                        nc.gpsimd.memset(Vm[:, :, :], 0.0).then_inc(vm_zero, 1)
                        nc.gpsimd.memset(Pc[:, :, :, :], 0.0).then_inc(vm_zero, 1)
                        nc.gpsimd.memset(sc[:, :, :], 0.0).then_inc(vm_zero, 1)
                if st.kind == "cmp":
                    pool.wait_ge(vm_zero, 3)
                    pool.wait_ge(cmp_dve, 4)
                    for hl in range(4):
                        pool.dma_start(Vm[32 * hl:32 * hl + NCMP, hl:NH:4, :], vcmp[0:NCMP, :, :])\
                            .then_inc(vm_landed, 16)
                if st.kind == "pleload":
                    go += 1
                    pool.wait_ge(pool_go, go)
                    pool.dma_start(pT_raw[:, :, :], p_d[st.layer]).then_inc(p_landed, 16)
                    pool.wait_ge(p_landed, 16 * (st.layer + 1))
                    nc.gpsimd.tensor_copy(phi[:, :, :], pT_raw[:, :, :]).then_inc(p_split, 1)
                    pool.wait_ge(p_split, 2 * st.layer + 1)
                    nc.gpsimd.tensor_tensor(plo[:, :, :], pT_raw[:, :, :], phi[:, :, :].bitcast(F32), ALU.subtract)\
                        .then_inc(p_split, 1)

        @block.scalar
        def _(act):
            step = Steps(act, act_step)
            act.dma_start(vec[:, :], vec_d).then_inc(vec_landed, 16)
            act.dma_start(const[:, :], const_d).then_inc(const_landed, 16)
            act.dma_start(w2[:, :], w2_d).then_inc(const_landed, 16)

            def hi(n, i=0, per=0):
                if n >= NS:
                    return
                act.wait_ge(slab_landed[n % 2], landed(n) + i * (8 * per))
                for cols, used, ready in ((FIRST, half_used, hi_half), (SECOND, slab_used, hi_ready)):
                    if n >= 2:
                        act.wait_ge(used, n - 1 + i * per)
                    nc.scalar.activation(whi[:, n % 2, cols], raw[:, n % 2, cols], ACT.Copy).then_inc(ready, 1)

            def start(st):
                act.wait_ge(vec_landed, 16)
                act.wait_ge(eps_ready, 2)
                step.done(nc.scalar.activation(cs[:, :, 0], vec[:, VCOL["c"]:VCOL["c"] + DT], ACT.Silu))
                step.done(nc.scalar.activation(cs[:, :, 1], vec[:, VCOL["c_ctx"]:VCOL["c_ctx"] + DT], ACT.Silu))
                nc.scalar.activation(c4[:, :, 0:2], cs[:, :, :], ACT.Copy).then_inc(c_ready, 1)
                hi(0)
                hi(1)
                act.dma_start(x[:, :, :], x_d).then_inc(x_landed, 16)

            def ada_row(n, q, i, per):
                act.wait_ge(slab_used, n + 1 + i * per)
                if q >= 2:
                    act.wait_ge(row_turned, q - 1 + 2 * i)
                nc.scalar.activation(arow[:, q % 2, :], B[2 + q % 2][0:4, 0:SLAB_N], ACT.Copy).then_inc(row_ready, 1)

            def ada(st):
                for c in range(2):
                    ada_row(st.n0 + c, st.q0 + c, 0, 0)
                    hi(st.n0 + c + 2)
                with act.Fori(0, st.slabs // 2 - 1) as i:
                    for c in range(2):
                        ada_row(st.n0 + c + 2, st.q0 + c + 2, i, 2)
                        hi(st.n0 + c + 4, i, 2)

            def up(st):
                both = st.ada // 2
                act.wait_ge(lines_done, 16)
                for first, count, per in ((0, both, 4), (both, 11 - both, 2)):
                    if not count:
                        continue
                    n = st.n0 + 4 * first
                    m = st.m0 + 2 * first
                    with act.Fori(0, count) as i:
                        nc.scalar.activation(junk_act[:, :], eps[:, :], ACT.Silu)
                        if per == 4:
                            ada_row(n, st.q0, i, per)
                            hi(n + 2, i, per)
                            hi(n + 3, i, per)
                        else:
                            hi(n + 2, i, per)
                        act.wait_ge(slab_used, n + per // 2 + i * per)
                        act.wait_ge(acc_free[(m + 1) % 2], room(m + 1) + i)
                        nc.scalar.activation(gate_sb[:, :, 0:st.T], acc[:, m % 2, :, 0:st.T], ACT.Silu)\
                            .then_inc(acc_free[m % 2], 1)
                        if per == 4:
                            ada_row(n + 2, st.q0 + 1, i, per)
                            hi(n + 4, i, per)
                        hi(n + per + 1, i, per)
                        act.wait_ge(acc_free[(m + 1) % 2], freed(m + 1) + i)
                        nc.scalar.activation(ghi[:, bass.ds(2 * first + 2 * i, 2), 0:st.T], prod[:, :, 0:st.T],
                                             ACT.Copy).then_inc(g_hi, 1)

            def residual(st):
                ks = st.slabs // 4
                with act.Fori(0, 2) as i:
                    for c in range(2):
                        for kk in range(ks):
                            if kk == ks - 1:
                                m = st.m0 + c
                                act.wait_ge(acc_free[m % 2], freed(m) + i)
                                act.wait_ge(sq_added, st.add0 + c + 1 + 2 * i)
                                nc.scalar.activation(sq[:, :, 0:st.T], x[:, bass.ds(2 * c + 4 * i, 2), 0:st.T],
                                                     ACT.Square).then_inc(sq_ready, 1)
                            hi(st.n0 + 2 + ks * c + kk, i, 2 * ks)

            def norm(st):
                x_final(act, st)
                T = st.T
                if not st.summed:
                    for c in range(DT):
                        if c >= 2:
                            act.wait_ge(sum_done, st.sum0 + c - 1)
                        nc.scalar.activation(sq[:, c % 2, 0:T], x[:, c, 0:T], ACT.Square).then_inc(sq_ready, 1)
                act.wait_ge(sum_done, st.sum0 + (1 if st.summed else DT))
                nc.scalar.activation(rs[:, 0:T], sums[:, 0:T], ACT.Sqrt, bias=eps[:, 0:1], scale=1.0 / D)\
                    .then_inc(std_ready, 1)
                if st.how == "final":
                    return
                for k in range(st.items):
                    if not st.shared:
                        act.wait_ge(u_ready, st.u0 + k + 1)
                    elif k % 2:
                        act.wait_ge(u_pool, st.up0 + k // 2 + 1)
                    else:
                        act.wait_ge(u_ready, st.u0 + k // 2 + 1)
                    c, s = (k // 2, k % 2) if st.items == 2 * DT else (k, 0)
                    dst = hhi[:, c, S * s:S * s + S]
                    if st.how == "mod":
                        ins = nc.scalar.activation(dst, ub[:, k % 4, :], ACT.Identity,
                                                   bias=mB[:, st.mod, c, s:s + 1])
                    elif k % 2:
                        ins = nc.scalar.activation(dst, ub[:, k % 4, :], ACT.Copy,
                                                   scale=vec[:, st.gain + c:st.gain + c + 1])
                    else:
                        ins = nc.scalar.activation(dst, ub[:, k % 4, :], ACT.Copy)
                    ins.then_inc(h_hi, 1)

            def pw1(st):
                with act.Fori(0, 4) as i:
                    act.wait_ge(slab_used, st.n0 + 1 + 2 * i)
                    act.wait_ge(acc_free[(st.m0 + 1) % 2], room(st.m0 + 1) + i)
                    for t in range(2):
                        ins = nc.scalar.activation(gate_sb[:, t, :], acc[:, st.m0 % 2, t, :], ACT.Sigmoid,
                                                   bias=vec[:, bass.ds(VCOL["pw1_b"] + DT + t + 2 * i, 1)])
                    ins.then_inc(acc_free[st.m0 % 2], 1)
                    hi(st.n0 + 2, i, 2)
                    hi(st.n0 + 3, i, 2)

            def conv(st):
                def tap(t, par, wait):
                    if wait is not None:
                        act.wait_ge(taps_used, wait)
                    for j in PE_TILES:
                        ins = nc.scalar.activation(diag[:, par, j - PE_TILES[0], :], ident, ACT.Copy,
                                                   scale=vec[:, bass.ds(VCOL["dw_w"] + CONV_W * j + t, 1)])
                    ins.then_inc(diag_ready, 1)

                tap(0, 0, None)
                tap(1, 1, None)
                with act.Fori(0, 14) as i:
                    tap(2 * i + 2, 0, 2 * i + 1)
                    tap(2 * i + 3, 1, 2 * i + 2)
                tap(30, 0, 29)
                act.wait_ge(taps_used, 31)
                for j in PE_TILES:
                    ins = nc.scalar.activation(v[:, j, :], conv_out(j), ACT.Identity,
                                               bias=vec[:, VCOL["dw_b"] + j:VCOL["dw_b"] + j + 1])
                    if j != PE_TILES[0]:
                        ins.then_inc(acc_free[(j - PE_TILES[0]) // 2], 1)
                for c in range(DT):
                    act.wait_ge(d_ready, c + 1)
                    if c >= 2:
                        act.wait_ge(sum_done, st.sum0 + c - 1)
                    nc.scalar.activation(sq[:, c % 2, :], v[:, c, :], ACT.Square).then_inc(sq_ready, 1)
                act.wait_ge(sum_done, st.sum0 + 8)
                nc.scalar.activation(rs[:, :], sums[:, :], ACT.Sqrt, bias=eps[:, 0:1], scale=1.0 / D)\
                    .then_inc(std_ready, 1)
                for c in range(DT):
                    act.wait_ge(u_ready, st.u0 + c + 1)
                    if c >= 2:
                        act.wait_ge(h_ready, st.h0 + c - 1)
                    step.done(nc.scalar.activation(sq[:, c % 2, :], v[:, c, :], ACT.Silu,
                                                   bias=vec[:, VCOL["ln_b"] + c:VCOL["ln_b"] + c + 1]))
                    nc.scalar.activation(hhi[:, c, :], sq[:, c % 2, :], ACT.Copy).then_inc(h_hi, 1)

            def qkv(st):
                for c in range(6):
                    n, m = st.n0 + c, st.m0 + c
                    act.wait_ge(slab_used, n + 1)
                    a = acc[:, m % 2]
                    if c < 4:
                        ins = nc.scalar.activation(QK[:, 2 * c:2 * c + 2, :], a[:, :, 0:S], ACT.Copy)
                    elif c == 4:
                        ins = nc.scalar.activation(kraw[:, :, :], a, ACT.Copy)
                    else:
                        ins = nc.scalar.activation(vt[:, 0:1024], a.rearrange("p a b -> p (a b)"), ACT.Copy)
                    ins.then_inc(acc_free[m % 2], 1)
                    hi(n + 2)

            def qknorm(st):
                n, m = st.n0, st.m0
                with act.Fori(0, st.slabs // 2) as i:
                    for c in range(2):
                        act.wait_ge(slab_used, n + c + 1 + 2 * i)
                        nc.scalar.activation(QK[:, bass.ds(4 * i + 2 * c, 2), :], acc[:, (m + c) % 2, :, 0:S], ACT.Copy)
                        nc.scalar.activation(sq[:, c, :], acc[:, (m + c) % 2, :, 0:S], ACT.Square)\
                            .then_inc(acc_free[(m + c) % 2], 1)
                        hi(n + c + 2, i, 2)
                    for c in range(2):
                        act.wait_ge(sum_done, st.sum0 + c + 1 + 2 * i)
                        act.wait_ge(qk_done, st.qk0 + c + 1 + 2 * i)
                        nc.scalar.activation(prod[:, c, :], B[1 + c][:, :], ACT.Sqrt, bias=eps[:, 0:1],
                                             scale=1.0 / HD).then_inc(std_ready, 1)

            def vab(st):
                with act.Fori(0, 2) as i:
                    for c in range(2):
                        m = st.m0 + c
                        act.wait_ge(slab_used, st.n0 + c + 1 + 2 * i)
                        nc.scalar.activation(
                            vt[:, :].rearrange("p (a b) -> p a b", a=2)[:, :, bass.ds(512 * i + 256 * c, S)],
                            acc[:, m % 2, :, 0:S], ACT.Copy).then_inc(acc_free[m % 2], 1)
                        hi(st.n0 + c + 2, i, 2)

            def nsakv(st):
                for c in range(5):
                    n, m = st.n0 + c, st.m0 + c
                    act.wait_ge(slab_used, n + 1)
                    a = acc[:, m % 2, :, 0:S]
                    if c < 2:
                        for half in range(2):
                            for src in range(2):
                                ins = nc.scalar.activation(
                                    craw[64 * half:64 * half + 64, c, 2 * src:2 * src + 2, 0:S - 16 * half],
                                    acc[64 * src:64 * src + 64, m % 2, :, 16 * half:S], ACT.Copy)
                    elif c < 4:
                        ins = nc.scalar.activation(
                            vt[:, 0:1024].rearrange("p (a b) -> p a b", a=2)[:, :, 256 * (c - 2):256 * (c - 1)],
                            a, ACT.Copy)
                    else:
                        ins = nc.scalar.activation(gates[:, :, :], a[:, :, 0:48], ACT.Sigmoid)
                    ins.then_inc(acc_free[m % 2], 1)
                    hi(n + 2)

            def cmp_(st):
                for kv in range(2):
                    act.wait_ge(cmp_dve, kv + 1)
                    nc.scalar.activation(bhi[:, kv], blk[:, kv], ACT.Copy).then_inc(blk_hi, 1)
                for kv in range(2):
                    m = st.m0 + kv
                    act.wait_ge(slab_used, st.n0 + kv + 1)
                    hi(st.n0 + kv + 2)
                    nc.scalar.activation(hid[:, kv, :, :].rearrange("p a b -> p (a b)"), acc[:, m % 2, 0, 0:64],
                                         ACT.Gelu_apprx_tanh, bias=vec[:, VCOL["cmp_b1"] + kv:VCOL["cmp_b1"] + kv + 1])\
                        .then_inc(acc_free[m % 2], 1)
                kf = kcmp[:, :, :].rearrange("p a b -> p (a b)")
                act.wait_ge(cmp_pe, 1)
                step.done(nc.scalar.activation(kf, B[1][:, 0:64], ACT.Identity,
                                               bias=vec[:, VCOL["cmp_k_b2"]:VCOL["cmp_k_b2"] + 1]))
                nc.scalar.activation(kcsq[:, :], kf, ACT.Square).then_inc(cmp_act, 1)
                act.wait_ge(cmp_pe, 3)
                nc.scalar.activation(kcr[:, :], B[2][:, 0:64], ACT.Sqrt, bias=eps[:, 0:1], scale=1.0 / HD)\
                    .then_inc(cmp_act, 1)
                for q, ncol in ((0, 7), (1, NCMP)):
                    act.wait_ge(cmp_dve, 5 + q)
                    nc.scalar.activation(Pc[:, q, :, 0:ncol], Pc[:, q, :, 0:ncol], ACT.Exp).then_inc(cmp_act, 1)
                for g in range(NKV):
                    act.wait_ge(cmp_pe, 8 + g)
                    nc.scalar.activation(PcT[:, g, :, :], B[1 + g % 2][:, 0:256], ACT.Copy).then_inc(cmp_act, 1)

            def copy_k(st):
                src = kraw if st.what == "window" else QK
                act.wait_ge(att_ready, st.att0 + 1)
                if st.what == "window":
                    for g in range(NKV):
                        ins = nc.scalar.activation(kd[0:64, 2 * g:2 * g + 2, :],
                                                   kraw[64 * (g % 2):64 * (g % 2) + 64, g // 2, :], ACT.Copy)
                else:
                    for j in range(8):
                        g = j % 4
                        ins = nc.scalar.activation(kd[0:64, j, :],
                                                   QK[64 * (g % 2):64 * (g % 2) + 64, 8 + 2 * (j // 4) + g // 2, :],
                                                   ACT.Copy)
                ins.then_inc(kd_act, 1)

            def att(st):
                if st.what != "ab":
                    copy_k(st)
                A0 = 32 * st.att0

                def exps(u):
                    act.wait_ge(m_ready, A0 + u + 1)
                    sp = stt4[:, u % 4]
                    keys = 512 if st.what == "window" else P * (u % 2 + 1)
                    for s in range(2 if st.what == "nsa" else 1):
                        ins = nc.scalar.activation(sc[:, u % 4, keys * s:keys * (s + 1)],
                                                   sc[:, u % 4, keys * s:keys * (s + 1)], ACT.Exp,
                                                   bias=sp[:, 2 + s:3 + s], accum_out=sp[:, 4 + s:5 + s])
                    if st.what == "window":
                        sink = VCOL["sink"] + u // 2
                        ins = nc.scalar.activation(sp[:, 6:7], vec[:, sink:sink + 1], ACT.Exp, bias=sp[:, 2:3])
                    ins.then_inc(e_ready, 1)

                def copied(u):
                    keys = 512 if st.what == "window" else P * (u % 2 + 1) * (2 if st.what == "nsa" else 1)
                    act.wait_ge(t_ready, 4 + A0 + u + 1)
                    act.wait_ge(pv_done, A0 + u + 1)
                    nc.scalar.activation(pT[:, u % 2, 0:keys], acc[:, u % 2, 1, 0:keys], ACT.Copy)\
                        .then_inc(pt_ready, 1)

                def out_hi(pair):
                    act.wait_ge(pv_done, 2 + A0 + 4 * pair + 4)
                    nc.scalar.activation(ohi[:, pair, :], acc[:, pair % 2, 0, 0:S], ACT.Copy).then_inc(o_hi, 1)

                for u in range(LEAD):
                    exps(u)
                for u in range(UNITS):
                    copied(u)
                    if u + LEAD < UNITS:
                        exps(u + LEAD)
                    if u % 4 == 1 and u > 4:
                        out_hi(u // 4 - 1)
                out_hi(DT - 1)

            def pleproj(st):
                for half, used in enumerate((half_used, slab_used)):
                    m = st.m0 + half
                    act.wait_ge(used, st.n0 + 1)
                    nc.scalar.activation(pp[:, 4 * half:4 * half + 4, :].rearrange("p a b -> p (a b)"),
                                         acc[:, m % 2].rearrange("p a b -> p (a b)"), ACT.Copy)\
                        .then_inc(acc_free[m % 2], 1)
                hi(st.n0 + 2)

            def plegate(st):
                for c in range(4):
                    n, m = st.n0 + c, st.m0 + c
                    act.wait_ge(slab_used, n + 1)
                    if c >= 2:
                        act.wait_ge(acc_free[m % 2], freed(m - 2))
                    nc.scalar.activation(gate_sb[:, :, (c % 2) * S:(c % 2 + 1) * S], acc[:, m % 2, :, 0:S],
                                         ACT.Sigmoid).then_inc(ple_gate, 1)
                    hi(n + 2)

            run = dict(start=start, ada=ada, up=up, down=residual, pw2=residual, wo=residual, norm=norm, pw1=pw1,
                       conv=conv, qkv=qkv, qknorm=qknorm, vab=vab, nsakv=nsakv, cmp=cmp_, att=att,
                       pleproj=pleproj, plegate=plegate)
            for st in plan:
                if st.kind in run:
                    run[st.kind](st)

        @block.vector
        def _(dve):
            step = Steps(dve, dve_step)

            def lo(n, i=0, per=0, halves=(0, 1)):
                if n >= NS:
                    return
                for half in halves:
                    cols, ready, low = ((FIRST, hi_half, lo_half), (SECOND, hi_ready, lo_ready))[half]
                    dve.wait_ge(ready, n + 1 + i * per)
                    nc.vector.tensor_tensor(wlo[:, n % 2, cols], raw[:, n % 2, cols],
                                            whi[:, n % 2, cols].bitcast(F32), ALU.subtract).then_inc(low, 1)

            def let_pool_load():
                nc.vector.memset(junk[:, :], 0.0).then_inc(pool_go, 1)

            def start(st):
                dve.wait_ge(vec_landed, 16)
                dve.wait_ge(const_landed, 32)
                for col in (VCOL["qk_gain_ab"], VCOL["qk_gain_nsa"]):
                    nc.vector.tensor_scalar(vec[:, col:col + 4], vec[:, col:col + 4], HD ** -0.5, None, ALU.mult)
                dve.wait_ge(c_ready, 1)
                nc.vector.tensor_tensor(c4[:, :, 2:4], cs[:, :, :], c4[:, :, 0:2].bitcast(F32), ALU.subtract)\
                    .then_inc(c_ready, 1)
                for j in range(2):
                    dve.wait_ge(line_pe, j + 1)
                    nc.vector.tensor_copy(lines[:, 384 * j:384 * j + 384], B[1 + j][0:NH, 0:384])\
                        .then_inc(lines_ready, 1)
                lo(0)
                lo(1)

            def ada(st):
                with dve.Fori(0, st.slabs // 2) as i:
                    lo(st.n0 + 2, i, 2)
                    lo(st.n0 + 3, i, 2)

            def mods(st):
                dve.wait_ge(row_turned, st.q0)
                gate = st.gate
                first = 24 * st.mod

                def sums_of(dst, tile):
                    M = Mod[:, 144 * st.layer + 2 * tile:144 * st.layer + 2 * tile + 2 * DT]
                    b = VCOL["ada_b"] + 72 * st.layer + tile
                    step.done(nc.vector.tensor_tensor(dst, M.rearrange("p (a b) -> p a b", b=2),
                                                      across(vec[:, b:b + DT], 2, 2), ALU.add))

                if gate is not True:
                    g = VCOL["norm_g"] + DT * (3 * st.layer + st.mod)
                    sums_of(mB[:, st.mod], first)
                    sums_of(mA[:, st.mod], first + DT)
                    step.done(nc.vector.scalar_tensor_tensor(mA[:, st.mod], mA[:, st.mod], 1.0,
                                                             across(vec[:, g:g + DT], 2, 2), ALU.add, ALU.mult))
                if gate is not False:
                    sums_of(mG[:, st.mod], first + 2 * DT)
                    if st.mod != 1:
                        step.done(nc.vector.tensor_scalar(mG[:, st.mod], mG[:, st.mod], 0.5, None, ALU.mult))

            def norm(st):
                x_final(dve, st)
                T = st.T
                dve.wait_ge(std_ready, st.std0 + 1)
                nc.vector.reciprocal(rs[:, 0:T], rs[:, 0:T]).then_inc(rs_ready, 1)
                dve.wait_ge(rs_ready, st.rs0 + 1)

                def scaled(k):
                    scaled_row(nc.vector, st, k).then_inc(u_ready, 1)

                def low(k):
                    c, s = place(st, k)
                    cols = slice(S * s, S * s + S)
                    dve.wait_ge(h_hi, st.h0 + k + 1)
                    if st.how == "mod":
                        ins = nc.vector.scalar_tensor_tensor(hlo[:, c, cols], ub[:, k % 4, :],
                                                             mB[:, st.mod, c, s:s + 1],
                                                             hhi[:, c, cols].bitcast(F32), ALU.add, ALU.subtract)
                    elif k % 2:
                        g = st.gain + c
                        ins = nc.vector.scalar_tensor_tensor(hlo[:, c, cols], ub[:, k % 4, :], vec[:, g:g + 1],
                                                             hhi[:, c, cols].bitcast(F32), ALU.mult, ALU.subtract)
                    else:
                        ins = nc.vector.tensor_tensor(hlo[:, c, cols], ub[:, k % 4, :],
                                                      hhi[:, c, cols].bitcast(F32), ALU.subtract)
                    ins.then_inc(h_ready, 1)

                if st.how == "final":
                    for k in range(st.items):
                        scaled(k)
                    return
                for k in (0, 2) if st.shared else (0, 1, 2):
                    scaled(k)
                for k in range(st.items):
                    low(k)
                    if k + 3 < st.items and (k % 2 or not st.shared):
                        if k:
                            dve.wait_ge(h_ready, st.h0 + k)
                        scaled(k + 3)

            def up(st):
                both = st.ada // 2
                for first, count, per in ((0, both, 4), (both, 11 - both, 2)):
                    if not count:
                        continue
                    n = st.n0 + 4 * first
                    m = st.m0 + 2 * first
                    T = st.T
                    with dve.Fori(0, count) as i:
                        for c in range(2, per + 1):
                            lo(n + c, i, per)
                        lo(n + per + 1, i, per, (0,))
                        dve.wait_ge(acc_free[m % 2], freed(m) + i)
                        dve.wait_ge(slab_used, n + per + i * per)
                        dve.wait_ge(g_lo, st.g0 + first + 1 + i)
                        nc.vector.tensor_tensor(prod[:, :, 0:T], gate_sb[:, :, 0:T], acc[:, (m + 1) % 2, :, 0:T],
                                                ALU.mult).then_inc(acc_free[(m + 1) % 2], 1)
                        lo(n + per + 1, i, per, (1,))
                        dve.wait_ge(g_hi, st.g0 + first + 1 + i)
                        tiles = bass.ds(2 * first + 2 * i, 2)
                        nc.vector.tensor_tensor(glo[:, tiles, 0:T], prod[:, :, 0:T],
                                                ghi[:, tiles, 0:T].bitcast(F32), ALU.subtract).then_inc(g_lo, 1)

            def residual(st):
                ks = st.slabs // 4
                xf = x[:, :, :].rearrange("p a b -> p (a b)")
                mGf = mG[:, :, :, :].rearrange("p a b c -> p (a b c)")
                dve.wait_ge(g_lo, st.g0 + 1)
                step.done(nc.vector.memset(prod[:, :, 0:st.T], 0.0))
                if st.kind == "pw2":
                    b2 = VCOL["pw2_b"]
                    step.done(nc.vector.tensor_tensor(gb[:, :, :], mG[:, 1], across(vec[:, b2:b2 + DT], 2, 2), ALU.mult))
                    for c in range(DT):
                        for s in range(2):
                            ins = nc.vector.tensor_scalar(x[:, c, S * s:S * s + S], x[:, c, S * s:S * s + S],
                                                          gb[:, c, s:s + 1], None, ALU.add)
                    step.done(ins)
                with dve.Fori(0, 2) as i:
                    for c in range(2):
                        m = st.m0 + c
                        for kk in range(ks):
                            n = st.n0 + ks * c + kk
                            if kk == ks - 1:
                                dve.wait_ge(slab_used, n + 1 + i * (2 * ks))
                                if st.mod is None:
                                    tiles = bass.ds(2 * c + 4 * i, 2)
                                    ins = nc.vector.tensor_tensor(x[:, tiles, 0:S], x[:, tiles, 0:S],
                                                                  acc[:, m % 2, :, 0:S], ALU.add)
                                else:
                                    for t in range(2):
                                        for s in range(st.T // S):
                                            at = bass.ds((2 * c + t) * 2 * S + S * s + i * (8 * S), S)
                                            g = bass.ds(16 * st.mod + 2 * (2 * c + t) + s + 8 * i, 1)
                                            ins = nc.vector.scalar_tensor_tensor(
                                                xf[:, at], acc[:, m % 2, t, S * s:S * s + S], mGf[:, g],
                                                xf[:, at], ALU.mult, ALU.add)
                                ins.then_inc(acc_free[m % 2], 1)
                                dve.wait_ge(sq_ready, st.sq0 + c + 1 + 2 * i)
                                dve.wait_ge(sq_added, st.add0 + c + 1 + 2 * i)
                                nc.vector.tensor_tensor(prod[:, :, 0:st.T], prod[:, :, 0:st.T], sq[:, :, 0:st.T],
                                                        ALU.add).then_inc(sq_added, 1)
                            lo(n + 2, i, 2 * ks)

            def pw1(st):
                nc.vector.memset(ub2[:, :, 0:PAD], 0.0)
                step.done(nc.vector.memset(ub2[:, :, PAD + S:SP_], 0.0))
                a, b = st.m0 % 2, (st.m0 + 1) % 2
                with dve.Fori(0, 4) as i:
                    lo(st.n0 + 2, i, 2)
                    dve.wait_ge(acc_free[a], freed(st.m0) + i)
                    dve.wait_ge(slab_used, st.n0 + 2 + 2 * i)
                    for t in range(2):
                        ins = nc.vector.scalar_tensor_tensor(
                            ub2[:, bass.ds(2 * t + 4 * i, 2), PAD:PAD + S],
                            acc[:, b, t, :].rearrange("p (s t) -> p s t", s=2),
                            vec[:, bass.ds(VCOL["pw1_b"] + t + 2 * i, 1)],
                            gate_sb[:, t, :].rearrange("p (s t) -> p s t", s=2), ALU.add, ALU.mult)
                    ins.then_inc(acc_free[b], 1)
                    lo(st.n0 + 3, i, 2)

            def conv(st):
                def tile(j):
                    return v[:, j, :].rearrange("p (s t) -> p s t", s=2)

                x_final(dve, st)
                for j in DVE_TILES:
                    w, b = VCOL["dw_w"] + CONV_W * j, VCOL["dw_b"] + j
                    nc.vector.tensor_scalar(tile(j), ub2[:, 2 * j:2 * j + 2, 0:S], vec[:, w:w + 1], vec[:, b:b + 1],
                                            ALU.mult, ALU.add).then_inc(conv_dve, 1)
                with dve.Fori(0, CONV_W - 1) as i:
                    for j in DVE_TILES:
                        dve.wait_ge(conv_dve, len(DVE_TILES) * i + j - DVE_TILES[0] + 1)
                        nc.vector.scalar_tensor_tensor(
                            tile(j), ub2[:, 2 * j:2 * j + 2, bass.ds(i + 1, S)],
                            vec[:, bass.ds(VCOL["dw_w"] + CONV_W * j + 1 + i, 1)], tile(j), ALU.mult, ALU.add)\
                            .then_inc(conv_dve, 1)
                dve.wait_ge(mean_done, 1)
                step.done(nc.vector.tensor_scalar(rs[:, :], B[2][:, :], 1.0 / D, None, ALU.mult))
                for c in range(DT):
                    nc.vector.tensor_tensor(v[:, c, :], v[:, c, :], rs[:, :], ALU.subtract).then_inc(d_ready, 1)
                dve.wait_ge(std_ready, st.std0 + 1)
                step.done(nc.vector.reciprocal(rs[:, :], rs[:, :]))

                def scaled(c):
                    g = VCOL["ln_g"] + c
                    nc.vector.scalar_tensor_tensor(v[:, c, :], v[:, c, :], vec[:, g:g + 1], rs[:, :],
                                                   ALU.mult, ALU.mult).then_inc(u_ready, 1)

                scaled(0)
                scaled(1)
                for c in range(DT):
                    dve.wait_ge(h_hi, st.h0 + c + 1)
                    nc.vector.tensor_tensor(hlo[:, c, :], sq[:, c % 2, :], hhi[:, c, :].bitcast(F32), ALU.subtract)\
                        .then_inc(h_ready, 1)
                    if c + 2 < DT:
                        scaled(c + 2)

            def qkv(st):
                let_pool_load()
                for c in range(6):
                    lo(st.n0 + c + 2)
                dve.wait_ge(rope_landed, 32)
                for j in range(5):
                    t = QK[:, 2 * j:2 * j + 2, :] if j < 4 else kraw[:, :, 0:S]
                    cos, sin = rope[:, 2 * (j // 4), :], rope[:, 2 * (j // 4) + 1, :]
                    tmp = prod[:, 0, :].rearrange("p (a b) -> p a b", a=2)
                    dve.wait_ge(rot_done, j + 1)
                    nc.vector.tensor_tensor(tmp, B[1 + j % 2][:, :].rearrange("p (a b) -> p a b", a=2),
                                            across(sin, 2), ALU.mult).then_inc(rope_done, 1)
                    step.done(nc.vector.tensor_tensor(t, t, across(cos, 2), ALU.mult))
                    dve.wait_ge(rope_done, j + 1)
                    step.done(nc.vector.tensor_tensor(t, t, tmp, ALU.add))

            def qknorm(st):
                let_pool_load()
                n = st.n0
                with dve.Fori(0, st.slabs // 2) as i:
                    step.loop(i, 2)
                    lo(n + 2, i, 2)
                    lo(n + 3, i, 2)
                    for c in range(2):
                        dve.wait_ge(std_ready, st.std0 + c + 1 + 2 * i)
                        step.done(nc.vector.reciprocal(prod[:, c, :], prod[:, c, :]))
                        tiles = QK[:, bass.ds(2 * c + 4 * i, 2), :]
                        nc.vector.scalar_tensor_tensor(
                            tiles, tiles, vec[:, bass.ds(st.gain + c + 2 * i, 1)],
                            prod[:, c, :].rearrange("p (a b) -> p a b", a=2), ALU.mult, ALU.mult)\
                            .then_inc(qk_done, 1)
                step.end(2, st.slabs // 2)

            def vab(st):
                with dve.Fori(0, 2) as i:
                    lo(st.n0 + 2, i, 2)
                    lo(st.n0 + 3, i, 2)

            def nsakv(st):
                for c in range(5):
                    lo(st.n0 + c + 2)

            def cmp_(st):
                dve.wait_ge(acc_free[st.m0 % 2], room(st.m0))
                dve.wait_ge(acc_free[(st.m0 + 1) % 2], room(st.m0 + 1))
                dve.wait_ge(vm_zero, 3)
                for kv in range(2):
                    r = craw[:, kv, 0, 0:1]
                    base = [list(r.ap[0])]
                    src = bass.AP(r.tensor, r.offset, base + [[1, 16], [S, NKV], [16, NCMP]])
                    pos = vec[:, VCOL["cmp_pos"] + 16 * kv:VCOL["cmp_pos"] + 16 * kv + 16]
                    pos = bass.AP(pos.tensor, pos.offset, [list(pos.ap[0]), [1, 16], [0, NKV], [0, NCMP]])
                    dst = blk[:, kv].rearrange("p l (t c) -> p l t c", t=NKV)[:, :, :, 0:NCMP]
                    nc.vector.tensor_tensor(dst, src, pos, ALU.add).then_inc(cmp_dve, 1)
                for kv in range(2):
                    dve.wait_ge(blk_hi, kv + 1)
                    nc.vector.tensor_tensor(blo[:, kv], blk[:, kv], bhi[:, kv].bitcast(F32), ALU.subtract)\
                        .then_inc(blk_lo, 1)
                for c in range(2):
                    lo(st.n0 + c + 2)
                dve.wait_ge(cmp_act, 2)
                step.done(nc.vector.reciprocal(kcr[:, :], kcr[:, :]))
                kf = kcmp[:, :, :].rearrange("p a b -> p (a b)")
                nc.vector.scalar_tensor_tensor(kf, kf, vec[:, VCOL["kn_cmp"]:VCOL["kn_cmp"] + 1], kcr[:, :],
                                               ALU.mult, ALU.mult).then_inc(cmp_dve, 1)
                dve.wait_ge(cmp_pe, 2)
                nc.vector.tensor_tensor(vcmp[:, :, :], B[3][0:16, 0:256].rearrange("p (a b) -> p a b", a=4),
                                        across(w2[0:16, 192:256], 4), ALU.add).then_inc(cmp_dve, 1)
                dve.wait_ge(bias_landed, 64)
                for q, ncol, at in ((0, 7, P + 31), (1, NCMP, 31)):
                    pc = Pc[:, q, :, 0:ncol]
                    for par in range(2):
                        dve.wait_ge(cmp_pe, 4 + 2 * q + par)
                        bank = B[(1, 2, 3, 0)[2 * q + par]]
                        step.done(nc.vector.tensor_tensor(
                            Pc[:, q, par:NH:2, 0:ncol], bank[:, 0:P].rearrange("p (a b) -> p a b", a=8)[:, :, 0:ncol],
                            bt[:, par:NH:2, at:S:16], ALU.add))
                    step.done(nc.vector.tensor_reduce(cst[:, 0, :], pc, AX.X, ALU.max))
                    nc.vector.tensor_tensor(pc, pc, across(cst[:, 0, :], ncol, 2), ALU.subtract).then_inc(cmp_dve, 1)
                for q, ncol in ((0, 7), (1, NCMP)):
                    pc = Pc[:, q, :, 0:ncol]
                    dve.wait_ge(cmp_act, 3 + q)
                    step.done(nc.vector.tensor_tensor(pc, pc, across(valid[:, q, 0:ncol], NH), ALU.mult))
                    step.done(nc.vector.tensor_reduce(cst[:, 1, :], pc, AX.X, ALU.add))
                    step.done(nc.vector.tensor_scalar(cst[:, 1, :], cst[:, 1, :], 1.0, None, ALU.max))
                    step.done(nc.vector.reciprocal(cst[:, 2, :], cst[:, 1, :]))
                    step.done(nc.vector.tensor_tensor(cst[:, 2, :], cst[:, 2, :], gates[:, q, 0:48:3], ALU.mult))
                    nc.vector.tensor_tensor(pc, pc, across(cst[:, 2, :], ncol, 2), ALU.mult).then_inc(cmp_dve, 1)

            def att(st):
                A0 = 32 * st.att0
                win, nsa = st.what == "window", st.what == "nsa"
                nc.vector.memset(junk[:, :], 0.0).then_inc(att_ready, 1)
                if not win:
                    dve.wait_ge(bias_landed, 64 if nsa else 32)
                if win:
                    for g in range(NKV):
                        ins = nc.vector.tensor_copy(
                            kd[64:P, 2 * g:2 * g + 2, :],
                            kraw[64 * (g % 2):64 * (g % 2) + 64, g // 2, :].rearrange("p (a b) -> p a b", a=2))
                    ins.then_inc(kd_dve, 1)
                if nsa:
                    for j in range(8):
                        g = j % 4
                        ins = nc.vector.tensor_copy(kd[64:P, j, :],
                                                    QK[64 * (g % 2):64 * (g % 2) + 64, 8 + 2 * (j // 4) + g // 2, :])
                    ins.then_inc(kd_dve, 1)

                def biased(u):
                    q, b = u % 2, u % 4
                    sp = stt4[:, b]
                    keys = 512 if win else P * (q + 1)
                    dve.wait_ge(s_ready, A0 + u + 1)
                    dve.wait_ge(t_ready, A0 + u + 1)
                    bias = mask[:, q, :] if win else bt[:, u // 2, P * (1 - q):S]
                    for s in range(2 if nsa else 1):
                        ins = nc.vector.tensor_tensor_reduce(sc[:, b, keys * s:keys * s + keys],
                                                             B[u % 4][:, keys * s:keys * s + keys], bias,
                                                             1.0, LOWEST, ALU.add, ALU.max, sp[:, s:s + 1])
                    ins.then_inc(s_free, 1)
                    dve.wait_ge(s_free, 4 + A0 + u + 1)
                    if win:
                        sink = VCOL["sink"] + u // 2
                        ins = nc.vector.tensor_scalar(sp[:, 2:3], sp[:, 0:1], vec[:, sink:sink + 1], -1.0,
                                                      ALU.max, ALU.mult)
                    else:
                        w = 2 if nsa else 1
                        ins = nc.vector.tensor_scalar(sp[:, 2:2 + w], sp[:, 0:w], -1.0, None, ALU.mult)
                    ins.then_inc(m_ready, 1)

                def normalised(u):
                    q, b = u % 2, u % 4
                    sp = stt4[:, b]
                    dve.wait_ge(e_ready, A0 + u + 1)
                    if win:
                        step.done(nc.vector.tensor_tensor(sp[:, 4:5], sp[:, 4:5], sp[:, 6:7], ALU.add))
                    w = 2 if nsa else 1
                    step.done(nc.vector.reciprocal(sp[:, 7:7 + w], sp[:, 4:4 + w]))
                    if nsa:
                        g = 3 * (u // 2) + 1
                        step.done(nc.vector.tensor_tensor(sp[:, 7:9], sp[:, 7:9], gates[:, q, g:g + 2], ALU.mult))
                    keys = 512 if win else P * (q + 1)
                    for s in range(w):
                        p = sc[:, b, keys * s:keys * s + keys]
                        ins = nc.vector.tensor_scalar(p, p, sp[:, 7 + s:8 + s], None, ALU.mult)
                    ins.then_inc(p_ready, 1)

                def out_lo(pair):
                    dve.wait_ge(o_hi, A0 // 4 + pair + 1)
                    nc.vector.tensor_tensor(olo[:, pair, :], acc[:, pair % 2, 0, 0:S],
                                            ohi[:, pair, :].bitcast(F32), ALU.subtract).then_inc(o_lo, 1)

                for u in range(LEAD):
                    biased(u)
                for u in range(UNITS):
                    normalised(u)
                    if u + LEAD < UNITS:
                        biased(u + LEAD)
                    if u % 4 == 2 and u > 4:
                        out_lo(u // 4 - 1)
                out_lo(DT - 1)

            def pleload(st):
                let_pool_load()

            def pleproj(st):
                lo(st.n0 + 2)

            def plegate(st):
                for c in range(4):
                    m = st.m0 + c
                    dve.wait_ge(ple_gate, 4 * st.layer + c + 1)
                    t = ub[:, 2 * (c % 2):2 * (c % 2) + 2, :]
                    step.done(nc.vector.tensor_tensor(t, gate_sb[:, :, (c % 2) * S:(c % 2 + 1) * S],
                                                      pp[:, 2 * c:2 * c + 2, :], ALU.mult))
                    xx = x[:, 2 * c:2 * c + 2, 0:S]
                    nc.vector.tensor_tensor(xx, xx, t, ALU.add).then_inc(acc_free[m % 2], 1)
                    lo(st.n0 + c + 2)

            run = dict(start=start, ada=ada, mods=mods, up=up, down=residual, pw2=residual, wo=residual, norm=norm,
                       pw1=pw1, conv=conv, qkv=qkv, qknorm=qknorm, vab=vab, nsakv=nsakv, cmp=cmp_, att=att,
                       pleload=pleload, pleproj=pleproj, plegate=plegate)
            for st in plan:
                if st.kind in run:
                    run[st.kind](st)

        @block.tensor
        def _(pe):
            def split_mm(out, w, xx, first, last):
                nc.tensor.matmul(out, w[0], xx[0], start=first, stop=False)
                nc.tensor.matmul(out, w[0], xx[1], start=False, stop=False)
                return nc.tensor.matmul(out, w[1], xx[0], start=False, stop=last)

            def w_at(n, a, b):
                return whi[:, n % 2, a:b], wlo[:, n % 2, a:b]

            def slab_there(n, i=0, per=0):
                pe.wait_ge(lo_half, n + 1 + i * per)

            def second_half(n, i=0, per=0):
                pe.wait_ge(lo_ready, n + 1 + i * per)

            def set_free(m, i=0, per=0):
                pe.wait_ge(acc_free[m % 2], room(m) + i * (per // 2))

            def tiles_of(n, m, op, T, i=0, per=0, k0=0, nk=SLAB_K, first=True, last=True, paced=None):
                for k in range(nk):
                    if k == SLAB_K // 2:
                        ins.then_inc(half_used, 1)
                        second_half(n, i, per)
                    if paced:
                        pe.wait_ge(h_ready, paced.h0 - paced.made + paced.made * (k + 1) // DT)
                    for t in range(2):
                        a = k * SLAB_N + t * P
                        ins = split_mm(acc[:, m % 2, t, 0:T], w_at(n, a, a + P),
                                       (op[0][:, k0 + k, 0:T], op[1][:, k0 + k, 0:T]),
                                       first and k == 0, last and k == nk - 1)
                return ins

            def tokens_of(n, m, count, cols=SLAB_N, i=0, per=0):
                for tt in range(count):
                    o = acc[:, m % 2, tt, 0:cols] if count == 2 else \
                        acc[:, m % 2, tt // 2, SLAB_N * (tt % 2):SLAB_N * (tt % 2) + SLAB_N]
                    for k in range(SLAB_K):
                        ks = slice(P * tt, P * tt + P)
                        a = k * SLAB_N
                        if k == SLAB_K // 2:
                            if tt == 0:
                                second_half(n, i, per)
                            if tt == count - 1:
                                ins.then_inc(half_used, 1)
                        nc.tensor.matmul(o, hhi[:, k, ks], whi[:, n % 2, a:a + cols], start=(k == 0), stop=False)
                        nc.tensor.matmul(o, hlo[:, k, ks], whi[:, n % 2, a:a + cols], start=False, stop=False)
                        ins = nc.tensor.matmul(o, hhi[:, k, ks], wlo[:, n % 2, a:a + cols], start=False,
                                               stop=(k == SLAB_K - 1))
                return ins

            def start(st):
                pe.wait_ge(loaded, 32)
                for j in range(2):
                    nc.tensor.matmul(B[1 + j][0:NH, 0:384], tab[:, :], hot[:, 384 * j:384 * j + 384],
                                     start=True, stop=True).then_inc(line_pe, 1)
                pe.wait_ge(c_ready, 2)
                pe.wait_ge(const_landed, 32)

            def ada_slab(n, q, i, per):
                slab_there(n, i, per)
                for k in range(SLAB_K):
                    if k == SLAB_K // 2:
                        ins.then_inc(half_used, 1)
                        second_half(n, i, per)
                    cols = slice(k * SLAB_N, (k + 1) * SLAB_N)
                    for half, w in enumerate((whi, wlo)):
                        ins = nc.tensor.matmul(B[2 + q % 2][0:4, 0:SLAB_N], c4[:, k, :], w[:, n % 2, cols],
                                               start=(k + half == 0), stop=(k + half == SLAB_K))
                ins.then_inc(slab_used, 1)

            def ada_turn(q, i):
                pe.wait_ge(row_ready, q + 1 + 2 * i)
                for t in range(2):
                    ins = nc.tensor.matmul(Mod[:, bass.ds(4 * q + 2 * t + 8 * i, 2)], arow[:, q % 2, P * t:P * t + P],
                                           pick, start=True, stop=True)
                ins.then_inc(row_turned, 1)

            def ada(st):
                with pe.Fori(0, st.slabs // 2) as i:
                    for c in range(2):
                        ada_slab(st.n0 + c, st.q0 + c, i, 2)
                    for c in range(2):
                        ada_turn(st.q0 + c, i)

            def norm(st):
                T = st.T
                if st.summed:
                    pe.wait_ge(sq_added, st.add0 + 1)
                    for c in range(2):
                        ins = nc.tensor.matmul(sums[:, 0:T], ones, prod[:, c, 0:T], start=(c == 0), stop=(c == 1))
                    ins.then_inc(sum_done, 1)
                    return
                for c in range(DT):
                    pe.wait_ge(sq_ready, st.sq0 + c + 1)
                    nc.tensor.matmul(sums[:, 0:T], ones, sq[:, c % 2, 0:T], start=(c == 0), stop=(c == DT - 1))\
                        .then_inc(sum_done, 1)

            def half_pair(st, c, n, m, i, per):
                slab_there(n, i, per)
                set_free(m, i, 2)
                tiles_of(n, m, (hhi, hlo), st.T, i, per, paced=st if c == 0 else None).then_inc(slab_used, 1)

            def up(st):
                both = st.ada // 2
                for first, count, per in ((0, both, 4), (both, 11 - both, 2)):
                    if not count:
                        continue
                    n, m = st.n0 + 4 * first, st.m0 + 2 * first
                    with pe.Fori(0, count) as i:
                        if per == 4:
                            ada_slab(n, st.q0, i, 4)
                        half_pair(st, 0, n + per // 2 - 1, m, i, per)
                        if per == 4:
                            ada_turn(st.q0, i)
                            ada_slab(n + 2, st.q0 + 1, i, 4)
                        half_pair(st, 1, n + per - 1, m + 1, i, per)
                        if per == 4:
                            ada_turn(st.q0 + 1, i)

            def pw1(st):
                with pe.Fori(0, 4) as i:
                    for c in range(2):
                        half_pair(st, c, st.n0 + c, st.m0 + c, i, 2)

            def residual(st):
                ks = st.slabs // 4
                if st.kind == "down":
                    pe.wait_ge(g_lo, st.g0 + 1)
                    op = (ghi, glo)
                elif st.kind == "wo":
                    pe.wait_ge(o_lo, 2 + 8 * st.att0)
                    op = (ohi, olo)
                else:
                    op = (hhi, hlo)
                with pe.Fori(0, 2) as i:
                    for c in range(2):
                        m = st.m0 + c
                        set_free(m, i, 2)
                        for kk in range(ks):
                            n = st.n0 + ks * c + kk
                            slab_there(n, i, 2 * ks)
                            nk = min(SLAB_K, HT - SLAB_K * kk) if ks == 3 else SLAB_K
                            tiles_of(n, m, op, st.T, i, 2 * ks, SLAB_K * kk, nk, kk == 0, kk == ks - 1,
                                     paced=st if st.kind == "pw2" and c == 0 else None).then_inc(slab_used, 1)

            def conv(st):
                x_final(pe, st)

                def tap(t, par, wait, first=False, last=False):
                    pe.wait_ge(diag_ready, wait)
                    for j in PE_TILES:
                        ins = nc.tensor.matmul(conv_out(j), diag[:, par, j - PE_TILES[0], :],
                                               ub2[:, 2 * j:2 * j + 2, bass.ds(t, S)], start=first, stop=last)
                    ins.then_inc(taps_used, 1)

                tap(0, 0, 1, first=True)
                tap(1, 1, 2)
                with pe.Fori(0, 14) as i:
                    tap(2 * i + 2, 0, 2 * i + 3)
                    tap(2 * i + 3, 1, 2 * i + 4)
                tap(30, 0, 31, last=True)
                m = st.m0 + 2
                pe.wait_ge(acc_free[0], 1 + (m + 1) // 2)
                pe.wait_ge(acc_free[1], 1 + m // 2)
                pe.wait_ge(conv_dve, len(DVE_TILES) * CONV_W)
                pe.wait_ge(conv_pool, len(POOL_TILES) * (2 * CONV_W - 1))
                for c in range(DT):
                    ins = nc.tensor.matmul(B[2][:, :], ones, v[:, c, :], start=(c == 0), stop=(c == DT - 1))
                ins.then_inc(mean_done, 1)
                for c in range(DT):
                    pe.wait_ge(sq_ready, st.sq0 + c + 1)
                    nc.tensor.matmul(sums[:, :], ones, sq[:, c % 2, :], start=(c == 0), stop=(c == DT - 1))\
                        .then_inc(sum_done, 1)

            def qkv(st):
                for c in range(6):
                    n, m = st.n0 + c, st.m0 + c
                    slab_there(n)
                    set_free(m)
                    if c < 5:
                        ins = tiles_of(n, m, (hhi, hlo), S if c < 4 else 2 * S, paced=st if c == 0 else None)
                    else:
                        ins = tokens_of(n, m, 4)
                    ins.then_inc(slab_used, 1)
                for j in range(5):
                    t = QK[:, 2 * j:2 * j + 2, :] if j < 4 else kraw[:, :, 0:S]
                    pe.wait_ge(acc_free[(st.m0 + j) % 2], freed(st.m0 + j))
                    if j >= 2:
                        pe.wait_ge(rope_done, j - 1)
                    nc.tensor.matmul(B[1 + j % 2][:, :], rot, t, start=True, stop=True).then_inc(rot_done, 1)

            def qknorm(st):
                n, m = st.n0, st.m0
                with pe.Fori(0, st.slabs // 2) as i:
                    for c in range(2):
                        slab_there(n + c, i, 2)
                        set_free(m + c, i, 2)
                        tiles_of(n + c, m + c, (hhi, hlo), S, i, 2, paced=None if c else st).then_inc(slab_used, 1)
                    for c in range(2):
                        pe.wait_ge(acc_free[(m + c) % 2], freed(m + c) + i)
                        nc.tensor.matmul(B[1 + c][:, :], headones, sq[:, c, :], start=True, stop=True)\
                            .then_inc(sum_done, 1)

            def vab(st):
                with pe.Fori(0, 2) as i:
                    for c in range(2):
                        slab_there(st.n0 + c, i, 2)
                        set_free(st.m0 + c, i, 2)
                        tokens_of(st.n0 + c, st.m0 + c, 2, SLAB_N, i, 2).then_inc(slab_used, 1)

            def nsakv(st):
                for c in range(5):
                    n, m = st.n0 + c, st.m0 + c
                    slab_there(n)
                    set_free(m)
                    ins = tiles_of(n, m, (hhi, hlo), S) if c < 2 else tokens_of(n, m, 2, SLAB_N if c < 4 else 48)
                    ins.then_inc(slab_used, 1)

            def cmp_(st):
                for kv in range(2):
                    m = st.m0 + kv
                    pe.wait_ge(blk_lo, kv + 1)
                    set_free(m)
                    n = st.n0 + kv
                    slab_there(n)
                    for k in range(16):
                        if k == 8:
                            ins.then_inc(half_used, 1)
                            second_half(n)
                        ins = split_mm(acc[:, m % 2, 0, 0:64], w_at(n, P * k, P * k + P),
                                       (bhi[:, kv, k, :], blo[:, kv, k, :]), k == 0, k == 15)
                    ins.then_inc(slab_used, 1)
                pe.wait_ge(acc_free[st.m0 % 2], freed(st.m0))
                nc.tensor.matmul(B[1][:, 0:64], w2[:, 0:P], hid[:, 0, :, :].rearrange("p a b -> p (a b)"),
                                 start=True, stop=True).then_inc(cmp_pe, 1)
                pe.wait_ge(acc_free[(st.m0 + 1) % 2], freed(st.m0 + 1))
                for g in range(NKV):
                    ins = nc.tensor.matmul(B[3][0:16, HD * g:HD * g + HD], hid[:, 1, 2 * (g % 2) + g // 2, :],
                                           w2[:, P:P + HD], start=True, stop=True)
                ins.then_inc(cmp_pe, 1)
                pe.wait_ge(cmp_act, 1)
                nc.tensor.matmul(B[2][:, 0:64], headones, kcsq[:, :], start=True, stop=True).then_inc(cmp_pe, 1)
                pe.wait_ge(cmp_dve, 4)
                pe.wait_ge(qk_done, 2 + st.qk0)
                for q, ncol in ((0, 7), (1, NCMP)):
                    for par in range(2):
                        bank = B[(1, 2, 3, 0)[2 * q + par]]
                        rows = slice(64 * par, 64 * par + 64)
                        for hh in range(8):
                            g = (2 * hh + par) // 4
                            ins = nc.tensor.matmul(bank[:, 16 * hh:16 * hh + ncol], QK[rows, hh, P * q:P * q + P],
                                                   kcmp[rows, 2 * (g % 2) + g // 2, 0:ncol], start=True, stop=True)
                        ins.then_inc(cmp_pe, 1)
                pe.wait_ge(cmp_dve, 8)
                for g in range(NKV):
                    if g >= 2:
                        pe.wait_ge(cmp_act, 5 + g - 2)
                    for q in range(2):
                        ins = nc.tensor.transpose(B[1 + g % 2][:, P * q:P * q + P],
                                                  Pc[:, q, 4 * g:4 * g + 4, :].rearrange("p a b -> p (a b)"), ident)
                    ins.then_inc(cmp_pe, 1)

            def att(st):
                A0 = 32 * st.att0
                win, nsa = st.what == "window", st.what == "nsa"
                x_final(pe, st)
                pe.wait_ge(att_ready, st.att0 + 1)
                if st.what != "ab":
                    pe.wait_ge(kd_dve, 2 if nsa else 1)
                    pe.wait_ge(kd_act, 2 if nsa else 1)
                if nsa:
                    pe.wait_ge(cmp_act, 8)
                    pe.wait_ge(vm_landed, 64)

                def scores(u):
                    q, tile, g = u % 2, u // 4, u // 8
                    rows = slice(HD * (u // 2 % 2), HD * (u // 2 % 2) + HD)
                    keys = 512 if win else P * (q + 1)
                    pe.wait_ge(s_free, A0 + u + 1)
                    for s in range(2 if nsa else 1):
                        if win:
                            kk = kd[rows, 2 * g:2 * g + 2, :].rearrange("p a b -> p (a b)")
                        elif nsa:
                            kk = kd[rows, 4 * s + g, 0:keys]
                        else:
                            kk = QK[rows, 8 + tile, 0:keys]
                        ins = nc.tensor.matmul(B[u % 4][:, keys * s:keys * s + keys], QK[rows, tile, P * q:P * q + P],
                                               kk, start=True, stop=True)
                    ins.then_inc(s_ready, 1)

                def turned(u):
                    q = u % 2
                    pe.wait_ge(p_ready, A0 + u + 1)
                    pe.wait_ge(pt_ready, A0 + u + 1)
                    nt = 4 if win else (q + 1) * (2 if nsa else 1)
                    for j in range(nt):
                        ins = nc.tensor.transpose(acc[:, q, 1, P * j:P * j + P], sc[:, u % 4, P * j:P * j + P], ident)
                    ins.then_inc(t_ready, 1)

                def values(u):
                    q, pair, g = u % 2, u // 4, u // 8
                    rows = slice(HD * (u // 2 % 2), HD * (u // 2 % 2) + HD)
                    o = acc[rows, pair % 2, 0, P * q:P * q + P]
                    if u % 4 == 0:
                        pe.wait_ge(o_lo, A0 // 4 + pair + 1)
                    pe.wait_ge(pt_ready, 2 + A0 + u + 1)
                    first = True
                    if nsa:
                        nc.tensor.matmul(o, Vm[:, u // 2, :], PcT[:, g, q, :], start=True, stop=False)
                        first = False
                    nk = 4 if win else q + 1
                    ns = 2 if nsa else 1
                    for s in range(ns):
                        for k in range(nk):
                            at = S * k + HD * g if win else 512 * k + S * s + HD * g if nsa else \
                                D * k + HD * (u // 2)
                            j = s * nk + k
                            ins = nc.tensor.matmul(o, vt[:, at:at + HD], pT[:, q, P * j:P * j + P], start=first,
                                                   stop=(j == ns * nk - 1))
                            first = False
                    ins.then_inc(pv_done, 1)

                for u in range(LEAD):
                    scores(u)
                for u in range(UNITS):
                    if u + LEAD < UNITS:
                        scores(u + LEAD)
                    turned(u)
                    if u:
                        values(u - 1)
                values(UNITS - 1)

            def pleproj(st):
                pe.wait_ge(p_split, 2 * st.layer + 2)
                slab_there(st.n0)
                for half in range(2):
                    m = st.m0 + half
                    set_free(m)
                    if half:
                        second_half(st.n0)
                    for j in range(4):
                        for k in range(2):
                            a = (2 * (2 * half + j // 2) + k) * SLAB_N + (j % 2) * P
                            ins = split_mm(acc[:, m % 2, j // 2, S * (j % 2):S * (j % 2) + S], w_at(st.n0, a, a + P),
                                           (phi[:, k, :], plo[:, k, :]), k == 0, k == 1)
                    ins.then_inc(slab_used if half else half_used, 1)

            def plegate(st):
                for c in range(4):
                    slab_there(st.n0 + c)
                    set_free(st.m0 + c)
                    tiles_of(st.n0 + c, st.m0 + c, (hhi, hlo), S, paced=None if c else st).then_inc(slab_used, 1)

            run = dict(start=start, ada=ada, norm=norm, up=up, pw1=pw1, down=residual, pw2=residual, wo=residual,
                       conv=conv, qkv=qkv, qknorm=qknorm, vab=vab, nsakv=nsakv, cmp=cmp_, att=att,
                       pleproj=pleproj, plegate=plegate)
            for st in plan:
                if st.kind in run:
                    run[st.kind](st)


def slabs_of(w):
    K, N = w.shape
    n = -(-N // SLAB_N)
    k = -(-K // (P * SLAB_K)) * SLAB_K
    full = np.zeros((k * P, n * SLAB_N), np.float32)
    full[:K, :N] = w
    a = full.reshape(k // SLAB_K, SLAB_K, P, n, SLAB_N)
    return list(a.transpose(3, 0, 2, 1, 4).reshape(n * (k // SLAB_K), P, SLAB))


def stream(z):
    out = []
    ada = slabs_of(np.asarray(z["ada_w"][0])) + slabs_of(np.asarray(z["ada_w"][1]))

    def pairs(a, b, extra=0):
        for j, (g, u) in enumerate(zip(slabs_of(a), slabs_of(b))):
            out.extend([ada.pop(0), g, ada.pop(0), u] if j < extra // 2 else [g, u])

    def ffn(wi, wo, extra=0):
        pairs(wi[:, :HID], wi[:, HID:], extra)
        out.extend(slabs_of(wo))

    for _ in range(10):
        out.append(ada.pop(0))
    for layer in range(2):
        ffn(z["ffn1_wi"][layer], z["ffn1_wo"][layer], 18 if layer else 22)
        if layer == 0:
            w = z["conv_pw1_w"][0]
            pairs(w[:, D:], w[:, :D])
            out.extend(slabs_of(z["conv_pw2_w"][0]))
            ffn(z["ffn2_wi"][0], z["ffn2_wo"][0], 22)
        else:
            out.extend(slabs_of(z["attn_w_qkv"][0]))
            out.extend(slabs_of(z["attn_w_o"][0]))
            ffn(z["ffn2_wi"][1], z["ffn2_wo"][1])
    for layer in range(2):
        if layer == 0:
            qa, ka, va, qb, kb, vb = np.split(z["w_in_ab_2"][0], 6, axis=1)
            out.extend(slabs_of(np.concatenate([qa, qb, ka, kb, va, vb], 1)))
            wo = z["w_out_ab_2"][0]
        else:
            q, kc, vc, ks, vs, kw, vw, g = np.split(z["w_in_nsa_2"][0], [D + 256 * j for j in range(7)], axis=1)
            out.extend(slabs_of(np.concatenate([q, ks, kw, kc, vc, vs, vw, g], 1)))
            for name in ("cmp_k_w1_2", "cmp_v_w1_2"):
                out.append(z[name][0].reshape(2, 16, HD, P).transpose(0, 2, 1, 3).reshape(P, SLAB))
            wo = z["w_out_nsa_2"][0]
        out.extend(slabs_of(wo))
        pairs(z["w_ffn_gate_2"][layer], z["w_ffn_up_2"][layer])
        out.extend(slabs_of(z["w_ffn_down_2"][layer]))
        w = z["w_ple_proj_2"][layer].reshape(2, P, 4, SLAB_N)
        out.append(w.transpose(1, 2, 0, 3).reshape(P, SLAB))
        out.extend(slabs_of(z["w_ple_gate_2"][layer]))
    return np.stack(out)


def columns(v):
    return np.asarray(v).reshape(-1, P).T


def both_halves(v):
    return np.concatenate([v, v]).reshape(P, 1)


def vectors(z):
    h = both_halves
    gains_ab = [z[n][0] for n in ("qn_moba_2", "qn_moba_2", "qn_dil_2", "qn_dil_2",
                                  "kn_moba_2", "kn_moba_2", "kn_dil_2", "kn_dil_2")]
    gains_nsa = [z[n][0] for n in ("qn_nsa_2",) * 4 + ("kn_slc_2", "kn_win_2")]
    pos = np.stack([z["cmp_k_pos_2"][0], z["cmp_v_pos_2"][0]]).reshape(2, 2, 16, HD)
    parts = dict(
        norm_g=columns(z["norm_g"]), ada_b=columns(z["ada_b"]), final_g=columns(z["final_g"]),
        pw1_b=columns(z["conv_pw1_b"]), dw_b=columns(z["conv_dw_b"]), ln_g=columns(z["conv_ln_g"]),
        ln_b=columns(z["conv_ln_b"]), pw2_b=columns(z["conv_pw2_b"]),
        dw_w=z["conv_dw_w"][0].reshape(CONV_W, DT, P).transpose(2, 1, 0).reshape(P, -1),
        c=columns(z["c"]), c_ctx=columns(z["c_ctx"]), norm_mix=columns(z["norm_mix_2"]),
        norm_ffn=columns(z["norm_ffn_2"]), norm_ple=columns(z["norm_ple_2"]),
        qk_gain_ab=np.concatenate([h(g) for g in gains_ab], 1),
        qk_gain_nsa=np.concatenate([h(g) for g in gains_nsa], 1),
        kn_cmp=h(z["kn_cmp_2"][0]), cmp_b1=np.stack([z["cmp_k_b1_2"][0], z["cmp_v_b1_2"][0]], 1),
        cmp_k_b2=h(z["cmp_k_b2_2"][0]), cmp_pos=pos.transpose(1, 3, 0, 2).reshape(P, 32),
        sink=np.broadcast_to(z["attn_sink"][0], (P, NH)))
    return np.concatenate([parts[n] for n, _ in VECTORS], 1)


def arrays_of(z):
    z = {k: np.asarray(v) for k, v in z.items()}
    tok = np.concatenate([z["x"][0], z["ctx"][0]], 0)
    w2 = np.concatenate([z["cmp_k_w2_2"][0], z["cmp_k_w2_2"][0], z["cmp_v_w2_2"][0],
                         np.broadcast_to(z["cmp_v_b2_2"][0], (P, HD))], 1)
    out = dict(
        slabs=stream(z), x_in=tok.reshape(2 * S, DT, P).transpose(2, 1, 0), vec=vectors(z),
        const=small_constants(), w2=w2, tab=z["rel_bias_2"], hot=line_tables(), rope=rope_tables(),
        mask=window_mask(), p=z["p_2"][:, 0].reshape(2, S, 2, P).transpose(0, 3, 2, 1))
    return {"in_" + k: np.ascontiguousarray(v, dtype=np.float32) for k, v in out.items()}


def kernel(**inputs):
    import concourse.bacc as _bacc
    from concourse.bass_utils import run_bass_kernel_spmd as _run

    arrays = arrays_of(inputs)
    nc = _bacc.Bacc("TRN2", target_bir_lowering=False, num_devices=1)
    args = [nc.dram_tensor(k, a.shape, F32, kind="ExternalInput").ap() for k, a in arrays.items()]
    args.append(nc.dram_tensor("out", (P, DT, S), F32, kind="ExternalOutput").ap())
    build(nc, *args)
    r = _run(nc, [arrays], core_ids=[0])
    return r.results[0]["out"].transpose(2, 1, 0).reshape(1, S, D)
```
